# Optimizing a Trainium2 kernel written in Bass

```python
import math
import jax, jax.numpy as jnp
from jax import lax
import numpy as np

D_MODEL = 1024
BATCH = 1
SEQ = 1024
DEPTH = 1

CHUNK = 64
PLE_DIM = 256
EPS = 1e-6
ATT_HEADS = 16
ATT_KV_HEADS = 4
ATT_HEAD_DIM = 64
WINDOW = 128
WINDOW_CHUNKS = WINDOW // CHUNK
REL_BUCKETS = 32
REL_MAX_DIST = 128
SSM_D_INNER = 2 * D_MODEL
SSM_HEAD_DIM = 64
SSM_HEADS = SSM_D_INNER // SSM_HEAD_DIM
SSM_GROUPS = 4
SSM_STATE = 128
SSM_CONV = 4
SSM_CONV_DIM = SSM_D_INNER + 2 * SSM_GROUPS * SSM_STATE
PEER_HEADS = 8
PEER_N_KEYS = 128
PEER_EXPERTS = PEER_N_KEYS * PEER_N_KEYS
PEER_TOPK = 16
PEER_QUERY_DIM = 256
PEER_HALF = PEER_QUERY_DIM // 2
PEER_TOKEN_BLOCK = 128
ATT_Q_W = ATT_HEADS * ATT_HEAD_DIM
ATT_KV_W = ATT_KV_HEADS * ATT_HEAD_DIM
IN_SPLITS = (ATT_Q_W, ATT_KV_W, ATT_KV_W, SSM_D_INNER, SSM_CONV_DIM, SSM_HEADS, D_MODEL, D_MODEL)
IN_WIDTH = sum(IN_SPLITS)

kernel_name = "hybrid_swa_ssd_peer_block"

def rms_norm(x, g):
    x32 = x.astype(jnp.float32)
    y = x32 * lax.rsqrt(jnp.mean(x32 * x32, axis=-1, keepdims=True) + EPS)
    return (y * g.astype(jnp.float32)).astype(x.dtype)

def t5_bucket(rel):
    nb = REL_BUCKETS // 2
    max_exact = nb // 2
    ret = jnp.where(rel > 0, nb, 0)
    n = jnp.abs(rel)
    nf = jnp.maximum(n, 1).astype(jnp.float32)
    large = max_exact + (jnp.log(nf / max_exact) / math.log(REL_MAX_DIST / max_exact)
                         * (nb - max_exact)).astype(jnp.int32)
    large = jnp.minimum(large, nb - 1)
    return ret + jnp.where(n < max_exact, n, large)

def chunk_band(t):
    nc = t.shape[1]
    pad = [(0, 0)] * t.ndim
    pad[1] = (WINDOW_CHUNKS - 1, 0)
    tp = jnp.pad(t, pad)
    return jnp.concatenate([tp[:, j:j + nc] for j in range(WINDOW_CHUNKS)], axis=2)

def window_attention(q, k, v, q_g, k_g, sinks, rel_bias):
    b, L = q.shape[:2]
    nc = L // CHUNK
    rep = ATT_HEADS // ATT_KV_HEADS
    band = WINDOW_CHUNKS * CHUNK
    q = rms_norm(q.reshape(b, L, ATT_HEADS, ATT_HEAD_DIM), q_g)
    k = rms_norm(k.reshape(b, L, ATT_KV_HEADS, ATT_HEAD_DIM), k_g)
    v = v.reshape(b, L, ATT_KV_HEADS, ATT_HEAD_DIM)
    qc = q.reshape(b, nc, CHUNK, ATT_KV_HEADS, rep, ATT_HEAD_DIM)
    kb = chunk_band(k.reshape(b, nc, CHUNK, ATT_KV_HEADS, ATT_HEAD_DIM))
    vb = chunk_band(v.reshape(b, nc, CHUNK, ATT_KV_HEADS, ATT_HEAD_DIM))
    s = jnp.einsum('bcqgrd,bckgd->bgrcqk', qc, kb).astype(jnp.float32) * (ATT_HEAD_DIM ** -0.5)
    qi = jnp.arange(CHUNK, dtype=jnp.int32)[:, None]
    kj = jnp.arange(band, dtype=jnp.int32)[None, :]
    rel = kj - (WINDOW_CHUNKS - 1) * CHUNK - qi
    bias = rel_bias.astype(jnp.float32)[t5_bucket(rel)]
    bias = jnp.transpose(bias, (2, 0, 1)).reshape(ATT_KV_HEADS, rep, 1, CHUNK, band)
    s = s + bias
    key_chunk = jnp.arange(nc)[:, None] - (WINDOW_CHUNKS - 1) + jnp.arange(band)[None, :] // CHUNK
    valid = (key_chunk >= 0)[None, None, None, :, None, :]
    s = jnp.where(valid, s, -jnp.inf)
    sink = sinks.astype(jnp.float32).reshape(ATT_KV_HEADS, rep, 1, 1, 1)
    m = jnp.maximum(jnp.max(s, axis=-1, keepdims=True), sink)
    e = jnp.exp(s - m)
    probs = e / (jnp.sum(e, axis=-1, keepdims=True) + jnp.exp(sink - m))
    o = jnp.einsum('bgrcqk,bckgd->bcqgrd', probs.astype(vb.dtype), vb)
    return o.reshape(b, L, ATT_Q_W)

def causal_conv(u, w):
    return lax.conv_general_dilated(u, w[:, None, :].astype(u.dtype), window_strides=(1,),
                                    padding=[(SSM_CONV - 1, 0)],
                                    dimension_numbers=('NWC', 'WIO', 'NWC'),
                                    feature_group_count=u.shape[-1])

def ssd_scan(x, dt, A, Bm, Cm):
    b, L, H, P = x.shape
    G, N = Bm.shape[-2:]
    nc = L // CHUNK
    hpg = H // G
    x = x.reshape(b, nc, CHUNK, G, hpg, P)
    dt = dt.reshape(b, nc, CHUNK, G, hpg)
    Bm = Bm.reshape(b, nc, CHUNK, G, N).astype(jnp.float32)
    Cm = Cm.reshape(b, nc, CHUNK, G, N).astype(jnp.float32)
    a = jnp.moveaxis(jnp.cumsum(dt * A.reshape(G, hpg), axis=2), 2, -1)
    dtx = x.astype(jnp.float32) * dt[..., None]
    causal = jnp.tril(jnp.ones((CHUNK, CHUNK), dtype=bool))
    decay_in = jnp.exp(jnp.where(causal, a[..., :, None] - a[..., None, :], -jnp.inf))
    cb = jnp.einsum('bctgn,bcsgn->bcgts', Cm, Bm)
    w_in = cb[:, :, :, None] * decay_in
    y_diag = jnp.einsum('bcghts,bcsghp->bctghp', w_in, dtx)
    decay_out = jnp.moveaxis(jnp.exp(a[..., -1:] - a), -1, 2)
    states = jnp.einsum('bcsgn,bcsghp->bcghpn', Bm, dtx * decay_out[..., None])
    chunk_decay = jnp.exp(a[..., -1])

    def step(h, inp):
        st, dec = inp
        return h * dec[..., None, None] + st, h

    h0 = jnp.zeros_like(states[:, 0])
    _, prev = lax.scan(step, h0, (jnp.moveaxis(states, 1, 0), jnp.moveaxis(chunk_decay, 1, 0)))
    prev = jnp.moveaxis(prev, 0, 1)
    y_off = jnp.einsum('bctgn,bcghpn->bctghp', Cm, prev) * jnp.moveaxis(jnp.exp(a), -1, 2)[..., None]
    return (y_diag + y_off).reshape(b, L, H, P)

def ssd_mixer(z, xbc, dt_raw, conv_w, conv_b, dt_bias, a_log, d_skip, norm_g):
    b, L = z.shape[:2]
    gn = SSM_GROUPS * SSM_STATE
    xbc = jax.nn.silu(causal_conv(xbc, conv_w) + conv_b)
    xs, Bm, Cm = jnp.split(xbc, [SSM_D_INNER, SSM_D_INNER + gn], axis=-1)
    xs = xs.reshape(b, L, SSM_HEADS, SSM_HEAD_DIM)
    Bm = Bm.reshape(b, L, SSM_GROUPS, SSM_STATE)
    Cm = Cm.reshape(b, L, SSM_GROUPS, SSM_STATE)
    dt = jax.nn.softplus(dt_raw.astype(jnp.float32) + dt_bias.astype(jnp.float32))
    A = -jnp.exp(a_log.astype(jnp.float32))
    y = ssd_scan(xs, dt, A, Bm, Cm) + d_skip.astype(jnp.float32)[:, None] * xs.astype(jnp.float32)
    y = y.reshape(b, L, SSM_D_INNER) * jax.nn.silu(z.astype(jnp.float32))
    yg = y.reshape(b, L, SSM_GROUPS, SSM_D_INNER // SSM_GROUPS)
    yg = yg * lax.rsqrt(jnp.mean(yg * yg, axis=-1, keepdims=True) + EPS)
    return (yg.reshape(b, L, SSM_D_INNER) * norm_g.astype(jnp.float32)).astype(z.dtype)

def peer(h, w_q, sub_keys, u_tab, v_tab):
    b, L, d = h.shape
    q = (h @ w_q).reshape(b, L, PEER_HEADS, 2, PEER_HALF)
    s = jnp.einsum('bshkd,hknd->bshkn', q, sub_keys).astype(jnp.float32)
    s_top, i_top = lax.top_k(s, PEER_TOPK)
    cand = (s_top[..., 0, :, None] + s_top[..., 1, None, :]).reshape(b, L, PEER_HEADS, PEER_TOPK * PEER_TOPK)
    sc, pos = lax.top_k(cand, PEER_TOPK)
    i1 = jnp.take_along_axis(i_top[..., 0, :], pos // PEER_TOPK, axis=-1)
    i2 = jnp.take_along_axis(i_top[..., 1, :], pos % PEER_TOPK, axis=-1)
    idx = i1 * PEER_N_KEYS + i2
    gate = jax.nn.softmax(sc, axis=-1)
    nb = (b * L) // PEER_TOKEN_BLOCK

    def block(args):
        hb, ib, gb = args
        u = jnp.take(u_tab, ib, axis=0)
        act = jnp.einsum('thkd,td->thk', u, hb).astype(jnp.float32)
        act = (jax.nn.gelu(act) * gb).astype(hb.dtype)
        v = jnp.take(v_tab, ib, axis=0)
        return jnp.einsum('thk,thkd->td', act, v).astype(hb.dtype)

    out = lax.map(block, (h.reshape(nb, PEER_TOKEN_BLOCK, d),
                          idx.reshape(nb, PEER_TOKEN_BLOCK, PEER_HEADS, PEER_TOPK),
                          gate.reshape(nb, PEER_TOKEN_BLOCK, PEER_HEADS, PEER_TOPK)))
    return out.reshape(b, L, d)

def setup_inputs(seed: int = 0) -> dict:
    key = jax.random.key(seed)
    ks = jax.random.split(key, 32)
    f32 = jnp.float32
    nrm = lambda k, shape, scale: jax.random.normal(k, shape, f32) * scale
    gain = lambda k, shape: 1.0 + 0.05 * jax.random.normal(k, shape, f32)
    dt0 = jnp.exp(jax.random.uniform(ks[10], (DEPTH, SSM_HEADS), f32) * (math.log(0.1) - math.log(0.001)) + math.log(0.001))
    return {
        "x": nrm(ks[0], (BATCH, SEQ, D_MODEL), 1.0),
        "p": nrm(ks[1], (DEPTH, BATCH, SEQ, PLE_DIM), 1.0),
        "norm_mix_g": gain(ks[2], (DEPTH, D_MODEL)),
        "w_in": nrm(ks[3], (DEPTH, D_MODEL, IN_WIDTH), D_MODEL ** -0.5),
        "q_norm_g": gain(ks[4], (DEPTH, ATT_HEAD_DIM)),
        "k_norm_g": gain(ks[5], (DEPTH, ATT_HEAD_DIM)),
        "attn_sinks": nrm(ks[6], (DEPTH, ATT_HEADS), 0.5),
        "rel_bias": nrm(ks[7], (REL_BUCKETS, ATT_HEADS), 0.1),
        "conv_w": nrm(ks[8], (DEPTH, SSM_CONV, SSM_CONV_DIM), SSM_CONV ** -0.5),
        "conv_b": nrm(ks[9], (DEPTH, SSM_CONV_DIM), 0.02),
        "dt_bias": dt0 + jnp.log(-jnp.expm1(-dt0)),
        "a_log": jnp.log(jax.random.uniform(ks[11], (DEPTH, SSM_HEADS), f32, 1.0, 16.0)),
        "d_skip": gain(ks[12], (DEPTH, SSM_HEADS)),
        "ssm_norm_g": gain(ks[13], (DEPTH, SSM_D_INNER)),
        "w_o_attn": nrm(ks[14], (DEPTH, ATT_Q_W, D_MODEL), ATT_Q_W ** -0.5),
        "w_o_ssm": nrm(ks[15], (DEPTH, SSM_D_INNER, D_MODEL), SSM_D_INNER ** -0.5),
        "w_out": nrm(ks[16], (DEPTH, D_MODEL, D_MODEL), D_MODEL ** -0.5),
        "norm_ffn_g": gain(ks[17], (DEPTH, D_MODEL)),
        "w_peer_q": nrm(ks[18], (DEPTH, D_MODEL, PEER_HEADS * PEER_QUERY_DIM), D_MODEL ** -0.5),
        "peer_sub_keys": nrm(ks[19], (DEPTH, PEER_HEADS, 2, PEER_N_KEYS, PEER_HALF), PEER_HALF ** -0.5),
        "peer_u": nrm(ks[20], (DEPTH, PEER_EXPERTS, D_MODEL), D_MODEL ** -0.5),
        "peer_v": nrm(ks[21], (DEPTH, PEER_EXPERTS, D_MODEL), (PEER_HEADS * PEER_TOPK) ** -0.5),
        "norm_ple_g": gain(ks[22], (DEPTH, D_MODEL)),
        "w_ple_gate": nrm(ks[23], (DEPTH, D_MODEL, D_MODEL), D_MODEL ** -0.5),
        "w_ple": nrm(ks[24], (DEPTH, PLE_DIM, D_MODEL), PLE_DIM ** -0.5),
    }

def reference(x, p, norm_mix_g, w_in, q_norm_g, k_norm_g, attn_sinks, rel_bias, conv_w, conv_b,
              dt_bias, a_log, d_skip, ssm_norm_g, w_o_attn, w_o_ssm, w_out, norm_ffn_g, w_peer_q,
              peer_sub_keys, peer_u, peer_v, norm_ple_g, w_ple_gate, w_ple):
    offsets = [int(o) for o in np.cumsum(IN_SPLITS)[:-1]]
    for i in range(DEPTH):
        h = rms_norm(x, norm_mix_g[i])
        proj = h @ w_in[i]
        q, k, v, z, xbc, dt_raw, g_att, g_ssm = jnp.split(proj, offsets, axis=-1)
        o_att = window_attention(q, k, v, q_norm_g[i], k_norm_g[i], attn_sinks[i], rel_bias) @ w_o_attn[i]
        o_ssm = ssd_mixer(z, xbc, dt_raw, conv_w[i], conv_b[i], dt_bias[i], a_log[i], d_skip[i],
                          ssm_norm_g[i]) @ w_o_ssm[i]
        mixed = jax.nn.sigmoid(g_att) * o_att + jax.nn.sigmoid(g_ssm) * o_ssm
        x = x + (mixed @ w_out[i]).astype(x.dtype)
        x = x + peer(rms_norm(x, norm_ffn_g[i]), w_peer_q[i], peer_sub_keys[i], peer_u[i], peer_v[i])
        ple_gate = jax.nn.sigmoid(rms_norm(x, norm_ple_g[i]) @ w_ple_gate[i])
        x = x + ((p[i] @ w_ple[i]) * ple_gate).astype(x.dtype)
    return x


_drawn_inputs = setup_inputs


def setup_inputs(seed=0):
    import zlib

    import numpy as np

    out = dict(_drawn_inputs(seed))
    spreads = {}
    factors = {'q_norm_g': 8.0,
     'k_norm_g': 8.0,
     'attn_sinks': 8.0,
     'rel_bias': 8.0,
     'conv_b': 4.132,
     'd_skip': 4.289,
     'norm_ffn_g': 6.589,
     'norm_ple_g': 18.478}
    for name, (base, spread) in spreads.items():
        noise = np.random.default_rng([zlib.crc32(name.encode()), seed]).standard_normal(out[name].shape)
        drawn = base * np.exp(spread * noise) if base else spread * noise
        out[name] = __import__('jax').numpy.asarray(drawn.astype(out[name].dtype))
    for name, factor in factors.items():
        out[name] = (out[name] * factor).astype(out[name].dtype)
    return out
```

```python
import concourse.bass as bass
from concourse import mybir
from contextlib import ExitStack
import numpy as np

F32 = mybir.dt.float32
F32R = mybir.dt.float32r
BF16 = mybir.dt.bfloat16
U32 = mybir.dt.uint32
ACT = mybir.ActivationFunctionType
ALU = mybir.AluOpType
AX = mybir.AxisListType

P = 128
T = 1024
HALF = 512
D = 1024
KD = D // P
EPS = 1e-6


class Phase(ExitStack):

    def __init__(self, nc):
        super().__init__()
        self.nc, self.semaphores = nc, []

    def semaphore(self, name):
        self.semaphores.append(self.nc.alloc_semaphore(name))
        return self.semaphores[-1]

    def __exit__(self, *failure):
        super().__exit__(*failure)
        if failure[0] is None:
            self.nc.clear_and_free_semaphores(self.semaphores)
            self.nc.all_engine_barrier()


def rms_phase(nc, name, x_dram, gain_dram, h_hi, h_lo, ones):
    ctx = Phase(nc)
    with ctx:
        x = ctx.enter_context(nc.sbuf_tensor(name + "_x", [P, KD, T], F32))
        gain = ctx.enter_context(nc.sbuf_tensor(name + "_gain", [P, KD], F32))
        square = ctx.enter_context(nc.sbuf_tensor(name + "_square", [P, 2, T], F32))
        rstd = ctx.enter_context(nc.sbuf_tensor(name + "_rstd", [P, T], F32))
        total = ctx.enter_context(nc.psum_tensor(name + "_total", [P, 2, HALF], F32))
        x_in = [ctx.semaphore(f"{name}_x_in{k}") for k in range(KD)]
        gain_in = ctx.semaphore(name + "_gain_in")
        squared = ctx.semaphore(name + "_squared")
        summed = ctx.semaphore(name + "_summed")
        inverse = ctx.semaphore(name + "_inverse")
        root = ctx.semaphore(name + "_root")
        scaled = ctx.semaphore(name + "_scaled")
        high = ctx.semaphore(name + "_high")
        block = ctx.enter_context(nc.Block())

        @block.sync
        def _(sp):
            sp.dma_start(gain[:], gain_dram).then_inc(gain_in, 16)
            for k in range(KD):
                sp.dma_start(x[:, k, :], x_dram[k * P:(k + 1) * P, :]).then_inc(x_in[k], 16)

        @block.scalar
        def _(act):
            for k in range(KD):
                act.wait_ge(x_in[k], 16)
                if k >= 2:
                    act.wait_ge(summed, k - 1)
                act.activation(square[:, k % 2, :], x[:, k, :], ACT.Square).then_inc(squared, 1)
            act.wait_ge(inverse, 3)
            act.activation(rstd[:], rstd[:], ACT.Sqrt).then_inc(root, 1)
            for k in range(KD):
                act.wait_ge(scaled, k + 1)
                act.activation(h_hi[:, k, :], x[:, k, :], ACT.Copy).then_inc(high, 1)

        @block.tensor
        def _(pe):
            for k in range(KD):
                pe.wait_ge(squared, k + 1)
                for half in range(2):
                    mm = pe.matmul(total[:, half, :], ones, square[:, k % 2, half * HALF:(half + 1) * HALF],
                                   start=(k == 0), stop=(k == KD - 1))
                mm.then_inc(summed, 1)

        @block.vector
        def _(dve):
            dve.wait_ge(summed, KD)
            dve.tensor_scalar(square[:, 0, :], total[:, :, :].rearrange("p a b -> p (a b)"), 1.0 / D, EPS,
                              ALU.mult, ALU.add).then_inc(inverse, 1)
            dve.wait_ge(inverse, 1)
            dve.reciprocal(rstd[:], square[:, 0, :]).then_inc(inverse, 2)
            dve.wait_ge(gain_in, 16)
            dve.wait_ge(root, 1)
            dve.tensor_tensor(square[:, 1, :], rstd[:], rstd[:], ALU.mult).then_inc(inverse, 1)
            dve.wait_ge(inverse, 4)
            dve.tensor_tensor(square[:, 1, :], square[:, 1, :], square[:, 0, :], ALU.mult).then_inc(inverse, 1)
            dve.wait_ge(inverse, 5)
            dve.tensor_scalar(square[:, 1, :], square[:, 1, :], -0.5, 1.5, ALU.mult, ALU.add).then_inc(inverse, 1)
            dve.wait_ge(inverse, 6)
            dve.tensor_tensor(rstd[:], rstd[:], square[:, 1, :], ALU.mult).then_inc(inverse, 1)
            dve.wait_ge(inverse, 7)
            for k in range(KD + 1):
                if k < KD:
                    dve.scalar_tensor_tensor(out=x[:, k, :], in0=x[:, k, :], scalar=gain[:, k:k + 1], in1=rstd[:],
                                             op0=ALU.mult, op1=ALU.mult).then_inc(scaled, 1)
                if k >= 1:
                    dve.wait_ge(high, k)
                    dve.wait_ge(scaled, k)
                    dve.tensor_tensor(h_lo[:, k - 1, :], x[:, k - 1, :], h_hi[:, k - 1, :].bitcast(F32), ALU.subtract)


def split_phase(nc, name, a_dram, tiles, a_hi, a_lo):
    ctx = Phase(nc)
    with ctx:
        raw = ctx.enter_context(nc.sbuf_tensor(name + "_raw", [P, 2, T], F32))
        raw_in = [ctx.semaphore(f"{name}_raw_in{b}") for b in range(2)]
        high = ctx.semaphore(name + "_high")
        low = ctx.semaphore(name + "_low")
        block = ctx.enter_context(nc.Block())

        @block.sync
        def _(sp):
            for k in range(tiles):
                if k >= 2:
                    sp.wait_ge(low, k - 1)
                sp.dma_start(raw[:, k % 2, :], a_dram[k * P:(k + 1) * P, :]).then_inc(raw_in[k % 2], 16)

        @block.scalar
        def _(act):
            for k in range(tiles):
                act.wait_ge(raw_in[k % 2], 16 * (k // 2 + 1))
                act.activation(a_hi[:, k, :], raw[:, k % 2, :], ACT.Copy).then_inc(high, 1)

        @block.vector
        def _(dve):
            for k in range(tiles):
                dve.wait_ge(high, k + 1)
                dve.tensor_tensor(a_lo[:, k, :], raw[:, k % 2, :], a_hi[:, k, :].bitcast(F32),
                                  ALU.subtract).then_inc(low, 1)


def linear_phase(nc, name, a_hi, a_lo, kt, w_dram, nt, out_dram, kind="copy", extra1=None, extra2=None):
    extras = [e for e in (extra1, extra2) if e is not None]
    assert nt == 1 or nt % 2 == 0
    turns = (nt - 1) // 2
    odd = nt % 2
    uses = [turns + 1, turns + 1 - odd]
    ctx = Phase(nc)
    with ctx:
        raw = ctx.enter_context(nc.sbuf_tensor(name + "_raw", [P, 2, kt * P], F32))
        w_hi = ctx.enter_context(nc.sbuf_tensor(name + "_w_hi", [P, 2, kt * P], F32R))
        w_lo = ctx.enter_context(nc.sbuf_tensor(name + "_w_lo", [P, 2, kt * P], F32R))
        out = ctx.enter_context(nc.sbuf_tensor(name + "_out", [P, 2, T], F32))
        side = [ctx.enter_context(nc.sbuf_tensor(f"{name}_side{j}", [P, 2, T], F32)) for j in range(len(extras))]
        acc = ctx.enter_context(nc.psum_tensor(name + "_acc", [P, 4, HALF], F32))
        two = range(2)
        raw_in = [ctx.semaphore(f"{name}_raw_in{b}") for b in two]
        high = [ctx.semaphore(f"{name}_high{b}") for b in two]
        low = [ctx.semaphore(f"{name}_low{b}") for b in two]
        product = [ctx.semaphore(f"{name}_product{b}") for b in two]
        drained = [ctx.semaphore(f"{name}_drained{b}") for b in two]
        side_in = [ctx.semaphore(f"{name}_side_in{b}") for b in two]
        gated = [ctx.semaphore(f"{name}_gated{b}") for b in two]
        step = ctx.semaphore(name + "_step")
        storing = ctx.semaphore(name + "_storing")
        stored = [ctx.semaphore(f"{name}_stored{b}") for b in two]
        block = ctx.enter_context(nc.Block())

        def bank(b):
            return acc[:, 2 * b:2 * b + 2, :].rearrange("p a b -> p (a b)")

        @block.sync
        def _(sp):
            for b in two:
                sp.sem_inc(stored[b], 16)

            def load(n, b):
                sp.dma_start(raw[:, b, :], w_dram[bass.ds(n * P, P), :]).then_inc(raw_in[b], 16)

            def load_sides(n, b, use):
                if extras:
                    sp.wait_ge(drained[b], use + 1)
                    for j, e in enumerate(extras):
                        sp.dma_start(side[j][:, b, :], e[bass.ds(n * P, P), :]).then_inc(side_in[b], 16)

            def store(n, b, use):
                sp.wait_ge(drained[b], use + 2)
                sp.sem_inc(storing, 1)
                sp.dma_start(out_dram[bass.ds(n * P, P), :], out[:, b, :]).then_inc(stored[b], 16)

            def next_load(n, b, use):
                sp.wait_ge(low[b], use + 1)
                load(n, b)

            load(0, 0)
            if nt > 1:
                load(1, 1)
            load_sides(0, 0, 0)
            if turns:
                with sp.Fori(0, turns) as i:
                    next_load(2 * i + 2, 0, i)
                    load_sides(2 * i + 1, 1, i)
                    store(2 * i, 0, i)
                    next_load(2 * i + 3, 1, i)
                    load_sides(2 * i + 2, 0, i + 1)
                    store(2 * i + 1, 1, i)
            if not odd:
                load_sides(nt - 1, 1, turns)
                store(nt - 2, 0, turns)
                store(nt - 1, 1, turns)
            else:
                store(nt - 1, 0, turns)
            for b in two:
                sp.wait_ge(stored[b], 16 * (uses[b] + 1))

        @block.scalar
        def _(act):
            def split(b, use):
                act.wait_ge(raw_in[b], use * 16 + 16)
                act.wait_ge(product[b], use + 1)
                act.activation(w_hi[:, b, :], raw[:, b, :], ACT.Copy).then_inc(high[b], 1)

            def gate(b, use):
                if kind in ("gate", "gate_add"):
                    act.wait_ge(side_in[b], use * (16 * len(extras)) + 16 * len(extras))
                    act.activation(side[0][:, b, :], side[0][:, b, :], ACT.Sigmoid).then_inc(gated[b], 1)
                if kind == "final":
                    act.wait_ge(product[b], use + 2)
                    act.wait_ge(stored[b], use * 16 + 16)
                    act.activation(out[:, b, :], bank(b), ACT.Sigmoid).then_inc(gated[b], 1)

            split(0, 0)
            if turns:
                with act.Fori(0, turns) as i:
                    split(1, i)
                    gate(0, i)
                    split(0, i + 1)
                    gate(1, i)
            if not odd:
                split(1, turns)
                gate(0, turns)
                gate(1, turns)
            else:
                gate(0, turns)

        @block.vector
        def _(dve):
            for b in two:
                dve.sem_inc(drained[b], 1)

            def split(b, use):
                dve.wait_ge(high[b], use + 1)
                dve.tensor_tensor(w_lo[:, b, :], raw[:, b, :], w_hi[:, b, :].bitcast(F32),
                                  ALU.subtract).then_inc(low[b], 1)

            def epilogue(b, use, n_step):
                dve.wait_ge(product[b], use + 2)
                dve.wait_ge(stored[b], use * 16 + 16)
                o, s0 = out[:, b, :], (side[0][:, b, :] if extras else None)
                if kind == "copy":
                    dve.tensor_copy(o, bank(b)).then_inc(drained[b], 1)
                elif kind == "add":
                    dve.wait_ge(side_in[b], use * 16 + 16)
                    dve.tensor_tensor(o, bank(b), s0, ALU.add).then_inc(drained[b], 1)
                elif kind == "gate":
                    dve.wait_ge(gated[b], use + 1)
                    dve.tensor_tensor(o, bank(b), s0, ALU.mult).then_inc(drained[b], 1)
                elif kind == "gate_add":
                    dve.wait_ge(gated[b], use + 1)
                    dve.tensor_tensor(o, bank(b), s0, ALU.mult).then_inc(step, 1)
                    dve.wait_ge(step, n_step)
                    dve.tensor_tensor(o, o, side[1][:, b, :], ALU.add).then_inc(drained[b], 1)
                elif kind == "final":
                    dve.wait_ge(gated[b], use + 1)
                    dve.wait_ge(side_in[b], use * 32 + 32)
                    dve.tensor_tensor(o, o, s0, ALU.mult).then_inc(step, 1)
                    dve.wait_ge(step, n_step)
                    dve.tensor_tensor(o, o, side[1][:, b, :], ALU.add).then_inc(drained[b], 1)

            split(0, 0)
            if turns:
                with dve.Fori(0, turns) as i:
                    split(1, i)
                    epilogue(0, i, i * 2 + 1)
                    split(0, i + 1)
                    epilogue(1, i, i * 2 + 2)
            if not odd:
                split(1, turns)
                epilogue(0, turns, 2 * turns + 1)
                epilogue(1, turns, 2 * turns + 2)
            else:
                epilogue(0, turns, 2 * turns + 1)

        @block.tensor
        def _(pe):
            for b in two:
                pe.sem_inc(product[b], 1)

            def multiply(b, use):
                pe.wait_ge(low[b], use + 1)
                pe.wait_ge(drained[b], use + 1)
                for k in range(kt):
                    for n_pass, (w, a) in enumerate(((w_hi, a_hi), (w_hi, a_lo), (w_lo, a_hi))):
                        for half in range(2):
                            mm = pe.matmul(acc[:, 2 * b + half, :], w[:, b, k * P:(k + 1) * P],
                                           a[:, k, half * HALF:(half + 1) * HALF],
                                           start=(k == 0 and n_pass == 0), stop=(k == kt - 1 and n_pass == 2))
                mm.then_inc(product[b], 1)

            if turns:
                with pe.Fori(0, turns) as i:
                    multiply(0, i)
                    multiply(1, i)
            multiply(0, turns)
            if not odd:
                multiply(1, turns)


Q_HEADS, KV_HEADS, HEAD_DIM = 16, 4, 64
Q_ROWS, K_ROWS, V_ROWS = 0, 1024, 1280
HEAD_ORDER = (0, 2, 1, 3)
BLOCK_KEYS = 192
BAND = 256
REL_COUNT = BLOCK_KEYS + P - 1
NORMED = (Q_HEADS + KV_HEADS) // 2


def attention_phase(nc, name, proj, qk_gain_dram, sink_dram, rel_bias_dram, onehot_dram, band_mask_dram,
                    flip_dram, rel_row_dram, out_dram, const):
    ctx = Phase(nc)
    with ctx:
        def sb(what, shape, dt=F32):
            return ctx.enter_context(nc.sbuf_tensor(f"{name}_{what}", shape, dt))

        def sem(what):
            return ctx.semaphore(f"{name}_{what}")

        qk = sb("qk", [P, NORMED, T])
        k_swap = sb("k_swap", [P, 2, T])
        v_t = sb("v_t", [P, 2, T])
        v = sb("v", [P, KD, KV_HEADS * HEAD_DIM])
        gain = sb("gain", [P, 2])
        square = sb("square", [P, 2, T])
        rstd = sb("rstd", [32, 3, T])
        bias = sb("bias", [P, Q_HEADS, BLOCK_KEYS])
        mask = sb("mask", [P, BLOCK_KEYS])
        onehot = sb("onehot", [32, REL_COUNT])
        rel_bias = sb("rel_bias", [32, Q_HEADS])
        rel_row = sb("rel_row", [Q_HEADS, REL_COUNT])
        sink = sb("sink", [P, Q_HEADS])
        score = sb("score", [P, 2, 4, BLOCK_KEYS])
        prob = sb("prob", [P, 2, 4, BAND])
        prob_t = sb("prob_t", [P, 2, 4, P])
        top = sb("top", [P, 2, 4])
        neg_top = sb("neg_top", [P, 2, 4])
        sink_gap = sb("sink_gap", [P, 2, 4])
        sink_exp = sb("sink_exp", [P, 2, 4])
        denom = sb("denom", [P, 2, 4])
        inverse = sb("inverse", [P, 2, 4])
        out = sb("out", [P, KD, T])

        qk_in = [sem(f"qk_in{k}") for k in range(NORMED)]
        v_in, small_in, swapped, rel_in, stored = (sem(s) for s in ("v_in", "small_in", "swapped", "rel_in", "stored"))
        squared, summed, rooting, rooted, spread, normed = (
            sem(s) for s in ("squared", "summed", "rooting", "rooted", "spread", "normed"))
        v_turned, v_ready, row_made, row_ready, row_stored, flipped, bias_ready, zeroed = (
            sem(s) for s in ("v_turned", "v_ready", "row_made", "row_ready", "row_stored", "flipped", "bias_ready", "zeroed"))

        with ExitStack() as first:
            norm_acc = first.enter_context(nc.psum_tensor(name + "_norm_acc", [P, 2, 2, HALF], F32))
            turn_acc = first.enter_context(nc.psum_tensor(name + "_turn_acc", [P, 2, HALF], F32))
            bias_rev = first.enter_context(nc.sbuf_tensor(name + "_bias_rev", [P, Q_HEADS, BLOCK_KEYS], F32))
            flip = first.enter_context(nc.sbuf_tensor(name + "_flip", [P, P], F32))
            row_acc = first.enter_context(nc.psum_tensor(name + "_row_acc", [P, HALF], F32))
            block = first.enter_context(nc.Block())

            @block.sync
            def _(sp):
                for dst, src in ((gain[:], qk_gain_dram), (rel_bias[:], rel_bias_dram), (onehot[:], onehot_dram),
                                 (mask[:], band_mask_dram), (flip[:], flip_dram)):
                    sp.dma_start(dst, src).then_inc(small_in, 16)
                sp.dma_start(sink[:], sink_dram.partition_broadcast(P)).then_inc(small_in, 16)
                for k in range(2):
                    sp.dma_start(v_t[:, k, :], proj[V_ROWS + k * P:V_ROWS + (k + 1) * P, :]).then_inc(v_in, 16)
                for k in range(NORMED):
                    sp.dma_start(qk[:, k, :], proj[k * P:(k + 1) * P, :]).then_inc(qk_in[k], 16)
                sp.wait_ge(row_ready, 1)
                sp.dma_start(rel_row_dram, rel_row[:]).then_inc(row_stored, 16)
                sp.wait_ge(row_stored, 16)
                toeplitz = bass.AP(rel_row_dram.tensor, 0, [[1, P], [REL_COUNT, Q_HEADS], [1, BLOCK_KEYS]])
                sp.dma_start(bias_rev[:], toeplitz).then_inc(rel_in, 16)
                sp.wait_ge(normed, NORMED)
                for k in range(2):
                    for s in range(2):
                        sp.dma_start(k_swap[64 * s:64 * s + 64, k, :],
                                     qk[64 - 64 * s:128 - 64 * s, 8 + k, :]).then_inc(swapped, 16)
                sp.wait_ge(swapped, 64)

            @block.scalar
            def _(act):
                for k in range(NORMED):
                    act.wait_ge(qk_in[k], 16)
                    if k >= 2:
                        act.wait_ge(summed, k - 1)
                    act.activation(square[:, k % 2, :], qk[:, k, :], ACT.Square).then_inc(squared, 1)
                act.wait_ge(rooting, 2)
                act.activation(rstd[:, 0, :], rstd[:, 1, :], ACT.Sqrt).then_inc(rooted, 1)

            @block.tensor
            def _(pe):
                pe.wait_ge(small_in, 96)
                pe.matmul(row_acc[:Q_HEADS, :REL_COUNT], rel_bias[:], onehot[:], start=True, stop=True).then_inc(row_made, 1)
                pe.wait_ge(v_in, 32)
                for m in range(KD):
                    if m >= 2:
                        pe.wait_ge(v_ready, m - 1)
                    for k in range(2):
                        mm = pe.transpose(turn_acc[:, m % 2, k * P:(k + 1) * P], v_t[:, k, m * P:(m + 1) * P],
                                          const.identity)
                    mm.then_inc(v_turned, 1)
                for k in range(NORMED):
                    pe.wait_ge(squared, k + 1)
                    for half in range(2):
                        mm = pe.matmul(norm_acc[:32, 0, half, :], const.head_pick[:, k, :],
                                       square[:, k % 2, half * HALF:(half + 1) * HALF],
                                       start=(k == 0), stop=(k == NORMED - 1))
                    mm.then_inc(summed, 1)
                pe.wait_ge(rooting, 6)
                for k in range(NORMED):
                    if k >= 2:
                        pe.wait_ge(normed, k - 1)
                    for half in range(2):
                        mm = pe.matmul(norm_acc[:, k % 2, half, :], const.head_spread[:, k, :],
                                       rstd[:, 0, half * HALF:(half + 1) * HALF], start=True, stop=True)
                    mm.then_inc(spread, 1)
                pe.wait_ge(rel_in, 16)
                for n in range(Q_HEADS // 2):
                    pe.wait_ge(v_ready, KD)
                    if n >= 2:
                        pe.wait_ge(bias_ready, n - 1)
                    pe.matmul(turn_acc[:, n % 2, :2 * BLOCK_KEYS], flip[:],
                              bias_rev[:, 2 * n:2 * n + 2, :].rearrange("p a b -> p (a b)"),
                              start=True, stop=True).then_inc(flipped, 1)

            @block.vector
            def _(dve):
                dve.wait_ge(row_made, 1)
                dve.tensor_copy(rel_row[:], row_acc[:Q_HEADS, :REL_COUNT]).then_inc(row_ready, 1)
                for m in range(KD):
                    dve.wait_ge(v_turned, m + 1)
                    dve.tensor_copy(v[:, m, :], turn_acc[:, m % 2, :2 * P]).then_inc(v_ready, 1)
                dve.memset(prob[:, :, :, 0:64], 0.0).then_inc(zeroed, 1)
                dve.wait_ge(summed, NORMED)
                mean, root, aux = rstd[:, 2, :], rstd[:, 0, :], rstd[:, 1, :]
                dve.tensor_scalar(mean, norm_acc[:32, 0, :, :].rearrange("p a b -> p (a b)"), 1.0 / HEAD_DIM, EPS,
                                  ALU.mult, ALU.add).then_inc(rooting, 1)
                dve.wait_ge(rooting, 1)
                dve.reciprocal(aux, mean).then_inc(rooting, 1)
                dve.wait_ge(rooted, 1)
                dve.tensor_tensor(aux, root, root, ALU.mult).then_inc(rooting, 1)
                dve.wait_ge(rooting, 3)
                dve.tensor_tensor(aux, aux, mean, ALU.mult).then_inc(rooting, 1)
                dve.wait_ge(rooting, 4)
                dve.tensor_scalar(aux, aux, -0.5, 1.5, ALU.mult, ALU.add).then_inc(rooting, 1)
                dve.wait_ge(rooting, 5)
                dve.tensor_tensor(root, root, aux, ALU.mult).then_inc(rooting, 1)
                for k in range(NORMED):
                    dve.wait_ge(spread, k + 1)
                    g = gain[:, 0:1] if k < 8 else gain[:, 1:2]
                    dve.scalar_tensor_tensor(out=qk[:, k, :], in0=qk[:, k, :], scalar=g,
                                             in1=norm_acc[:, k % 2, :, :].rearrange("p a b -> p (a b)"),
                                             op0=ALU.mult, op1=ALU.mult).then_inc(normed, 1)
                dve.wait_ge(small_in, 96)
                for n in range(Q_HEADS // 2):
                    dve.wait_ge(flipped, n + 1)
                    dve.tensor_tensor(bias[:, 2 * n:2 * n + 2, :],
                                      turn_acc[:, n % 2, :2 * BLOCK_KEYS].rearrange("p (a b) -> p a b", a=2),
                                      mask[:].unsqueeze(1).to_broadcast([P, 2, BLOCK_KEYS]), ALU.add).then_inc(bias_ready, 1)

        scores_made, scaled, topped, exped, probs_ready, turned, probs_turned, summed_up, out_ready, chain = (
            sem(s) for s in ("scores_made", "scaled", "topped", "exped", "probs_ready", "turned", "probs_turned",
                             "summed_up", "out_ready", "chain"))
        STEPS = KD * KV_HEADS
        with ExitStack() as second:
            s_acc = second.enter_context(nc.psum_tensor(name + "_s_acc", [P, 2, 4, 256], F32))
            t_acc = second.enter_context(nc.psum_tensor(name + "_t_acc", [P, 2, 4, P], F32))
            o_acc = second.enter_context(nc.psum_tensor(name + "_o_acc", [P, 4, P], F32))
            block = second.enter_context(nc.Block())

            def reach(m):
                return 64 if m == 0 else 0

            @block.tensor
            def _(pe):
                def scores(s):
                    m, kv = divmod(s, KV_HEADS)
                    first_key = m * P - 64 + reach(m)
                    if s >= 2:
                        pe.wait_ge(scaled, s - 1)
                    for h in range(4):
                        head = 4 * kv + HEAD_ORDER[h]
                        at = 64 * (head % 2)
                        keys = qk[:, 8 + kv // 2, :] if kv % 2 == head % 2 else k_swap[:, kv // 2, :]
                        mm = pe.matmul(s_acc[:, s % 2, h, reach(m):BLOCK_KEYS],
                                       qk[at:at + 64, head // 2, m * P:(m + 1) * P],
                                       keys[at:at + 64, first_key:(m + 1) * P], start=True, stop=True)
                    mm.then_inc(scores_made, 1)

                scores(0)
                scores(1)
                for s in range(STEPS):
                    m, kv = divmod(s, KV_HEADS)
                    halves = (1,) if m == 0 else (0, 1)
                    pe.wait_ge(probs_ready, s + 1)
                    if s >= 1:
                        pe.wait_ge(probs_turned, s)
                    for half in halves:
                        for h in range(4):
                            mm = pe.transpose(t_acc[:, half, h, :], prob[:, s % 2, h, half * P:(half + 1) * P],
                                              const.identity)
                    mm.then_inc(turned, 1)
                    if s + 2 < STEPS:
                        scores(s + 2)
                    pe.wait_ge(probs_turned, s + 1)
                    if s >= 1:
                        pe.wait_ge(out_ready, s)
                    for parity in range(2):
                        for n, half in enumerate(halves):
                            mm = pe.matmul(o_acc[64 * parity:64 * parity + 64, 0:2, :],
                                           v[:, m - 1 + half, kv * HEAD_DIM:(kv + 1) * HEAD_DIM],
                                           prob_t[:, half, 2 * parity:2 * parity + 2, :], start=(n == 0), stop=(n == len(halves) - 1))
                    mm.then_inc(summed_up, 1)

            @block.scalar
            def _(act):
                def exps(s):
                    m, kv = divmod(s, KV_HEADS)
                    lo = reach(m)
                    act.wait_ge(topped, s + 1)
                    if s >= 2:
                        act.wait_ge(turned, s - 1)
                        act.wait_ge(probs_ready, s - 1)
                    for h in range(4):
                        act.activation(prob[:, s % 2, h, 64 + lo:BAND], score[:, s % 2, h, lo:], ACT.Exp,
                                       bias=neg_top[:, s % 2, h:h + 1], accum_out=denom[:, s % 2, h:h + 1])
                    act.activation(sink_exp[:, s % 2, :], sink_gap[:, s % 2, :], ACT.Exp).then_inc(exped, 1)

                exps(0)
                for s in range(STEPS):
                    if s + 1 < STEPS:
                        exps(s + 1)
                    half = slice(1, 2) if s < KV_HEADS else slice(0, 2)
                    act.wait_ge(turned, s + 1)
                    if s >= 1:
                        act.wait_ge(summed_up, s)
                    act.activation(prob_t[:, half, :, :], t_acc[:, half, :, :], ACT.Copy).then_inc(probs_turned, 1)

            @block.vector
            def _(dve):
                links = [0]

                def link(instruction):
                    links[0] += 1
                    instruction.then_inc(chain, 1)
                    dve.wait_ge(chain, links[0])

                def tops(s):
                    m, kv = divmod(s, KV_HEADS)
                    b, lo, heads = s % 2, reach(m), slice(4 * kv, 4 * kv + 4)
                    dve.wait_ge(scores_made, s + 1)
                    if s >= 2:
                        dve.wait_ge(exped, s - 1)
                    ins = dve.scalar_tensor_tensor(out=score[:, b, :, lo:], in0=s_acc[:, b, :, lo:BLOCK_KEYS],
                                                   scalar=HEAD_DIM ** -0.5, in1=bias[:, heads, lo:],
                                                   op0=ALU.mult, op1=ALU.add)
                    ins.then_inc(scaled, 1)
                    dve.wait_ge(scaled, s + 1)
                    link(dve.tensor_reduce(top[:, b, :], score[:, b, :, lo:], AX.X, ALU.max))
                    link(dve.tensor_tensor(top[:, b, :], top[:, b, :], sink[:, heads], ALU.max))
                    dve.tensor_scalar(neg_top[:, b, :], top[:, b, :], -1.0, None, ALU.mult)
                    dve.tensor_tensor(sink_gap[:, b, :], sink[:, heads], top[:, b, :], ALU.subtract).then_inc(topped, 1)

                def normalise(s):
                    b = s % 2
                    dve.wait_ge(exped, s + 1)
                    link(dve.tensor_tensor(denom[:, b, :], denom[:, b, :], sink_exp[:, b, :], ALU.add))
                    link(dve.reciprocal(inverse[:, b, :], denom[:, b, :]))
                    lo = 64 + reach(s // KV_HEADS)
                    dve.tensor_tensor(prob[:, b, :, lo:], prob[:, b, :, lo:],
                                      inverse[:, b, :].unsqueeze(2).to_broadcast([P, 4, BAND - lo]),
                                      ALU.mult).then_inc(probs_ready, 1)

                def drain(s):
                    m, kv = divmod(s, KV_HEADS)
                    dve.wait_ge(summed_up, s + 1)
                    dve.tensor_copy(out[:, 2 * kv:2 * kv + 2, m * P:(m + 1) * P], o_acc[:, 0:2, :]).then_inc(out_ready, 1)

                tops(0)
                for s in range(STEPS):
                    if s + 1 < STEPS:
                        tops(s + 1)
                    normalise(s)
                    if s >= 1:
                        drain(s - 1)
                drain(STEPS - 1)

            @block.sync
            def _(sp):
                sp.wait_ge(out_ready, STEPS)
                for k in range(KD):
                    sp.dma_start(out_dram[k * P:(k + 1) * P, :], out[:, k, :]).then_inc(stored, 16)
                sp.wait_ge(stored, 16 * KD)


SSM_TILES = 16
SSM_HEADS = 32
GROUPS = 4
CHUNKS = T // P
CONV_TILES = 24
TAPS = 4
Z_ROWS, XBC_ROWS = 1536, 3584


def ssm_phase(nc, name, proj, dt_dram, conv_dram, head_dram, tile_dram, causal_dram, out_dram, const):
    ctx = Phase(nc)
    with ctx:
        def sb(what, shape, dt=F32):
            return ctx.enter_context(nc.sbuf_tensor(f"{name}_{what}", shape, dt))

        def sem(what):
            return ctx.semaphore(f"{name}_{what}")

        conv = sb("conv", [P, CONV_TILES, T])
        a_t = sb("a_t", [32, T])
        a = sb("a", [P, CHUNKS, SSM_HEADS])
        dt = sb("dt", [P, CHUNKS, SSM_HEADS])
        dt_out = sb("dt_out", [P, CHUNKS, SSM_HEADS])
        decay = sb("decay", [P, CHUNKS, SSM_HEADS])
        tile_par = sb("tile_par", [P, SSM_TILES, 2])
        identity16 = sb("identity16", [P, P], BF16)
        causal16 = sb("causal16", [P, 4, P], BF16)

        with ExitStack() as first:
            def fsb(what, shape, dt=F32):
                return first.enter_context(nc.sbuf_tensor(f"{name}_{what}", shape, dt))

            conv_in = fsb("conv_in", [P, 2, T + TAPS - 1])
            mixed = fsb("mixed", [P, 2, T])
            taps = fsb("taps", [P, CONV_TILES, TAPS + 1])
            head = fsb("head", [32, 2])
            rate = fsb("rate", [32, 1])
            raw = fsb("dt_raw", [32, T])
            one = fsb("one", [32, P])
            work = [fsb(f"work{k}", [32, T]) for k in range(6)]
            spread_decay = fsb("spread_decay", [32, CHUNKS, 32])
            causal = fsb("causal", [P, P])
            t_acc = first.enter_context(nc.psum_tensor(name + "_turn_acc", [P, 3, HALF], F32))
            d_acc = first.enter_context(nc.psum_tensor(name + "_decay_acc", [P, HALF], F32))
            small_in, dt_in, chain, acted, turned, padded, mixed_up, silued = (
                sem(s) for s in ("small_in", "dt_in", "chain", "acted", "turned", "padded", "mixed_up", "silued"))
            tile_in = [sem(f"tile_in{b}") for b in range(2)]
            block = first.enter_context(nc.Block())

            @block.sync
            def _(sp):
                for dst, src in ((head[:], head_dram), (taps[:], conv_dram), (tile_par[:], tile_dram),
                                 (causal[:], causal_dram)):
                    sp.dma_start(dst, src).then_inc(small_in, 16)
                sp.dma_start(raw[:], dt_dram[0:32, :]).then_inc(dt_in, 16)
                sp.wait_ge(padded, 1)
                for k in range(CONV_TILES):
                    if k >= 2:
                        sp.wait_ge(mixed_up, k - 1)
                    sp.dma_start(conv_in[:, k % 2, TAPS - 1:],
                                 proj[XBC_ROWS + k * P:XBC_ROWS + (k + 1) * P, :]).then_inc(tile_in[k % 2], 16)

            @block.scalar
            def _(act):
                act.wait_ge(chain, 2)
                act.activation(work[1][:], work[1][:], ACT.Exp, scale=-1.0).then_inc(acted, 1)
                act.wait_ge(small_in, 64)
                act.activation(rate[:], head[:, 1:2], ACT.Exp).then_inc(acted, 1)
                act.wait_ge(chain, 3)
                act.activation(work[3][:], work[2][:], ACT.Ln).then_inc(acted, 1)
                act.wait_ge(chain, 13 + CHUNKS + 1)
                act.activation(work[0][:], work[0][:], ACT.Exp, scale=-1.0).then_inc(acted, 1)
                act.activation(work[2][:, 0:CHUNKS], a_t[:, P - 1::P], ACT.Exp).then_inc(acted, 1)
                for k in range(CONV_TILES):
                    act.wait_ge(mixed_up, k + 1)
                    act.activation(conv[:, k, :], mixed[:, k % 2, :], ACT.Silu).then_inc(silued, 1)

            @block.tensor
            def _(pe):
                pe.wait_ge(chain, 13 + CHUNKS + 2)
                for j, src in enumerate((a_t, work[5], work[0])):
                    for c in range(CHUNKS):
                        mm = pe.transpose(t_acc[:, j, c * 32:(c + 1) * 32], src[:, c * P:(c + 1) * P],
                                          const.identity[0:32, 0:32])
                mm.then_inc(turned, 1)
                pe.wait_ge(chain, 13 + CHUNKS + 3)
                pe.matmul(d_acc[:, 0:256], const.ones[0:32, :], spread_decay[:, :, :].rearrange("p a b -> p (a b)"),
                          start=True, stop=True).then_inc(turned, 1)

            @block.vector
            def _(dve):
                links = [0]

                def link(instruction):
                    links[0] += 1
                    instruction.then_inc(chain, 1)
                    dve.wait_ge(chain, links[0])

                x, e, u, log, w4, dt_t = (w[:] for w in work)
                dve.memset(conv_in[:, :, 0:TAPS - 1], 0.0).then_inc(padded, 1)
                dve.memset(one[:], 1.0)
                dve.wait_ge(small_in, 64)
                dve.wait_ge(dt_in, 16)
                link(dve.tensor_scalar(x, raw[:], head[:, 0:1], None, ALU.add))
                link(dve.scalar_tensor_tensor(out=e, in0=x, scalar=-1.0, in1=x, op0=ALU.mult, op1=ALU.max))
                dve.wait_ge(acted, 1)
                link(dve.tensor_scalar(u, e, 1.0, None, ALU.add))
                link(dve.tensor_scalar(w4, u, -1.0, None, ALU.add))
                link(dve.tensor_scalar(dt_t, w4, 0.0, None, ALU.is_equal))
                link(dve.tensor_tensor(w4, w4, dt_t, ALU.add))
                link(dve.tensor_tensor(dt_t, dt_t, e, ALU.mult))
                dve.wait_ge(acted, 3)
                link(dve.tensor_tensor(e, log, e, ALU.mult))
                link(dve.reciprocal(log, w4))
                link(dve.tensor_tensor(e, e, log, ALU.mult))
                link(dve.tensor_tensor(dt_t, dt_t, e, ALU.add))
                link(dve.scalar_tensor_tensor(out=dt_t, in0=x, scalar=0.0, in1=dt_t, op0=ALU.max, op1=ALU.add))
                link(dve.tensor_scalar(x, dt_t, rate[:, 0:1], -1.0, ALU.mult, ALU.mult))
                for c in range(CHUNKS):
                    at = slice(c * P, (c + 1) * P)
                    link(dve.tensor_tensor_scan(out=a_t[:, at], data0=one[:], data1=x[:, at], initial=0.0,
                                                op0=ALU.mult, op1=ALU.add))
                a3 = a_t[:].rearrange("p (c t) -> p c t", c=CHUNKS)
                link(dve.tensor_tensor(x.rearrange("p (c t) -> p c t", c=CHUNKS), a3,
                                       a3[:, :, P - 1:P].to_broadcast([32, CHUNKS, P]), ALU.subtract))
                dve.wait_ge(acted, 5)
                link(dve.tensor_tensor(x, x, dt_t, ALU.mult))
                link(dve.tensor_tensor(spread_decay[:], work[2][:, 0:CHUNKS].unsqueeze(2).to_broadcast([32, CHUNKS, 32]),
                                       const.identity[0:32, 0:32].unsqueeze(1).to_broadcast([32, CHUNKS, 32]), ALU.mult))
                dve.wait_ge(turned, 2)
                for j, dst in enumerate((a, dt, dt_out)):
                    dve.tensor_copy(dst[:].rearrange("p a b -> p (a b)"), t_acc[:, j, 0:256])
                dve.tensor_copy(decay[:].rearrange("p a b -> p (a b)"), d_acc[:, 0:256])
                dve.tensor_copy(identity16[:], const.identity)
                dve.tensor_copy(causal16[:], causal[:].unsqueeze(1).to_broadcast([P, 4, P]))
                for k in range(CONV_TILES):
                    b = k % 2
                    dve.wait_ge(tile_in[b], 16 * (k // 2 + 1))
                    if k >= 2:
                        dve.wait_ge(silued, k - 1)
                    link(dve.tensor_scalar(mixed[:, b, :], conv_in[:, b, 3:3 + T], taps[:, k, 3:4], taps[:, k, 4:5],
                                           ALU.mult, ALU.add))
                    for tap in range(TAPS - 1):
                        ins = dve.scalar_tensor_tensor(out=mixed[:, b, :], in0=conv_in[:, b, tap:tap + T],
                                                       scalar=taps[:, k, tap:tap + 1], in1=mixed[:, b, :],
                                                       op0=ALU.mult, op1=ALU.add)
                        if tap < TAPS - 2:
                            link(ins)
                    ins.then_inc(mixed_up, 1)

        b_nat = sb("b_nat", [P, CHUNKS, GROUPS, P])
        cb = sb("cb", [P, GROUPS, T])
        with ExitStack() as second:
            turn = second.enter_context(nc.psum_tensor(name + "_b_acc", [P, 2, GROUPS, P], F32))
            dots = second.enter_context(nc.psum_tensor(name + "_cb_acc", [P, 2, HALF], F32))
            b_turned, b_read, dotted, dots_read = (sem(s) for s in ("b_turned", "b_read", "dotted", "dots_read"))
            block = second.enter_context(nc.Block())

            @block.tensor
            def _(pe):
                for c in range(CHUNKS):
                    at = slice(c * P, (c + 1) * P)
                    if c >= 2:
                        pe.wait_ge(b_read, c - 1)
                        pe.wait_ge(dots_read, c - 1)
                    for g in range(GROUPS):
                        mm = pe.transpose(turn[:, c % 2, g, :], conv[:, 16 + g, at], const.identity)
                    mm.then_inc(b_turned, 1)
                    for g in range(GROUPS):
                        mm = pe.matmul(dots[:, c % 2, g * P:(g + 1) * P], conv[:, 16 + g, at], conv[:, 20 + g, at],
                                       start=True, stop=True)
                    mm.then_inc(dotted, 1)

            @block.scalar
            def _(act):
                for c in range(CHUNKS):
                    act.wait_ge(b_turned, c + 1)
                    act.activation(b_nat[:, c, :, :], turn[:, c % 2, :, :], ACT.Copy).then_inc(b_read, 1)

            @block.vector
            def _(dve):
                for c in range(CHUNKS):
                    dve.wait_ge(dotted, c + 1)
                    dve.tensor_copy(cb[:, :, c * P:(c + 1) * P],
                                    dots[:, c % 2, :].rearrange("p (g t) -> p g t", g=GROUPS)).then_inc(dots_read, 1)

        scaled_x = sb("scaled_x", [P, CHUNKS, 2, 64])
        out_x = sb("out_x", [P, CHUNKS, 2, 64])
        weight = sb("weight", [P, 2, T])
        state = sb("state", [P, CHUNKS, 2, 64])
        grown = sb("grown", [P, T])
        z = sb("z", [P, 4, T])
        y = sb("y", [P, 4, T])
        square, aux = weight[:, 1, :], weight[:, 0, :]
        rstd = scaled_x[:, :, :, :].rearrange("p a b c -> p (a b c)")
        pair_a = ctx.enter_context(nc.psum_tensor(name + "_pair_a", [P, 2, HALF], F32))
        pair_b = ctx.enter_context(nc.psum_tensor(name + "_pair_b", [P, 2, HALF], F32))
        pair_c = ctx.enter_context(nc.psum_tensor(name + "_pair_c", [P, 2, HALF], F32))
        pair_d = ctx.enter_context(nc.psum_tensor(name + "_pair_d", [P, 2, HALF], F32))
        (x_turned, x_scaled, b_made, b_free, states_made, state_ready, decayed, weighted, grown_up, from_state, within,
         y_read, y_done, squared, summed, rooting, rooted, normed, z_in, z_ready, stored, chain2) = (
            sem(s) for s in ("x_turned", "x_scaled", "b_made", "b_free", "states_made", "state_ready", "decayed",
                             "weighted", "grown_up", "from_state", "within", "y_read", "y_done", "squared", "summed",
                             "rooting", "rooted", "normed", "z_in", "z_ready", "stored", "chain2"))
        block = ctx.enter_context(nc.Block())

        @block.sync
        def _(sp):
            for g in range(GROUPS):
                if g >= 1:
                    sp.wait_ge(summed, g)
                for k in range(4):
                    at = Z_ROWS + (4 * g + k) * P
                    sp.dma_start(z[:, k, :], proj[at:at + P, :]).then_inc(z_in, 16)
                if g >= 1:
                    for k in range(4):
                        sp.wait_ge(normed, 4 * (g - 1) + k + 1)
                        sp.dma_start(out_dram[(4 * (g - 1) + k) * P:(4 * (g - 1) + k + 1) * P, :],
                                     y[:, k, :]).then_inc(stored, 16)
            for k in range(4):
                sp.wait_ge(normed, 13 + k)
                sp.dma_start(out_dram[(12 + k) * P:(13 + k) * P, :], y[:, k, :]).then_inc(stored, 16)
            sp.wait_ge(stored, 16 * SSM_TILES)

        @block.tensor
        def _(pe):
            for j in range(SSM_TILES):
                g = j // 4
                if j >= 1:
                    pe.wait_ge(state_ready, j)
                for c in range(CHUNKS):
                    mm = pe.transpose(pair_a[:, c // 4, c % 4 * P:(c % 4 + 1) * P], conv[:, j, c * P:(c + 1) * P],
                                      const.identity)
                mm.then_inc(x_turned, 1)
                for h in range(3):
                    if 3 * j + h >= 1:
                        pe.wait_ge(b_free, 3 * j + h)
                    for half in range(2):
                        part = a_t[:, half * HALF:(half + 1) * HALF]
                        if h < 2:
                            pe.matmul(pair_b[:, half, :], const.head_spread[:, j, 64 * h:64 * h + 1].to_broadcast([32, P]),
                                      part, start=True, stop=False)
                            mm = pe.matmul(pair_b[:, half, :], identity16[:], causal16[:, :, :].rearrange("p a b -> p (a b)"),
                                           start=False, stop=True)
                        else:
                            mm = pe.matmul(pair_b[:, half, :], const.head_spread[:, j, :], part, start=True, stop=True)
                    mm.then_inc(b_made, 1)
                pe.wait_ge(x_scaled, j + 1)
                for c in range(CHUNKS - 1):
                    mm = pe.matmul(pair_a[:, c // 4, c % 4 * P:(c % 4 + 1) * P], b_nat[:, c, g, :],
                                   out_x[:, c, :, :].rearrange("p a b -> p (a b)"), start=True, stop=True)
                mm.then_inc(states_made, 1)
                pe.wait_ge(state_ready, j + 1)
                if j >= 1:
                    pe.wait_ge(y_read, j)
                if j >= 4 and j % 4 == 0:
                    pe.wait_ge(rooting, 7 * (j // 4 - 1) + 1)
                for c in range(1, CHUNKS):
                    mm = pe.matmul(pair_c[:, c // 4, c % 4 * P:(c % 4 + 1) * P],
                                   state[:, c, :, :].rearrange("p a b -> p (a b)"), conv[:, 20 + g, c * P:(c + 1) * P],
                                   start=True, stop=True)
                mm.then_inc(from_state, 1)
                for h in range(2):
                    pe.wait_ge(weighted, 2 * j + h + 1)
                    for c in range(CHUNKS):
                        mm = pe.matmul(pair_d[64 * h:64 * h + 64, c // 4, c % 4 * P:(c % 4 + 1) * P],
                                       scaled_x[:, c, h, :], weight[:, h, c * P:(c + 1) * P], start=True, stop=True)
                mm.then_inc(within, 1)
                if j % 4 == 3:
                    pe.wait_ge(y_read, j + 1)
                    for k in range(4):
                        pe.wait_ge(squared, 4 * g + k + 1)
                        for half in range(2):
                            mm = pe.matmul(pair_c[:, half, :], const.ones, z[:, k, half * HALF:(half + 1) * HALF],
                                           start=(k == 0), stop=(k == 3))
                    mm.then_inc(summed, 1)

        @block.scalar
        def _(act):
            for j in range(SSM_TILES):
                g = j // 4
                if j % 4 == 0:
                    act.wait_ge(z_in, 64 * (g + 1))
                    for k in range(4):
                        act.activation(z[:, k, :], z[:, k, :], ACT.Silu).then_inc(z_ready, 1)
                for h in range(2):
                    act.wait_ge(b_free, 3 * j + h + 1)
                    act.activation(weight[:, h, :], weight[:, h, :], ACT.Exp).then_inc(decayed, 1)
                act.wait_ge(b_made, 3 * j + 3)
                if j >= 1:
                    act.wait_ge(y_read, j)
                act.activation(grown[:], pair_b[:, :, :].rearrange("p a b -> p (a b)"), ACT.Exp).then_inc(b_free, 1)
                act.wait_ge(y_done, j + 1)
                act.activation(z[:, j % 4, :], y[:, j % 4, :], ACT.Square).then_inc(squared, 1)
                if j % 4 == 3:
                    act.wait_ge(rooting, 7 * g + 2)
                    act.activation(rstd, aux, ACT.Sqrt).then_inc(rooted, 1)

        @block.vector
        def _(dve):
            links = [0]

            def link(instruction):
                links[0] += 1
                instruction.then_inc(chain2, 1)
                dve.wait_ge(chain2, links[0])

            def flat(ap):
                return ap.rearrange("p a b -> p (a b)")

            for j in range(SSM_TILES):
                g = j // 4
                heads = slice(2 * j, 2 * j + 2)
                dve.wait_ge(x_turned, j + 1)
                if j >= 1:
                    dve.wait_ge(within, j)
                if j % 4 == 0 and j >= 4:
                    dve.wait_ge(normed, j)
                turned = pair_a[:, :, :].rearrange("p a (c h d) -> p (a c) h d", c=4, h=2)
                for dst, scale in ((scaled_x, dt), (out_x, dt_out)):
                    ins = dve.tensor_tensor(dst[:, :, :, :], turned,
                                            scale[:, :, heads].unsqueeze(3).to_broadcast([P, CHUNKS, 2, 64]), ALU.mult)
                ins.then_inc(x_scaled, 1)
                for h in range(2):
                    dve.wait_ge(b_made, 3 * j + h + 1)
                    if j >= 1:
                        dve.wait_ge(within, j)
                    dve.tensor_tensor(weight[:, h, :].rearrange("p (c t) -> p c t", c=CHUNKS),
                                      flat(pair_b[:, :, :]).rearrange("p (c t) -> p c t", c=CHUNKS),
                                      a[:, :, 2 * j + h].unsqueeze(2).to_broadcast([P, CHUNKS, P]),
                                      ALU.subtract).then_inc(b_free, 1)
                dve.wait_ge(states_made, j + 1)
                if j >= 1:
                    dve.wait_ge(from_state, j)
                for c in range(CHUNKS - 1):
                    made = pair_a[:, c // 4, c % 4 * P:(c % 4 + 1) * P].rearrange("p (h d) -> p h d", h=2)
                    if c == 0:
                        link(dve.tensor_copy(state[:, 1, :, :], made))
                        continue
                    for h in range(2):
                        ins = dve.scalar_tensor_tensor(out=state[:, c + 1, h, :], in0=state[:, c, h, :],
                                                       scalar=decay[:, c, 2 * j + h:2 * j + h + 1], in1=made[:, h, :],
                                                       op0=ALU.mult, op1=ALU.add)
                        if h == 1 and c < CHUNKS - 2:
                            link(ins)
                ins.then_inc(state_ready, 1)
                for h in range(2):
                    dve.wait_ge(decayed, 2 * j + h + 1)
                    dve.tensor_tensor(weight[:, h, :], weight[:, h, :], cb[:, g, :], ALU.mult).then_inc(weighted, 1)
                dve.wait_ge(from_state, j + 1)
                dve.wait_ge(b_free, 3 * j + 3)
                out = y[:, j % 4, :]
                if j >= 4:
                    dve.wait_ge(stored, 64 * g)
                link(dve.tensor_tensor(out[:, P:], flat(pair_c[:, :, :])[:, P:], grown[:, P:], ALU.mult))
                dve.wait_ge(within, j + 1)
                dve.tensor_copy(out[:, :P], pair_d[:, 0, :P])
                ins = dve.tensor_tensor(out[:, P:], out[:, P:], flat(pair_d[:, :, :])[:, P:], ALU.add)
                ins.then_inc(y_read, 1)
                dve.wait_ge(y_read, j + 1)
                link(dve.scalar_tensor_tensor(out=out, in0=conv[:, j, :], scalar=tile_par[:, j, 0:1], in1=out,
                                              op0=ALU.mult, op1=ALU.add))
                dve.wait_ge(z_ready, 4 * g + j % 4 + 1)
                dve.tensor_tensor(out, out, z[:, j % 4, :], ALU.mult).then_inc(y_done, 1)
                if j % 4 == 3:
                    dve.wait_ge(summed, g + 1)
                    base = 7 * g
                    dve.tensor_scalar(square, flat(pair_c[:, :, :]), 1.0 / 512, EPS, ALU.mult, ALU.add).then_inc(rooting, 1)
                    dve.wait_ge(rooting, base + 1)
                    dve.reciprocal(aux, square).then_inc(rooting, 1)
                    dve.wait_ge(rooted, g + 1)
                    dve.tensor_tensor(aux, rstd, rstd, ALU.mult).then_inc(rooting, 1)
                    dve.wait_ge(rooting, base + 3)
                    dve.tensor_tensor(aux, aux, square, ALU.mult).then_inc(rooting, 1)
                    dve.wait_ge(rooting, base + 4)
                    dve.tensor_scalar(aux, aux, -0.5, 1.5, ALU.mult, ALU.add).then_inc(rooting, 1)
                    dve.wait_ge(rooting, base + 5)
                    dve.tensor_tensor(rstd, rstd, aux, ALU.mult).then_inc(rooting, 2)
                    dve.wait_ge(rooting, base + 7)
                    dve.wait_ge(squared, 4 * g + 4)
                    for k in range(4):
                        dve.scalar_tensor_tensor(out=y[:, k, :], in0=y[:, k, :], scalar=tile_par[:, 4 * g + k, 1:2],
                                                 in1=rstd, op0=ALU.mult, op1=ALU.mult).then_inc(normed, 1)


PEER_HEADS = 8
TOP = 16
KEYS = 128
SCORE_SETS = 2 * PEER_HEADS
LOWEST = -3e38


def routing_phase(nc, name, q_dram, keys_dram, count_dram, i1_t, i2_t, gate_t, const):
    ctx = Phase(nc)
    with ctx:
        def sb(what, shape, dt=F32):
            return ctx.enter_context(nc.sbuf_tensor(f"{name}_{what}", shape, dt))

        def sem(what):
            return ctx.semaphore(f"{name}_{what}")

        q = sb("q", [P, SCORE_SETS, P])
        keys = sb("keys", [P, SCORE_SETS, KEYS])
        count = sb("count", [P, KEYS])
        score = sb("score", [P, SCORE_SETS, KEYS])
        best = sb("best", [P, SCORE_SETS, TOP])
        index = sb("index", [P, SCORE_SETS, TOP], U32)
        index_f = sb("index_f", [P, SCORE_SETS, TOP])
        pair = sb("pair", [P, PEER_HEADS, TOP, TOP])
        total = sb("total", [P, PEER_HEADS, TOP])
        place = sb("place", [P, PEER_HEADS, TOP], U32)
        part = sb("part", [P, 2, PEER_HEADS * TOP], U32)
        part_f = sb("part_f", [P, 2, PEER_HEADS * TOP])
        hit = sb("hit", [P, PEER_HEADS, TOP, TOP])
        found = sb("found", [P, 3, PEER_HEADS * TOP])
        denom = sb("denom", [P, 2, PEER_HEADS])
        acc = ctx.enter_context(nc.psum_tensor(name + "_acc", [P, SCORE_SETS, KEYS], F32))
        turn = ctx.enter_context(nc.psum_tensor(name + "_turn", [P, 3, P], F32))
        (small_in, q_in, scored, copied, chain, begun, shifted, exped, ready, turned, kept) = (
            sem(s) for s in ("small_in", "q_in", "scored", "copied", "chain", "begun", "shifted", "exped", "ready",
                             "turned", "kept"))
        block = ctx.enter_context(nc.Block())
        TILES = T // P

        @block.sync
        def _(sp):
            sp.dma_start(keys[:], keys_dram).then_inc(small_in, 16)
            sp.dma_start(count[:], count_dram).then_inc(small_in, 16)
            sp.sem_inc(scored, 1)
            q_view = q_dram.rearrange("(s p) t -> p s t", p=P)
            with sp.Fori(0, TILES) as m:
                sp.wait_ge(scored, m + 1)
                sp.dma_start(q[:], q_view[:, :, bass.ds(m * P, P)]).then_inc(q_in, 16)

        @block.tensor
        def _(pe):
            pe.wait_ge(small_in, 32)
            with pe.Fori(0, TILES) as m:
                pe.wait_ge(q_in, m * 16 + 16)
                pe.wait_ge(copied, m + 1)
                for s in range(SCORE_SETS):
                    mm = pe.matmul(acc[:, s, :], q[:, s, :], keys[:, s, :], start=True, stop=True)
                mm.then_inc(scored, 1)
                pe.wait_ge(ready, m + 1)
                pe.wait_ge(kept, m + 1)
                for j in range(3):
                    mm = pe.transpose(turn[:, j, :], found[:, j, :], const.identity)
                mm.then_inc(turned, 1)

        @block.scalar
        def _(act):
            act.sem_inc(copied, 1)
            act.sem_inc(kept, 1)
            act.sem_inc(turned, 1)
            with act.Fori(0, TILES) as m:
                act.wait_ge(scored, m + 2)
                act.wait_ge(shifted, m + 1)
                act.activation(score[:], acc[:], ACT.Copy).then_inc(copied, 1)
                act.wait_ge(shifted, m + 2)
                act.activation(found[:, 2, :], found[:, 2, :], ACT.Exp).then_inc(exped, 1)
                act.wait_ge(turned, m + 2)
                for j, dst in enumerate((i1_t, i2_t, gate_t)):
                    ins = act.activation(dst[:, bass.ds(m * P, P)], turn[:, j, :], ACT.Copy)
                ins.then_inc(kept, 1)

        @block.vector
        def _(dve):
            def search(values, best8x2, index8x2, link):
                link(dve.max(best8x2[:, 0:8], values))
                link(dve.max_index(index8x2[:, 0:8], best8x2[:, 0:8], values))
                link(dve.match_replace(values, best8x2[:, 0:8], values, LOWEST))
                link(dve.max(best8x2[:, 8:16], values))
                link(dve.max_index(index8x2[:, 8:16], best8x2[:, 8:16], values))

            dve.sem_inc(shifted, 1)
            dve.wait_ge(small_in, 32)
            with dve.Fori(0, TILES) as m:
                links = [0]
                dve.sem_clear(chain)

                def link(instruction):
                    links[0] += 1
                    instruction.then_inc(chain, 1)
                    dve.wait_ge(chain, links[0])

                dve.wait_ge(copied, m + 2)
                dve.sem_inc(begun, 1)
                for s in range(SCORE_SETS):
                    search(score[:, s, :], best[:, s, :], index[:, s, :], link)
                link(dve.tensor_copy(index_f[:], index[:]))
                halves = best[:, :, :].rearrange("p (h two) k -> p h two k", two=2)
                shape = [P, PEER_HEADS, TOP, TOP]
                link(dve.tensor_tensor(pair[:], halves[:, :, 0, :].unsqueeze(3).to_broadcast(shape),
                                       halves[:, :, 1, :].unsqueeze(2).to_broadcast(shape), ALU.add))
                for h in range(PEER_HEADS):
                    search(pair[:, h, :, :].rearrange("p a b -> p (a b)"), total[:, h, :], place[:, h, :], link)
                dve.wait_ge(turned, m + 1)
                link(dve.tensor_tensor(found[:, 2, :].rearrange("p (h k) -> p h k", k=TOP), total[:],
                                       total[:, :, 0:1].to_broadcast([P, PEER_HEADS, TOP]), ALU.subtract))
                link(dve.tensor_scalar(part[:, 0, :], place[:].rearrange("p h k -> p (h k)"), 4, None,
                                       ALU.logical_shift_right))
                link(dve.tensor_scalar(part[:, 1, :], place[:].rearrange("p h k -> p (h k)"), 15, None,
                                       ALU.bitwise_and))
                link(dve.tensor_copy(part_f[:], part[:]))
                dve.sem_inc(shifted, 1)
                rank = count[:, 0:TOP].unsqueeze(1).to_broadcast([P, PEER_HEADS * TOP, TOP])
                ids = index_f[:, :, :].rearrange("p (h two) k -> p h two k", two=2)
                hit_rows = hit[:].rearrange("p h k j -> p (h k) j")
                for j in range(2):
                    link(dve.tensor_tensor(hit_rows, rank,
                                           part_f[:, j, :].unsqueeze(2).to_broadcast([P, PEER_HEADS * TOP, TOP]),
                                           ALU.is_equal))
                    link(dve.tensor_tensor(hit[:], hit[:], ids[:, :, j, :].unsqueeze(2).to_broadcast(shape), ALU.mult))
                    link(dve.tensor_reduce(found[:, j, :], hit_rows, AX.X, ALU.add))
                dve.wait_ge(exped, m + 1)
                weights = found[:, 2, :].rearrange("p (h k) -> p h k", k=TOP)
                link(dve.tensor_reduce(denom[:, 0, :], weights, AX.X, ALU.add))
                link(dve.reciprocal(denom[:, 1, :], denom[:, 0, :]))
                link(dve.tensor_tensor(weights, weights,
                                       denom[:, 1, :].unsqueeze(2).to_broadcast([P, PEER_HEADS, TOP]), ALU.mult))
                dve.sem_inc(ready, 1)


def spread_gates_phase(nc, name, i1_t, i2_t, gate_t, count_dram, g_dram):
    GROUP = 8
    GROUPS_PER_BLOCK = P // GROUP
    BLOCKS = T // P
    ctx = Phase(nc)
    with ctx:
        def sb(what, shape, dt=F32):
            return ctx.enter_context(nc.sbuf_tensor(f"{name}_{what}", shape, dt))

        def sem(what):
            return ctx.semaphore(f"{name}_{what}")

        count = sb("count", [P, KEYS])
        first = sb("first", [P, 2, GROUP, KEYS])
        second = sb("second", [P, 2, GROUP, KEYS])
        gates = [sb(f"gates{b}", [P, KEYS, P]) for b in range(2)]
        acc = ctx.enter_context(nc.psum_tensor(name + "_acc", [P, 2, GROUP, KEYS], F32))
        count_in, made, spread, drained = (sem(s) for s in ("count_in", "made", "spread", "drained"))
        stored = [sem(f"stored{b}") for b in range(2)]
        block = ctx.enter_context(nc.Block())
        two = range(2)

        @block.sync
        def _(sp):
            sp.dma_start(count[:], count_dram).then_inc(count_in, 16)
            for b in two:
                sp.sem_inc(stored[b], 16)
            with sp.Fori(0, BLOCKS // 2) as i:
                for b in two:
                    sp.wait_ge(drained, i * (2 * GROUPS_PER_BLOCK) + ((b + 1) * GROUPS_PER_BLOCK + 2))
                    sp.dma_start(g_dram[:, :, bass.ds(i * (2 * P) + b * P, P)], gates[b][:]).then_inc(stored[b], 16)
            for b in two:
                sp.wait_ge(stored[b], 16 * (BLOCKS // 2 + 1))

        @block.vector
        def _(dve):
            dve.wait_ge(count_in, 16)
            with dve.Fori(0, T // (2 * GROUP)) as i:
                for b in two:
                    dve.wait_ge(spread, i * 2 + (b + 1))
                    for n in range(GROUP):
                        token = i * (2 * GROUP) + (b * GROUP + n)
                        dve.tensor_scalar(second[:, b, n, :], count[:], i2_t[:, bass.ds(token, 1)], None, ALU.is_equal)
                        ins = dve.tensor_scalar(first[:, b, n, :], count[:], i1_t[:, bass.ds(token, 1)],
                                                gate_t[:, bass.ds(token, 1)], ALU.is_equal, ALU.mult)
                    ins.then_inc(made, 1)

        @block.tensor
        def _(pe):
            pe.sem_inc(spread, 2)
            with pe.Fori(0, T // (2 * GROUP)) as i:
                for b in two:
                    pe.wait_ge(made, i * 2 + (b + 1))
                    pe.wait_ge(drained, i * 2 + (b + 1))
                    for n in range(GROUP):
                        mm = pe.matmul(acc[:, b, n, :], second[:, b, n, :], first[:, b, n, :], start=True, stop=True)
                    mm.then_inc(spread, 1)

        @block.scalar
        def _(act):
            act.sem_inc(drained, 2)
            with act.Fori(0, BLOCKS // 2) as i:
                for blk in two:
                    act.wait_ge(stored[blk], i * 16 + 16)
                    for r in range(GROUPS_PER_BLOCK):
                        act.wait_ge(spread, i * (2 * GROUPS_PER_BLOCK) + (blk * GROUPS_PER_BLOCK + r + 3))
                        act.activation(gates[blk][:, :, r * GROUP:(r + 1) * GROUP],
                                       acc[:, r % 2, :, :].rearrange("p n k -> p k n"), ACT.Copy).then_inc(drained, 1)


def experts_phase(nc, name, h_hi, h_lo, u_dram, v_dram, g_dram, x_dram, out_dram):
    PAIRS = KEYS // 2
    ctx = Phase(nc)
    with ctx:
        def sb(what, shape, dt=F32):
            return ctx.enter_context(nc.sbuf_tensor(f"{name}_{what}", shape, dt))

        def sem(what):
            return ctx.semaphore(f"{name}_{what}")

        u_raw, u_hi, u_lo = sb("u_raw", [P, KD, 2, P]), sb("u_hi", [P, KD, 2, P], F32R), sb("u_lo", [P, KD, 2, P], F32R)
        v_raw, v_hi, v_lo = sb("v_raw", [P, 2, D]), sb("v_hi", [P, 2, D], F32R), sb("v_lo", [P, 2, D], F32R)
        gate = sb("gate", [P, 2, T])
        hidden = sb("hidden", [P, 2, T])
        a_hi, a_lo = sb("a_hi", [P, 2, 2, T], F32R), sb("a_lo", [P, 2, 2, T], F32R)
        total = sb("total", [P, KD, T])
        u_acc = ctx.enter_context(nc.psum_tensor(name + "_u_acc", [P, 2, 2, HALF], F32))
        v_acc = ctx.enter_context(nc.psum_tensor(name + "_v_acc", [P, 4, HALF], F32))
        two = range(2)
        u_in, v_in, x_in, stored = (sem(s) for s in ("u_in", "v_in", "x_in", "stored"))
        gate_in = [sem(f"gate_in{e}") for e in two]
        u_high, u_split, v_high, v_split = (sem(s) for s in ("u_high", "u_split", "v_high", "v_split"))
        u_done = [sem(f"u_done{e}") for e in two]
        gelued = [sem(f"gelued{e}") for e in two]
        gated = [sem(f"gated{e}") for e in two]
        a_high = [sem(f"a_high{e}") for e in two]
        a_split = [sem(f"a_split{e}") for e in two]
        v_done, added, v_pair = sem("v_done"), sem("added"), sem("v_pair")
        block = ctx.enter_context(nc.Block())
        BANKS = 4
        OUTS = 2 * KD
        LOOPS = PAIRS // 2 - 2

        def steps(engine, step):
            step(0, 0)
            with engine.Fori(0, LOOPS) as i:
                step(i * 2 + 1, 1)
                step(i * 2 + 2, 0)
            for g in range(2 * LOOPS + 1, PAIRS + 1):
                step(g, g % 2)

        def is_static(g):
            return isinstance(g, int)

        @block.sync
        def _(sp):
            def load_u(g):
                sp.dma_start(u_raw[:].rearrange("p a b c -> p (a b c)"), u_dram[bass.ds(g * P, P), :]).then_inc(u_in, 16)

            def load_v(g):
                sp.dma_start(v_raw[:].rearrange("p a b -> p (a b)"), v_dram[bass.ds(g * P, P), :]).then_inc(v_in, 16)

            def load_gate(g, e):
                sp.dma_start(gate[:, e, :], g_dram[:, bass.ds(g * 2 + e, 1), :].rearrange("p a t -> p (a t)")
                             ).then_inc(gate_in[e], 16)

            load_u(0)
            for e in two:
                load_gate(0, e)
            for k in range(KD):
                sp.dma_start(total[:, k, :], x_dram[k * P:(k + 1) * P, :]).then_inc(x_in, 16)
            load_v(0)
            sp.wait_ge(u_split, 1)
            load_u(1)

            def step(g, slot):
                first, last = is_static(g) and g == 0, is_static(g) and g >= PAIRS
                if last:
                    return
                if not first:
                    sp.wait_ge(v_split, g)
                    load_v(g)
                more = not (is_static(g) and g + 1 >= PAIRS)
                if more:
                    sp.wait_ge(gated[0], g + 1)
                    load_gate(g + 1, 0)
                if not (is_static(g) and g + 2 >= PAIRS):
                    sp.wait_ge(u_split, g + 2)
                    load_u(g + 2)
                if more:
                    sp.wait_ge(gated[1], g + 1)
                    load_gate(g + 1, 1)

            steps(sp, step)
            sp.wait_ge(added, PAIRS * OUTS + BANKS)
            for k in range(KD):
                sp.dma_start(out_dram[k * P:(k + 1) * P, :], total[:, k, :]).then_inc(stored, 16)
            sp.wait_ge(stored, 16 * KD)

        @block.tensor
        def _(pe):
            def step(g, slot):
                first, last = is_static(g) and g == 0, is_static(g) and g >= PAIRS
                if not last:
                    pe.wait_ge(u_split, g + 1)
                    for e in two:
                        if not first:
                            pe.wait_ge(gelued[e], g)
                        for k in range(KD):
                            for n_pass, (w, h) in enumerate(((u_hi, h_hi), (u_hi, h_lo), (u_lo, h_hi))):
                                for half in two:
                                    mm = pe.matmul(u_acc[:, e, half, :], w[:, k, e, :],
                                                   h[:, k, half * HALF:(half + 1) * HALF],
                                                   start=(k == 0 and n_pass == 0), stop=(k == KD - 1 and n_pass == 2))
                        mm.then_inc(u_done[e], 1)
                if not first:
                    old = 1 - slot
                    pe.wait_ge(v_split, g)
                    for e in two:
                        pe.wait_ge(a_split[e], g)
                    for n in range(OUTS):
                        d, half = divmod(n, 2)
                        pe.wait_ge(added, (g - 1) * OUTS + (n + 1))
                        for e in two:
                            for n_pass, (w, a) in enumerate(((v_hi, a_hi), (v_hi, a_lo), (v_lo, a_hi))):
                                mm = pe.matmul(v_acc[:, n % BANKS, :], w[:, e, d * P:(d + 1) * P],
                                               a[:, old, e, half * HALF:(half + 1) * HALF],
                                               start=(e == 0 and n_pass == 0), stop=(e == 1 and n_pass == 2))
                        mm.then_inc(v_done, 1)
            pe.sem_inc(added, BANKS)
            steps(pe, step)

        @block.scalar
        def _(act):
            def split_u(g):
                act.wait_ge(u_in, g * 16 + 16)
                if not (is_static(g) and g == 0):
                    act.wait_ge(u_done[1], g)
                act.activation(u_hi[:], u_raw[:], ACT.Copy).then_inc(u_high, 1)

            def step(g, slot):
                first, last = is_static(g) and g == 0, is_static(g) and g >= PAIRS
                if not first:
                    act.wait_ge(v_in, g * 16)
                    if not (is_static(g) and g == 1):
                        act.wait_ge(v_done, (g - 1) * OUTS)
                    act.activation(v_hi[:], v_raw[:], ACT.Copy).then_inc(v_high, 1)
                if last:
                    return
                for e in two:
                    if e == 1 and not (is_static(g) and g + 1 >= PAIRS):
                        split_u(g + 1)
                    act.wait_ge(u_done[e], g + 1)
                    if not first:
                        act.wait_ge(a_split[e], g)
                    act.activation(hidden[:, e, :], u_acc[:, e, :, :].rearrange("p a b -> p (a b)"),
                                   ACT.Gelu_apprx_tanh).then_inc(gelued[e], 1)
                    act.wait_ge(gated[e], g + 1)
                    act.activation(a_hi[:, slot, e, :], hidden[:, e, :], ACT.Copy).then_inc(a_high[e], 1)

            split_u(0)
            steps(act, step)

        @block.vector
        def _(dve):
            def split_u(g):
                dve.wait_ge(u_high, g + 1)
                dve.tensor_tensor(u_lo[:].rearrange("p a b c -> p (a b c)"), u_raw[:].rearrange("p a b c -> p (a b c)"),
                                  u_hi[:].rearrange("p a b c -> p (a b c)").bitcast(F32), ALU.subtract).then_inc(u_split, 1)

            def step(g, slot):
                first, last = is_static(g) and g == 0, is_static(g) and g >= PAIRS

                def add(n):
                    d, half = divmod(n, 2)
                    at = slice(half * HALF, (half + 1) * HALF)
                    dve.wait_ge(v_done, (g - 1) * OUTS + (n + 1))
                    dve.tensor_tensor(total[:, d, at], total[:, d, at], v_acc[:, n % BANKS, :], ALU.add).then_inc(added, 1)

                def take_gate(e):
                    dve.wait_ge(gelued[e], g + 1)
                    dve.wait_ge(gate_in[e], g * 16 + 16)
                    dve.tensor_tensor(hidden[:, e, :], hidden[:, e, :], gate[:, e, :], ALU.mult).then_inc(gated[e], 1)

                def split_a(e):
                    dve.wait_ge(a_high[e], g + 1)
                    dve.tensor_tensor(a_lo[:, slot, e, :], hidden[:, e, :], a_hi[:, slot, e, :].bitcast(F32),
                                      ALU.subtract).then_inc(a_split[e], 1)

                if not first:
                    dve.wait_ge(v_high, g)
                    dve.tensor_tensor(v_lo[:].rearrange("p a b -> p (a b)"), v_raw[:].rearrange("p a b -> p (a b)"),
                                      v_hi[:].rearrange("p a b -> p (a b)").bitcast(F32), ALU.subtract).then_inc(v_split, 1)
                if not last:
                    take_gate(0)
                    split_a(0)
                    if not (is_static(g) and g + 1 >= PAIRS):
                        split_u(g + 1)
                if not first:
                    add(0)
                    add(1)
                if not last:
                    take_gate(1)
                if not first:
                    for n in range(2, 6):
                        add(n)
                if not last:
                    split_a(1)
                if not first:
                    for n in range(6, OUTS):
                        add(n)

            dve.wait_ge(x_in, 16 * KD)
            split_u(0)
            steps(dve, step)


def shape_constants():
    c = {}
    c["identity"] = np.eye(P, dtype=np.float32)
    c["flip"] = np.ascontiguousarray(c["identity"][::-1])
    p = np.arange(P)
    pick = (np.arange(32)[None, None, :] == 2 * np.arange(16)[None, :, None] + (p // 64)[:, None, None])
    c["head_pick"] = pick.astype(np.float32).reshape(P, 16 * 32)
    c["head_spread"] = np.ascontiguousarray(pick.transpose(2, 1, 0)).astype(np.float32).reshape(32, 16 * P)
    rel = np.arange(REL_COUNT) - (REL_COUNT - P)
    near = np.abs(rel)
    far = 8 + sum((rel * rel >= 64 * 2 ** q).astype(np.int64) for q in range(1, 8))
    bucket = np.where(rel > 0, 16, 0) + np.where(near < 8, near, far)
    c["bucket_onehot"] = (np.arange(32)[:, None] == bucket[None, :]).astype(np.float32)
    age = np.arange(BLOCK_KEYS)[None, :] // 64 - (p // 64)[:, None]
    c["band_mask"] = np.where((age == 0) | (age == 1), 0.0, NEGATIVE).astype(np.float32)
    c["causal_mask"] = np.where(p[:, None] <= p[None, :], 0.0, NEGATIVE).astype(np.float32)
    c["count"] = np.broadcast_to(np.arange(P, dtype=np.float32), (P, P)).copy()
    return c


NEGATIVE = -1e30


class Constants:

    def __init__(self, nc, ctx, arrays):
        def sb(what, shape, dt=F32):
            return ctx.enter_context(nc.sbuf_tensor("const_" + what, shape, dt))

        identity, ones = sb("identity", [P, P]), sb("ones", [P, P])
        pick, spread = sb("head_pick", [P, 16, 32]), sb("head_spread", [32, 16, P])
        loaded = ctx.enter_context(nc.semaphore("const_loaded"))
        with nc.Block() as block:
            @block.sync
            def _(sp):
                sp.dma_start(identity[:], arrays["identity"]).then_inc(loaded, 16)
                sp.dma_start(pick[:], arrays["head_pick"]).then_inc(loaded, 16)
                sp.dma_start(spread[:], arrays["head_spread"]).then_inc(loaded, 16)
                sp.wait_ge(loaded, 48)

            @block.vector
            def _(dve):
                dve.memset(ones[:], 1.0)
        self.identity, self.ones, self.head_pick, self.head_spread = identity[:], ones[:], pick[:], spread[:]


IN_TILES = 68
GATE_ATT_ROWS, GATE_SSM_ROWS = 6656, 7680


def build_layer(nc, a, out):
    def scratch(what, rows, cols=T):
        return nc.dram_tensor("scratch_" + what, (rows, cols), F32, kind="Internal").ap()

    proj, dt_raw = scratch("proj", IN_TILES * P), scratch("dt", P)
    rel_row = scratch("rel_row", Q_HEADS, REL_COUNT)
    att, ssm = scratch("att", 1024), scratch("ssm", 2048)
    mixed_ssm, mixed = scratch("mixed_ssm", D), scratch("mixed", D)
    x1, x2, query, ple = scratch("x1", D), scratch("x2", D), scratch("query", 2048), scratch("ple", D)
    gates = nc.dram_tensor("scratch_gates", (KEYS, KEYS, T), F32, kind="Internal").ap()
    ctx = ExitStack()
    with ctx:
        const = Constants(nc, ctx, a)

        def parts(scope, tiles, what):
            return [scope.enter_context(nc.sbuf_tensor(f"{what}_{part}", [P, tiles, T], F32R)) for part in ("hi", "lo")]

        with ExitStack() as scope:
            h = parts(scope, KD, "h_mix")
            rms_phase(nc, "norm_mix", a["x"], a["norm_mix_g"], *h, const.ones)
            linear_phase(nc, "in_proj", *h, KD, a["w_in"], IN_TILES, proj)
            linear_phase(nc, "dt_proj", *h, KD, a["w_dt"], 1, dt_raw)
        attention_phase(nc, "attention", proj, a["qk_norm_g"], a["attn_sinks"], a["rel_bias"], a["bucket_onehot"],
                        a["band_mask"], a["flip"], rel_row, att, const)
        ssm_phase(nc, "ssm", proj, dt_raw, a["conv"], a["head_par"], a["tile_par"], a["causal_mask"], ssm, const)
        with ExitStack() as scope:
            y = parts(scope, SSM_TILES, "y_ssm")
            split_phase(nc, "ssm_split", ssm, SSM_TILES, *y)
            linear_phase(nc, "o_ssm", *y, SSM_TILES, a["w_o_ssm"], KD, mixed_ssm, "gate",
                         proj[GATE_SSM_ROWS:GATE_SSM_ROWS + D, :])
        with ExitStack() as scope:
            o = parts(scope, KD, "o_att")
            split_phase(nc, "att_split", att, KD, *o)
            linear_phase(nc, "o_att", *o, KD, a["w_o_attn"], KD, mixed, "gate_add",
                         proj[GATE_ATT_ROWS:GATE_ATT_ROWS + D, :], mixed_ssm)
        with ExitStack() as scope:
            m = parts(scope, KD, "mixed")
            split_phase(nc, "mixed_split", mixed, KD, *m)
            linear_phase(nc, "out_proj", *m, KD, a["w_out"], KD, x1, "add", a["x"])
        with ExitStack() as scope:
            h = parts(scope, KD, "h_query")
            rms_phase(nc, "norm_query", x1, a["norm_ffn_g"], *h, const.ones)
            linear_phase(nc, "query", *h, KD, a["w_peer_q"], SCORE_SETS, query)
        with ExitStack() as scope:
            i1_t, i2_t, gate_t = (scope.enter_context(nc.sbuf_tensor(n, [P, T], F32)) for n in ("i1_t", "i2_t", "gate_t"))
            routing_phase(nc, "routing", query, a["peer_keys"], a["count"], i1_t, i2_t, gate_t, const)
            spread_gates_phase(nc, "spread_gates", i1_t, i2_t, gate_t, a["count"], gates)
        with ExitStack() as scope:
            h = parts(scope, KD, "h_ffn")
            rms_phase(nc, "norm_ffn", x1, a["norm_ffn_g"], *h, const.ones)
            experts_phase(nc, "experts", *h, a["peer_u"], a["peer_v"], gates, x1, x2)
        with ExitStack() as scope:
            e = parts(scope, 2, "embedding")
            split_phase(nc, "ple_split", a["p"], 2, *e)
            linear_phase(nc, "ple", *e, 2, a["w_ple"], KD, ple)
        with ExitStack() as scope:
            h = parts(scope, KD, "h_ple")
            rms_phase(nc, "norm_ple", x2, a["norm_ple_g"], *h, const.ones)
            linear_phase(nc, "ple_gate", *h, KD, a["w_ple_gate"], KD, out, "final", ple, x2)


def weight_tiles(w):
    k, n = w.shape[0] // P, w.shape[1] // P
    return w.reshape(k, P, n, P).transpose(2, 1, 0, 3).reshape(n * P, k * P)


def per_partition(*rows):
    stacked = np.stack([r.reshape(-1, P).T for r in rows], axis=-1)
    return stacked[:, :, 0] if len(rows) == 1 else stacked


def kernel(**inputs):
    import concourse.bacc as bacc
    from concourse.bass_utils import run_bass_kernel_spmd

    i = {k: np.asarray(v) for k, v in inputs.items()}
    one = {k: v[0] for k, v in i.items()}
    w_in = one["w_in"]
    dt_at = 1024 + 256 + 256 + 2048 + 3072
    order = np.arange(Q_HEADS).reshape(KV_HEADS, 4)[:, list(HEAD_ORDER)].reshape(-1)
    w_dt = np.zeros((D, P), w_in.dtype)
    w_dt[:, :SSM_HEADS] = w_in[:, dt_at:dt_at + SSM_HEADS]
    arrays = {
        "x": one["x"].T,
        "p": one["p"][0].T,
        "norm_mix_g": per_partition(one["norm_mix_g"]),
        "norm_ffn_g": per_partition(one["norm_ffn_g"]),
        "norm_ple_g": per_partition(one["norm_ple_g"]),
        "w_in": weight_tiles(np.concatenate([w_in[:, :dt_at], w_in[:, dt_at + SSM_HEADS:]], axis=1)),
        "w_dt": weight_tiles(w_dt),
        "qk_norm_g": np.stack([np.tile(one["q_norm_g"], 2), np.tile(one["k_norm_g"], 2)], axis=1),
        "attn_sinks": one["attn_sinks"][order],
        "rel_bias": i["rel_bias"][:, order],
        "conv": per_partition(*one["conv_w"], one["conv_b"]),
        "head_par": np.stack([one["dt_bias"], one["a_log"]], axis=1),
        "tile_par": per_partition(np.repeat(one["d_skip"], 64), one["ssm_norm_g"]),
        "w_o_attn": weight_tiles(one["w_o_attn"]),
        "w_o_ssm": weight_tiles(one["w_o_ssm"]),
        "w_out": weight_tiles(one["w_out"]),
        "w_peer_q": weight_tiles(one["w_peer_q"]),
        "peer_keys": one["peer_sub_keys"].reshape(SCORE_SETS, KEYS, P).transpose(2, 0, 1),
        "peer_u": one["peer_u"].reshape(KEYS // 2, 2, KEYS, KD, P).transpose(0, 4, 3, 1, 2).reshape(-1, 2 * D),
        "peer_v": one["peer_v"].reshape(KEYS // 2, 2, KEYS, D).transpose(0, 2, 1, 3).reshape(-1, 2 * D),
        "w_ple_gate": weight_tiles(one["w_ple_gate"]),
        "w_ple": weight_tiles(one["w_ple"]),
        **shape_constants(),
    }
    arrays = {k: np.ascontiguousarray(v) for k, v in arrays.items()}
    nc = bacc.Bacc("TRN2", target_bir_lowering=False, num_devices=1)
    aps = {k: nc.dram_tensor("in_" + k, v.shape, mybir.dt.from_np(v.dtype), kind="ExternalInput").ap()
           for k, v in arrays.items()}
    out = nc.dram_tensor("out", (D, T), F32, kind="ExternalOutput").ap()
    build_layer(nc, aps, out)
    r = run_bass_kernel_spmd(nc, [{"in_" + k: v for k, v in arrays.items()}], core_ids=[0])
    return np.ascontiguousarray(r.results[0]["out"].T)[None]
```

```python
import concourse.bass as bass
from concourse import mybir
from contextlib import ExitStack
import numpy as np

F32 = mybir.dt.float32
F32R = mybir.dt.float32r
BF16 = mybir.dt.bfloat16
U32 = mybir.dt.uint32
ACT = mybir.ActivationFunctionType
ALU = mybir.AluOpType
AX = mybir.AxisListType

P = 128
T = 1024
HALF = 512
D = 1024
KD = D // P
EPS = 1e-6


class Phase(ExitStack):

    def __init__(self, nc):
        super().__init__()
        self.nc, self.semaphores = nc, []

    def semaphore(self, name):
        self.semaphores.append(self.nc.alloc_semaphore(name))
        return self.semaphores[-1]

    def __exit__(self, *failure):
        super().__exit__(*failure)
        if failure[0] is None:
            self.nc.clear_and_free_semaphores(self.semaphores)
            self.nc.all_engine_barrier()




Q_HEADS, KV_HEADS, HEAD_DIM = 16, 4, 64
Q_ROWS, V_ROWS = 3072, 4352
HEAD_ORDER = (0, 2, 1, 3)
BLOCK_KEYS = 192
BAND = 256
REL_COUNT = BLOCK_KEYS + P - 1
NORMED = (Q_HEADS + KV_HEADS) // 2


def attention_phase(nc, name, proj, qk_gain_dram, sink_dram, rel_bias_dram, onehot_dram, band_mask_dram,
                    flip_dram, rel_row_dram, out_dram, const):
    ctx = Phase(nc)
    with ctx:
        def sb(what, shape, dt=F32):
            return ctx.enter_context(nc.sbuf_tensor(f"{name}_{what}", shape, dt))

        def sem(what):
            return ctx.semaphore(f"{name}_{what}")

        qk = sb("qk", [P, NORMED, T])
        k_swap = sb("k_swap", [P, 2, T])
        v_t = sb("v_t", [P, 2, T])
        v = sb("v", [P, KD, KV_HEADS * HEAD_DIM])
        gain = sb("gain", [P, 2])
        square = sb("square", [P, 2, T])
        rstd = sb("rstd", [32, 3, T])
        bias = sb("bias", [P, Q_HEADS, BLOCK_KEYS])
        mask = sb("mask", [P, BLOCK_KEYS])
        onehot = sb("onehot", [32, REL_COUNT])
        rel_bias = sb("rel_bias", [32, Q_HEADS])
        rel_row = sb("rel_row", [Q_HEADS, REL_COUNT])
        sink = sb("sink", [P, Q_HEADS])
        score = sb("score", [P, 2, 4, BLOCK_KEYS])
        prob = sb("prob", [P, 2, 4, BAND])
        prob_t = sb("prob_t", [P, 2, 4, P])
        top = sb("top", [P, 2, 4])
        neg_top = sb("neg_top", [P, 2, 4])
        sink_gap = sb("sink_gap", [P, 2, 4])
        sink_exp = sb("sink_exp", [P, 2, 4])
        denom = sb("denom", [P, 2, 4])
        inverse = sb("inverse", [P, 2, 4])
        out = sb("out", [P, KD, T])

        qk_in = [sem(f"qk_in{k}") for k in range(NORMED)]
        v_in, small_in, swapped, rel_in, stored = (sem(s) for s in ("v_in", "small_in", "swapped", "rel_in", "stored"))
        squared, summed, rooting, rooted, spread, normed = (
            sem(s) for s in ("squared", "summed", "rooting", "rooted", "spread", "normed"))
        v_turned, v_ready, row_made, row_ready, row_stored, flipped, bias_ready, zeroed = (
            sem(s) for s in ("v_turned", "v_ready", "row_made", "row_ready", "row_stored", "flipped", "bias_ready", "zeroed"))

        with ExitStack() as first:
            norm_acc = first.enter_context(nc.psum_tensor(name + "_norm_acc", [P, 2, 2, HALF], F32))
            turn_acc = first.enter_context(nc.psum_tensor(name + "_turn_acc", [P, 2, HALF], F32))
            bias_rev = first.enter_context(nc.sbuf_tensor(name + "_bias_rev", [P, Q_HEADS, BLOCK_KEYS], F32))
            flip = first.enter_context(nc.sbuf_tensor(name + "_flip", [P, P], F32))
            row_acc = first.enter_context(nc.psum_tensor(name + "_row_acc", [P, HALF], F32))
            block = first.enter_context(nc.Block())

            @block.sync
            def _(sp):
                for dst, src in ((gain[:], qk_gain_dram), (rel_bias[:], rel_bias_dram), (onehot[:], onehot_dram),
                                 (mask[:], band_mask_dram), (flip[:], flip_dram)):
                    sp.dma_start(dst, src).then_inc(small_in, 16)
                sp.dma_start(sink[:], sink_dram.partition_broadcast(P)).then_inc(small_in, 16)
                for k in range(2):
                    sp.dma_start(v_t[:, k, :], proj[V_ROWS + k * P:V_ROWS + (k + 1) * P, :]).then_inc(v_in, 16)
                for k in range(NORMED):
                    sp.dma_start(qk[:, k, :], proj[Q_ROWS + k * P:Q_ROWS + (k + 1) * P, :]).then_inc(qk_in[k], 16)
                sp.wait_ge(row_ready, 1)
                sp.dma_start(rel_row_dram, rel_row[:]).then_inc(row_stored, 16)
                sp.wait_ge(row_stored, 16)
                toeplitz = bass.AP(rel_row_dram.tensor, 0, [[1, P], [REL_COUNT, Q_HEADS], [1, BLOCK_KEYS]])
                sp.dma_start(bias_rev[:], toeplitz).then_inc(rel_in, 16)
                sp.wait_ge(normed, NORMED)
                for k in range(2):
                    for s in range(2):
                        sp.dma_start(k_swap[64 * s:64 * s + 64, k, :],
                                     qk[64 - 64 * s:128 - 64 * s, 8 + k, :]).then_inc(swapped, 16)
                sp.wait_ge(swapped, 64)

            @block.scalar
            def _(act):
                for k in range(NORMED):
                    act.wait_ge(qk_in[k], 16)
                    if k >= 2:
                        act.wait_ge(summed, k - 1)
                    act.activation(square[:, k % 2, :], qk[:, k, :], ACT.Square).then_inc(squared, 1)
                act.wait_ge(rooting, 2)
                act.activation(rstd[:, 0, :], rstd[:, 1, :], ACT.Sqrt).then_inc(rooted, 1)

            @block.tensor
            def _(pe):
                pe.wait_ge(small_in, 96)
                pe.matmul(row_acc[:Q_HEADS, :REL_COUNT], rel_bias[:], onehot[:], start=True, stop=True).then_inc(row_made, 1)
                pe.wait_ge(v_in, 32)
                for m in range(KD):
                    if m >= 2:
                        pe.wait_ge(v_ready, m - 1)
                    for k in range(2):
                        mm = pe.transpose(turn_acc[:, m % 2, k * P:(k + 1) * P], v_t[:, k, m * P:(m + 1) * P],
                                          const.identity)
                    mm.then_inc(v_turned, 1)
                for k in range(NORMED):
                    pe.wait_ge(squared, k + 1)
                    for half in range(2):
                        mm = pe.matmul(norm_acc[:32, 0, half, :], const.head_pick[:, k, :],
                                       square[:, k % 2, half * HALF:(half + 1) * HALF],
                                       start=(k == 0), stop=(k == NORMED - 1))
                    mm.then_inc(summed, 1)
                pe.wait_ge(rooting, 6)
                for k in range(NORMED):
                    if k >= 2:
                        pe.wait_ge(normed, k - 1)
                    for half in range(2):
                        mm = pe.matmul(norm_acc[:, k % 2, half, :], const.head_spread[:, k, :],
                                       rstd[:, 0, half * HALF:(half + 1) * HALF], start=True, stop=True)
                    mm.then_inc(spread, 1)
                pe.wait_ge(rel_in, 16)
                for n in range(Q_HEADS // 2):
                    pe.wait_ge(v_ready, KD)
                    if n >= 2:
                        pe.wait_ge(bias_ready, n - 1)
                    pe.matmul(turn_acc[:, n % 2, :2 * BLOCK_KEYS], flip[:],
                              bias_rev[:, 2 * n:2 * n + 2, :].rearrange("p a b -> p (a b)"),
                              start=True, stop=True).then_inc(flipped, 1)

            @block.vector
            def _(dve):
                dve.wait_ge(row_made, 1)
                dve.tensor_copy(rel_row[:], row_acc[:Q_HEADS, :REL_COUNT]).then_inc(row_ready, 1)
                for m in range(KD):
                    dve.wait_ge(v_turned, m + 1)
                    dve.tensor_copy(v[:, m, :], turn_acc[:, m % 2, :2 * P]).then_inc(v_ready, 1)
                dve.memset(prob[:, :, :, 0:64], 0.0).then_inc(zeroed, 1)
                dve.wait_ge(summed, NORMED)
                mean, root, aux = rstd[:, 2, :], rstd[:, 0, :], rstd[:, 1, :]
                dve.tensor_scalar(mean, norm_acc[:32, 0, :, :].rearrange("p a b -> p (a b)"), 1.0 / HEAD_DIM, EPS,
                                  ALU.mult, ALU.add).then_inc(rooting, 1)
                dve.wait_ge(rooting, 1)
                dve.reciprocal(aux, mean).then_inc(rooting, 1)
                dve.wait_ge(rooted, 1)
                dve.tensor_tensor(aux, root, root, ALU.mult).then_inc(rooting, 1)
                dve.wait_ge(rooting, 3)
                dve.tensor_tensor(aux, aux, mean, ALU.mult).then_inc(rooting, 1)
                dve.wait_ge(rooting, 4)
                dve.tensor_scalar(aux, aux, -0.5, 1.5, ALU.mult, ALU.add).then_inc(rooting, 1)
                dve.wait_ge(rooting, 5)
                dve.tensor_tensor(root, root, aux, ALU.mult).then_inc(rooting, 1)
                for k in range(NORMED):
                    dve.wait_ge(spread, k + 1)
                    g = gain[:, 0:1] if k < 8 else gain[:, 1:2]
                    dve.scalar_tensor_tensor(out=qk[:, k, :], in0=qk[:, k, :], scalar=g,
                                             in1=norm_acc[:, k % 2, :, :].rearrange("p a b -> p (a b)"),
                                             op0=ALU.mult, op1=ALU.mult).then_inc(normed, 1)
                dve.wait_ge(small_in, 96)
                for n in range(Q_HEADS // 2):
                    dve.wait_ge(flipped, n + 1)
                    dve.tensor_tensor(bias[:, 2 * n:2 * n + 2, :],
                                      turn_acc[:, n % 2, :2 * BLOCK_KEYS].rearrange("p (a b) -> p a b", a=2),
                                      mask[:].unsqueeze(1).to_broadcast([P, 2, BLOCK_KEYS]), ALU.add).then_inc(bias_ready, 1)

        scores_made, scaled, topped, exped, probs_ready, turned, probs_turned, summed_up, out_ready, chain = (
            sem(s) for s in ("scores_made", "scaled", "topped", "exped", "probs_ready", "turned", "probs_turned",
                             "summed_up", "out_ready", "chain"))
        STEPS = KD * KV_HEADS
        with ExitStack() as second:
            s_acc = second.enter_context(nc.psum_tensor(name + "_s_acc", [P, 2, 4, 256], F32))
            t_acc = second.enter_context(nc.psum_tensor(name + "_t_acc", [P, 2, 4, P], F32))
            o_acc = second.enter_context(nc.psum_tensor(name + "_o_acc", [P, 4, P], F32))
            block = second.enter_context(nc.Block())

            def reach(m):
                return 64 if m == 0 else 0

            @block.tensor
            def _(pe):
                def scores(s):
                    m, kv = divmod(s, KV_HEADS)
                    first_key = m * P - 64 + reach(m)
                    if s >= 2:
                        pe.wait_ge(scaled, s - 1)
                    for h in range(4):
                        head = 4 * kv + HEAD_ORDER[h]
                        at = 64 * (head % 2)
                        keys = qk[:, 8 + kv // 2, :] if kv % 2 == head % 2 else k_swap[:, kv // 2, :]
                        mm = pe.matmul(s_acc[:, s % 2, h, reach(m):BLOCK_KEYS],
                                       qk[at:at + 64, head // 2, m * P:(m + 1) * P],
                                       keys[at:at + 64, first_key:(m + 1) * P], start=True, stop=True)
                    mm.then_inc(scores_made, 1)

                scores(0)
                scores(1)
                for s in range(STEPS):
                    m, kv = divmod(s, KV_HEADS)
                    halves = (1,) if m == 0 else (0, 1)
                    pe.wait_ge(probs_ready, s + 1)
                    if s >= 1:
                        pe.wait_ge(probs_turned, s)
                    for half in halves:
                        for h in range(4):
                            mm = pe.transpose(t_acc[:, half, h, :], prob[:, s % 2, h, half * P:(half + 1) * P],
                                              const.identity)
                    mm.then_inc(turned, 1)
                    if s + 2 < STEPS:
                        scores(s + 2)
                    pe.wait_ge(probs_turned, s + 1)
                    if s >= 1:
                        pe.wait_ge(out_ready, s)
                    for parity in range(2):
                        for n, half in enumerate(halves):
                            mm = pe.matmul(o_acc[64 * parity:64 * parity + 64, 0:2, :],
                                           v[:, m - 1 + half, kv * HEAD_DIM:(kv + 1) * HEAD_DIM],
                                           prob_t[:, half, 2 * parity:2 * parity + 2, :], start=(n == 0), stop=(n == len(halves) - 1))
                    mm.then_inc(summed_up, 1)

            @block.scalar
            def _(act):
                def exps(s):
                    m, kv = divmod(s, KV_HEADS)
                    lo = reach(m)
                    act.wait_ge(topped, s + 1)
                    if s >= 2:
                        act.wait_ge(turned, s - 1)
                        act.wait_ge(probs_ready, s - 1)
                    for h in range(4):
                        act.activation(prob[:, s % 2, h, 64 + lo:BAND], score[:, s % 2, h, lo:], ACT.Exp,
                                       bias=neg_top[:, s % 2, h:h + 1], accum_out=denom[:, s % 2, h:h + 1])
                    act.activation(sink_exp[:, s % 2, :], sink_gap[:, s % 2, :], ACT.Exp).then_inc(exped, 1)

                exps(0)
                for s in range(STEPS):
                    if s + 1 < STEPS:
                        exps(s + 1)
                    half = slice(1, 2) if s < KV_HEADS else slice(0, 2)
                    act.wait_ge(turned, s + 1)
                    if s >= 1:
                        act.wait_ge(summed_up, s)
                    act.activation(prob_t[:, half, :, :], t_acc[:, half, :, :], ACT.Copy).then_inc(probs_turned, 1)

            @block.vector
            def _(dve):
                links = [0]

                def link(instruction):
                    links[0] += 1
                    instruction.then_inc(chain, 1)
                    dve.wait_ge(chain, links[0])

                def tops(s):
                    m, kv = divmod(s, KV_HEADS)
                    b, lo, heads = s % 2, reach(m), slice(4 * kv, 4 * kv + 4)
                    dve.wait_ge(scores_made, s + 1)
                    if s >= 2:
                        dve.wait_ge(exped, s - 1)
                    ins = dve.scalar_tensor_tensor(out=score[:, b, :, lo:], in0=s_acc[:, b, :, lo:BLOCK_KEYS],
                                                   scalar=HEAD_DIM ** -0.5, in1=bias[:, heads, lo:],
                                                   op0=ALU.mult, op1=ALU.add)
                    ins.then_inc(scaled, 1)
                    dve.wait_ge(scaled, s + 1)
                    link(dve.tensor_reduce(top[:, b, :], score[:, b, :, lo:], AX.X, ALU.max))
                    link(dve.tensor_tensor(top[:, b, :], top[:, b, :], sink[:, heads], ALU.max))
                    dve.tensor_scalar(neg_top[:, b, :], top[:, b, :], -1.0, None, ALU.mult)
                    dve.tensor_tensor(sink_gap[:, b, :], sink[:, heads], top[:, b, :], ALU.subtract).then_inc(topped, 1)

                def normalise(s):
                    b = s % 2
                    dve.wait_ge(exped, s + 1)
                    link(dve.tensor_tensor(denom[:, b, :], denom[:, b, :], sink_exp[:, b, :], ALU.add))
                    link(dve.reciprocal(inverse[:, b, :], denom[:, b, :]))
                    lo = 64 + reach(s // KV_HEADS)
                    dve.tensor_tensor(prob[:, b, :, lo:], prob[:, b, :, lo:],
                                      inverse[:, b, :].unsqueeze(2).to_broadcast([P, 4, BAND - lo]),
                                      ALU.mult).then_inc(probs_ready, 1)

                def drain(s):
                    m, kv = divmod(s, KV_HEADS)
                    dve.wait_ge(summed_up, s + 1)
                    dve.tensor_copy(out[:, 2 * kv:2 * kv + 2, m * P:(m + 1) * P], o_acc[:, 0:2, :]).then_inc(out_ready, 1)

                tops(0)
                for s in range(STEPS):
                    if s + 1 < STEPS:
                        tops(s + 1)
                    normalise(s)
                    if s >= 1:
                        drain(s - 1)
                drain(STEPS - 1)

            @block.sync
            def _(sp):
                sp.wait_ge(out_ready, STEPS)
                for k in range(KD):
                    sp.dma_start(out_dram[k * P:(k + 1) * P, :], out[:, k, :]).then_inc(stored, 16)
                sp.wait_ge(stored, 16 * KD)


SSM_TILES = 16
SSM_HEADS = 32
GROUPS = 4
CHUNKS = T // P
CONV_TILES = 24
TAPS = 4
XBC_ROWS, Z_ROWS, DT_ROWS = 0, 4608, 8704
XS_BUFFERS = 3


def ssm_phase(nc, name, proj, head_dram, tile_dram, causal_dram, spread_dram, out_dram, const):
    ctx = Phase(nc)
    with ctx:
        def sb(what, shape, dt=F32):
            return ctx.enter_context(nc.sbuf_tensor(f"{name}_{what}", shape, dt))

        def sem(what):
            return ctx.semaphore(f"{name}_{what}")

        b_c = sb("b_c", [P, 2 * GROUPS, T])
        a_hi, a_lo = sb("a_hi", [32, T], F32R), sb("a_lo", [32, T], F32R)
        spread = sb("spread", [32, SSM_TILES, P], F32R)
        neg_a = sb("neg_a", [P, CHUNKS, SSM_HEADS])
        dt = sb("dt", [P, CHUNKS, SSM_HEADS])
        dt_out = sb("dt_out", [P, CHUNKS, SSM_HEADS])
        decay = sb("decay", [P, CHUNKS, SSM_HEADS])
        tile_par = sb("tile_par", [P, SSM_TILES, 2])
        identity16 = sb("identity16", [P, P], BF16)
        causal16 = sb("causal16", [P, 4, P], BF16)
        b_nat = sb("b_nat", [P, CHUNKS, GROUPS, P])
        cb = sb("cb", [P, GROUPS, T])

        with ExitStack() as first:
            def fsb(what, shape, dt=F32):
                return first.enter_context(nc.sbuf_tensor(f"{name}_{what}", shape, dt))

            head = fsb("head", [32, 2])
            rate = fsb("rate", [32, 1])
            raw = fsb("dt_raw", [32, T])
            one = fsb("one", [32, P])
            a_t = fsb("a_t", [32, T])
            work = [fsb(f"work{k}", [32, T]) for k in range(6)]
            spread_decay = fsb("spread_decay", [32, CHUNKS, 32])
            causal = fsb("causal", [P, P])
            spread_in = fsb("spread_in", [32, SSM_TILES, P])
            turn = first.enter_context(nc.psum_tensor(name + "_b_acc", [P, 2, GROUPS, P], F32))
            dots = first.enter_context(nc.psum_tensor(name + "_cb_acc", [P, 2, HALF], F32))
            t_acc = first.enter_context(nc.psum_tensor(name + "_turn_acc", [P, 3, HALF], F32))
            d_acc = first.enter_context(nc.psum_tensor(name + "_decay_acc", [P, HALF], F32))
            small_in, pick_in, dt_in, b_in, c_in, chain, acted, turned, b_turned, b_read, dotted, dots_read, a_high = (
                sem(s) for s in ("small_in", "pick_in", "dt_in", "b_in", "c_in", "chain", "acted", "turned", "b_turned",
                                 "b_read", "dotted", "dots_read", "a_high"))
            block = first.enter_context(nc.Block())

            @block.sync
            def _(sp):
                sp.dma_start(raw[:], proj[DT_ROWS:DT_ROWS + 32, :]).then_inc(dt_in, 16)
                for dst, src in ((head[:], head_dram), (tile_par[:], tile_dram), (causal[:], causal_dram)):
                    sp.dma_start(dst, src).then_inc(small_in, 16)
                for g in range(2 * GROUPS):
                    at = XBC_ROWS + (SSM_TILES + g) * P
                    sp.dma_start(b_c[:, g, :], proj[at:at + P, :]).then_inc(b_in if g < GROUPS else c_in, 16)
                sp.dma_start(spread_in[:], spread_dram).then_inc(pick_in, 16)

            @block.scalar
            def _(act):
                act.wait_ge(chain, 2)
                act.activation(work[1][:], work[1][:], ACT.Exp, scale=-1.0).then_inc(acted, 1)
                act.wait_ge(small_in, 48)
                act.activation(rate[:], head[:, 1:2], ACT.Exp).then_inc(acted, 1)
                act.wait_ge(chain, 3)
                act.activation(work[3][:], work[2][:], ACT.Ln).then_inc(acted, 1)
                for c in range(CHUNKS):
                    act.wait_ge(b_turned, c + 1)
                    act.activation(b_nat[:, c, :, :], turn[:, c % 2, :, :], ACT.Copy).then_inc(b_read, 1)
                    act.wait_ge(dotted, c + 1)
                    act.activation(cb[:, :, c * P:(c + 1) * P], dots[:, c % 2, :].rearrange("p (g t) -> p g t", g=GROUPS),
                                   ACT.Copy).then_inc(dots_read, 1)
                act.wait_ge(chain, 13 + CHUNKS + 1)
                act.activation(work[0][:], work[0][:], ACT.Exp, scale=-1.0).then_inc(acted, 1)
                act.activation(work[2][:, 0:CHUNKS], a_t[:, P - 1::P], ACT.Exp).then_inc(acted, 1)
                act.activation(a_hi[:], a_t[:], ACT.Copy).then_inc(a_high, 1)
                act.wait_ge(pick_in, 16)
                act.activation(spread[:], spread_in[:], ACT.Copy)

            @block.tensor
            def _(pe):
                pe.wait_ge(b_in, 16 * GROUPS)
                for c in range(CHUNKS):
                    at = slice(c * P, (c + 1) * P)
                    if c >= 2:
                        pe.wait_ge(b_read, c - 1)
                        pe.wait_ge(dots_read, c - 1)
                    for g in range(GROUPS):
                        mm = pe.transpose(turn[:, c % 2, g, :], b_c[:, g, at], const.identity)
                    mm.then_inc(b_turned, 1)
                    if c == 0:
                        pe.wait_ge(c_in, 16 * GROUPS)
                    for g in range(GROUPS):
                        mm = pe.matmul(dots[:, c % 2, g * P:(g + 1) * P], b_c[:, g, at], b_c[:, GROUPS + g, at],
                                       start=True, stop=True)
                    mm.then_inc(dotted, 1)
                pe.wait_ge(chain, 13 + CHUNKS + 2)
                for j, src in enumerate((a_t, work[5], work[0])):
                    for c in range(CHUNKS):
                        mm = pe.transpose(t_acc[:, j, c * 32:(c + 1) * 32], src[:, c * P:(c + 1) * P],
                                          const.identity[0:32, 0:32])
                mm.then_inc(turned, 1)
                pe.wait_ge(chain, 13 + CHUNKS + 3)
                pe.matmul(d_acc[:, 0:256], const.ones[0:32, :], spread_decay[:, :, :].rearrange("p a b -> p (a b)"),
                          start=True, stop=True).then_inc(turned, 1)

            @block.vector
            def _(dve):
                links = [0]

                def link(instruction):
                    links[0] += 1
                    instruction.then_inc(chain, 1)
                    dve.wait_ge(chain, links[0])

                x, e, u, log, w4, dt_t = (w[:] for w in work)
                dve.memset(one[:], 1.0)
                dve.wait_ge(small_in, 48)
                dve.wait_ge(dt_in, 16)
                link(dve.tensor_scalar(x, raw[:], head[:, 0:1], None, ALU.add))
                link(dve.scalar_tensor_tensor(out=e, in0=x, scalar=-1.0, in1=x, op0=ALU.mult, op1=ALU.max))
                dve.wait_ge(acted, 1)
                link(dve.tensor_scalar(u, e, 1.0, None, ALU.add))
                link(dve.tensor_scalar(w4, u, -1.0, None, ALU.add))
                link(dve.tensor_scalar(dt_t, w4, 0.0, None, ALU.is_equal))
                link(dve.tensor_tensor(w4, w4, dt_t, ALU.add))
                link(dve.tensor_tensor(dt_t, dt_t, e, ALU.mult))
                dve.wait_ge(acted, 3)
                link(dve.tensor_tensor(e, log, e, ALU.mult))
                link(dve.reciprocal(log, w4))
                link(dve.tensor_tensor(e, e, log, ALU.mult))
                link(dve.tensor_tensor(dt_t, dt_t, e, ALU.add))
                link(dve.scalar_tensor_tensor(out=dt_t, in0=x, scalar=0.0, in1=dt_t, op0=ALU.max, op1=ALU.add))
                link(dve.tensor_scalar(x, dt_t, rate[:, 0:1], -1.0, ALU.mult, ALU.mult))
                for c in range(CHUNKS):
                    at = slice(c * P, (c + 1) * P)
                    link(dve.tensor_tensor_scan(out=a_t[:, at], data0=one[:], data1=x[:, at], initial=0.0,
                                                op0=ALU.mult, op1=ALU.add))
                a3 = a_t[:].rearrange("p (c t) -> p c t", c=CHUNKS)
                link(dve.tensor_tensor(x.rearrange("p (c t) -> p c t", c=CHUNKS), a3,
                                       a3[:, :, P - 1:P].to_broadcast([32, CHUNKS, P]), ALU.subtract))
                dve.wait_ge(acted, 5)
                link(dve.tensor_tensor(x, x, dt_t, ALU.mult))
                link(dve.tensor_tensor(spread_decay[:], work[2][:, 0:CHUNKS].unsqueeze(2).to_broadcast([32, CHUNKS, 32]),
                                       const.identity[0:32, 0:32].unsqueeze(1).to_broadcast([32, CHUNKS, 32]), ALU.mult))
                dve.tensor_copy(identity16[:], const.identity)
                dve.tensor_copy(causal16[:], causal[:].unsqueeze(1).to_broadcast([P, 4, P]))
                dve.wait_ge(a_high, 1)
                dve.tensor_tensor(a_lo[:], a_t[:], a_hi[:].bitcast(F32), ALU.subtract)
                dve.wait_ge(turned, 2)
                dve.tensor_scalar(neg_a[:].rearrange("p a b -> p (a b)"), t_acc[:, 0, 0:256], -1.0, None, ALU.mult)
                for j, dst in ((1, dt), (2, dt_out)):
                    dve.tensor_copy(dst[:].rearrange("p a b -> p (a b)"), t_acc[:, j, 0:256])
                dve.tensor_copy(decay[:].rearrange("p a b -> p (a b)"), d_acc[:, 0:256])

        xs = sb("xs", [P, XS_BUFFERS, T])
        scaled_x = sb("scaled_x", [P, CHUNKS, 2, 64])
        out_x = sb("out_x", [P, CHUNKS, 2, 64])
        weight = sb("weight", [P, 2, T])
        state = sb("state", [P, CHUNKS, 2, 64])
        grown = sb("grown", [P, T])
        z = sb("z", [P, 4, T])
        y = sb("y", [P, 4, T])
        square = sb("square", [P, 4, T])
        rstd = sb("rstd", [P, T])
        mean, aux = square[:, 0, :], square[:, 1, :]
        pair_a = ctx.enter_context(nc.psum_tensor(name + "_pair_a", [P, 2, HALF], F32))
        pair_b = ctx.enter_context(nc.psum_tensor(name + "_pair_b", [P, 2, HALF], F32))
        pair_c = ctx.enter_context(nc.psum_tensor(name + "_pair_c", [P, 2, HALF], F32))
        pair_d = ctx.enter_context(nc.psum_tensor(name + "_pair_d", [P, 2, HALF], F32))
        xs_in = [sem(f"xs_in{b}") for b in range(XS_BUFFERS)]
        z_in = [sem(f"z_in{g}") for g in range(GROUPS)]
        (x_turned, x_scaled, b_made, decayed, grown_up, states_made, state_ready, weighted, from_state, off_done, within,
         y_read, y_done, squared, summed, rooting, rooted, normed, gated, chain2) = (
            sem(s) for s in ("x_turned", "x_scaled", "b_made", "decayed", "grown_up", "states_made", "state_ready",
                             "weighted", "from_state", "off_done", "within", "y_read", "y_done", "squared", "summed",
                             "rooting", "rooted", "normed", "gated", "chain2"))
        stored = [sem(f"stored{k}") for k in range(4)]
        block = ctx.enter_context(nc.Block())

        @block.sync
        def _(sp):
            def load_xs(j):
                sp.dma_start(xs[:, j % XS_BUFFERS, :],
                             proj[XBC_ROWS + j * P:XBC_ROWS + (j + 1) * P, :]).then_inc(xs_in[j % XS_BUFFERS], 16)

            def load_z(g):
                for k in range(4):
                    at = Z_ROWS + (4 * g + k) * P
                    sp.dma_start(z[:, k, :], proj[at:at + P, :]).then_inc(z_in[g], 16)

            load_xs(0)
            load_z(0)
            for j in range(1, XS_BUFFERS):
                load_xs(j)
            for j in range(SSM_TILES):
                if j >= 4:
                    sp.wait_ge(normed, j - 3)
                    sp.dma_start(out_dram[(j - 4) * P:(j - 3) * P, :], y[:, j % 4, :]).then_inc(stored[j % 4], 16)
                if j % 4 == 3 and j + 1 < SSM_TILES:
                    sp.wait_ge(y_done, j + 1)
                    load_z(j // 4 + 1)
                if j + XS_BUFFERS < SSM_TILES:
                    sp.wait_ge(y_done, j + 1)
                    load_xs(j + XS_BUFFERS)
            for k in range(4):
                sp.wait_ge(normed, 13 + k)
                sp.dma_start(out_dram[(12 + k) * P:(13 + k) * P, :], y[:, k, :]).then_inc(stored[k], 16)
            for k in range(4):
                sp.wait_ge(stored[k], 16 * GROUPS)

        @block.tensor
        def _(pe):
            def turn_xs(j):
                pe.wait_ge(xs_in[j % XS_BUFFERS], 16 * (j // XS_BUFFERS + 1))
                if j >= 1:
                    pe.wait_ge(state_ready, j)
                for c in range(CHUNKS):
                    mm = pe.transpose(pair_a[:, c // 4, c % 4 * P:(c % 4 + 1) * P],
                                      xs[:, j % XS_BUFFERS, c * P:(c + 1) * P], const.identity)
                mm.then_inc(x_turned, 1)

            def spread_a(j, h):
                if h < 2:
                    if h == 0 and j >= 1:
                        pe.wait_ge(grown_up, j)
                    if h == 1:
                        pe.wait_ge(decayed, 2 * j + 1)
                else:
                    pe.wait_ge(decayed, 2 * j + 2)
                for half in range(2):
                    lhs = (spread[:, j, 64 * h:64 * h + 1].to_broadcast([32, P]) if h < 2 else spread[:, j, :])
                    pe.matmul(pair_b[:, half, :], lhs, a_hi[:, half * HALF:(half + 1) * HALF], start=True, stop=False)
                    mm = pe.matmul(pair_b[:, half, :], lhs, a_lo[:, half * HALF:(half + 1) * HALF],
                                   start=False, stop=(h == 2))
                    if h < 2:
                        mm = pe.matmul(pair_b[:, half, :], identity16[:], causal16[:, :, :].rearrange("p a b -> p (a b)"),
                                       start=False, stop=True)
                mm.then_inc(b_made, 1)

            def sum_group(g):
                pe.wait_ge(off_done, 4 * g + 4)
                pe.wait_ge(squared, 4 * g + 4)
                for k in range(4):
                    for half in range(2):
                        mm = pe.matmul(pair_c[:, half, :], const.ones, square[:, k, half * HALF:(half + 1) * HALF],
                                       start=(k == 0), stop=(k == 3))
                mm.then_inc(summed, 1)

            turn_xs(0)
            spread_a(0, 0)
            spread_a(0, 1)
            for j in range(SSM_TILES):
                g = j // 4
                pe.wait_ge(x_scaled, j + 1)
                for c in range(CHUNKS - 1):
                    mm = pe.matmul(pair_a[:, c // 4, c % 4 * P:(c % 4 + 1) * P], b_nat[:, c, g, :],
                                   out_x[:, c, :, :].rearrange("p a b -> p (a b)"), start=True, stop=True)
                mm.then_inc(states_made, 1)
                spread_a(j, 2)
                if j >= 1:
                    pe.wait_ge(y_read, j)
                for h in range(2):
                    pe.wait_ge(weighted, 2 * j + h + 1)
                    for c in range(CHUNKS):
                        mm = pe.matmul(pair_d[64 * h:64 * h + 64, c // 4, c % 4 * P:(c % 4 + 1) * P],
                                       scaled_x[:, c, h, :], weight[:, h, c * P:(c + 1) * P], start=True, stop=True)
                mm.then_inc(within, 1)
                if j + 1 < SSM_TILES:
                    turn_xs(j + 1)
                    spread_a(j + 1, 0)
                if j % 4 == 0 and j >= 4:
                    sum_group(g - 1)
                    pe.wait_ge(rooting, 7 * (g - 1) + 1)
                elif j >= 1:
                    pe.wait_ge(off_done, j)
                pe.wait_ge(state_ready, j + 1)
                for c in range(1, CHUNKS):
                    mm = pe.matmul(pair_c[:, c // 4, c % 4 * P:(c % 4 + 1) * P],
                                   state[:, c, :, :].rearrange("p a b -> p (a b)"), b_c[:, GROUPS + g, c * P:(c + 1) * P],
                                   start=True, stop=True)
                mm.then_inc(from_state, 1)
                if j + 1 < SSM_TILES:
                    spread_a(j + 1, 1)
            sum_group(GROUPS - 1)

        @block.scalar
        def _(act):
            def decays(j, h):
                act.wait_ge(b_made, 3 * j + h + 1)
                if j >= 1:
                    act.wait_ge(within, j)
                for c in range(CHUNKS):
                    ins = act.activation(weight[:, h, c * P:(c + 1) * P], pair_b[:, c // 4, c % 4 * P:(c % 4 + 1) * P],
                                         ACT.Exp, bias=neg_a[:, c, 2 * j + h:2 * j + h + 1])
                ins.then_inc(decayed, 1)

            def silu_gate(j):
                if j % 4 == 0:
                    act.wait_ge(z_in[j // 4], 64)
                act.activation(z[:, j % 4, :], z[:, j % 4, :], ACT.Silu).then_inc(gated, 1)

            decays(0, 0)
            decays(0, 1)
            for j in range(SSM_TILES):
                g = j // 4
                act.wait_ge(b_made, 3 * j + 3)
                if j >= 1:
                    act.wait_ge(off_done, j)
                act.activation(grown[:], pair_b[:, :, :].rearrange("p a b -> p (a b)"), ACT.Exp).then_inc(grown_up, 1)
                silu_gate(j)
                if j + 1 < SSM_TILES:
                    decays(j + 1, 0)
                if j % 4 == 0 and j >= 4:
                    act.wait_ge(rooting, 7 * (g - 1) + 2)
                    act.activation(rstd[:], aux, ACT.Sqrt).then_inc(rooted, 1)
                if j + 1 < SSM_TILES:
                    decays(j + 1, 1)
                act.wait_ge(y_done, j + 1)
                if j % 4 == 0 and j >= 4:
                    act.wait_ge(rooting, 7 * (g - 1) + 7)
                act.activation(square[:, j % 4, :], y[:, j % 4, :], ACT.Square).then_inc(squared, 1)
            act.wait_ge(rooting, 7 * (GROUPS - 1) + 2)
            act.activation(rstd[:], aux, ACT.Sqrt).then_inc(rooted, 1)

        @block.vector
        def _(dve):
            links = [0]

            def link(instruction):
                links[0] += 1
                instruction.then_inc(chain2, 1)
                dve.wait_ge(chain2, links[0])

            def flat(ap):
                return ap.rearrange("p a b -> p (a b)")

            def scale_xs(j):
                dve.wait_ge(x_turned, j + 1)
                if j >= 1:
                    dve.wait_ge(within, j)
                turned = pair_a[:, :, :].rearrange("p a (c h d) -> p (a c) h d", c=4, h=2)
                for dst, scale in ((out_x, dt_out), (scaled_x, dt)):
                    ins = dve.tensor_tensor(dst[:, :, :, :], turned,
                                            scale[:, :, 2 * j:2 * j + 2].unsqueeze(3).to_broadcast([P, CHUNKS, 2, 64]),
                                            ALU.mult)
                ins.then_inc(x_scaled, 1)

            def weigh(j, h):
                dve.wait_ge(decayed, 2 * j + h + 1)
                dve.tensor_tensor(weight[:, h, :], weight[:, h, :], cb[:, j // 4, :], ALU.mult).then_inc(weighted, 1)

            def scan(j):
                dve.wait_ge(states_made, j + 1)
                if j >= 1:
                    dve.wait_ge(from_state, j)
                for c in range(CHUNKS - 1):
                    made = pair_a[:, c // 4, c % 4 * P:(c % 4 + 1) * P].rearrange("p (h d) -> p h d", h=2)
                    if c == 0:
                        link(dve.tensor_copy(state[:, 1, :, :], made))
                        continue
                    for h in range(2):
                        ins = dve.scalar_tensor_tensor(out=state[:, c + 1, h, :], in0=state[:, c, h, :],
                                                       scalar=decay[:, c, 2 * j + h:2 * j + h + 1], in1=made[:, h, :],
                                                       op0=ALU.mult, op1=ALU.add)
                        if h == 1 and c < CHUNKS - 2:
                            link(ins)
                ins.then_inc(state_ready, 1)

            def outputs(j):
                dve.wait_ge(from_state, j + 1)
                dve.wait_ge(grown_up, j + 1)
                out, g = y[:, j % 4, :], j // 4
                if j >= 4:
                    dve.wait_ge(stored[j % 4], 16 * g)
                dve.tensor_tensor(out[:, P:], flat(pair_c[:, :, :])[:, P:], grown[:, P:], ALU.mult).then_inc(off_done, 1)
                dve.wait_ge(within, j + 1)
                dve.tensor_copy(out[:, :P], pair_d[:, 0, :P])
                dve.wait_ge(off_done, j + 1)
                dve.tensor_tensor(out[:, P:], out[:, P:], flat(pair_d[:, :, :])[:, P:], ALU.add).then_inc(y_read, 1)
                dve.wait_ge(y_read, j + 1)
                link(dve.scalar_tensor_tensor(out=out, in0=xs[:, j % XS_BUFFERS, :], scalar=tile_par[:, j, 0:1], in1=out,
                                              op0=ALU.mult, op1=ALU.add))
                dve.wait_ge(gated, j + 1)
                dve.tensor_tensor(out, out, z[:, j % 4, :], ALU.mult).then_inc(y_done, 1)

            def norm_root(g):
                dve.wait_ge(summed, g + 1)
                base = 7 * g
                dve.tensor_scalar(mean, flat(pair_c[:, :, :]), 1.0 / 512, EPS, ALU.mult, ALU.add).then_inc(rooting, 1)
                dve.wait_ge(rooting, base + 1)
                dve.reciprocal(aux, mean).then_inc(rooting, 1)

            def norm_group(g):
                base = 7 * g
                dve.wait_ge(rooted, g + 1)
                dve.tensor_tensor(aux, rstd[:], rstd[:], ALU.mult).then_inc(rooting, 1)
                dve.wait_ge(rooting, base + 3)
                dve.tensor_tensor(aux, aux, mean, ALU.mult).then_inc(rooting, 1)
                dve.wait_ge(rooting, base + 4)
                dve.tensor_scalar(aux, aux, -0.5, 1.5, ALU.mult, ALU.add).then_inc(rooting, 1)
                dve.wait_ge(rooting, base + 5)
                dve.tensor_tensor(rstd[:], rstd[:], aux, ALU.mult).then_inc(rooting, 2)
                dve.wait_ge(rooting, base + 7)
                for k in range(4):
                    dve.scalar_tensor_tensor(out=y[:, k, :], in0=y[:, k, :], scalar=tile_par[:, 4 * g + k, 1:2],
                                             in1=rstd[:], op0=ALU.mult, op1=ALU.mult).then_inc(normed, 1)

            scale_xs(0)
            weigh(0, 0)
            weigh(0, 1)
            for j in range(SSM_TILES):
                scan(j)
                if j + 1 < SSM_TILES:
                    scale_xs(j + 1)
                    weigh(j + 1, 0)
                if j % 4 == 0 and j >= 4:
                    norm_root(j // 4 - 1)
                if j + 1 < SSM_TILES:
                    weigh(j + 1, 1)
                if j % 4 == 0 and j >= 4:
                    norm_group(j // 4 - 1)
                outputs(j)
            norm_root(GROUPS - 1)
            norm_group(GROUPS - 1)
class Activations:

    def __init__(self, nc, scope, what, kt, source, gain=None):
        self.kt, self.source, self.gain, self.what = kt, source, gain, what
        self.hi, self.lo = (scope.enter_context(nc.sbuf_tensor(f"{what}_{part}", [P, kt, T], F32R)) for part in ("hi", "lo"))
        self.rstd = scope.enter_context(nc.sbuf_tensor(what + "_rstd", [P, T], F32)) if gain is not None else None


def linear_phase(nc, name, a, w_dram, segments, out_dram, extra1=None, extra2=None, const=None, taps_dram=None):
    kt, source, normed = a.kt, a.source, a.gain is not None
    extras = [e for e in (extra1, extra2) if e is not None]
    nt = sum(tiles for tiles, _ in segments)
    kinds = [kind for _, kind in segments]
    uses = [(nt + 1) // 2, nt // 2]
    depth = 4 if kt <= 8 else 2
    depth = min(depth, kt)
    ctx = Phase(nc)
    with ctx:
        def sb(what, shape, dt=F32):
            return ctx.enter_context(nc.sbuf_tensor(f"{name}_{what}", shape, dt))

        def sem(what):
            return ctx.semaphore(f"{name}_{what}")

        two = range(2)
        raw, w_hi, w_lo = sb("raw", [P, 2, kt * P]), sb("w_hi", [P, 2, kt * P], F32R), sb("w_lo", [P, 2, kt * P], F32R)
        out = sb("out", [P, 2, T])
        side = [sb(f"side{j}", [P, 2, T]) for j in range(len(extras))]
        acc = ctx.enter_context(nc.psum_tensor(name + "_acc", [P, 4, HALF], F32))
        raw_in, high, low, product, drained, side_in, gated, stored, silued, scaled = (
            [sem(f"{what}{b}") for b in two] for what in
            ("raw_in", "high", "low", "product", "drained", "side_in", "gated", "stored", "silued", "scaled"))
        step, storing = sem("step"), sem("storing")
        if source is not None:
            a_raw = sb("a_raw", [P, depth, T])
            a_in = [sem(f"a_in{b}") for b in range(depth)]
            a_high, a_low, squared, summed, inverse, root, gain_in = (
                sem(s) for s in ("a_high", "a_low", "squared", "summed", "inverse", "root", "gain_in"))
        if source is not None and normed:
            gain, square = sb("gain", [P, kt]), sb("square", [P, 2, T])
            total = ctx.enter_context(nc.psum_tensor(name + "_total", [P, 2, HALF], F32))
        if "conv" in kinds:
            conv_tiles = dict((kind, tiles) for tiles, kind in segments)["conv"]
            taps, padded = sb("taps", [P, conv_tiles, TAPS + 1]), sb("padded", [P, 2, T + TAPS - 1])
            taps_in = sem("taps_in")
        block = ctx.enter_context(nc.Block())

        def bank(b):
            return acc[:, 2 * b:2 * b + 2, :].rearrange("p a b -> p (a b)")

        def all_turns(engine, step_of, peel=False):
            at = 0
            for tiles, kind in segments:
                ends = at + tiles == nt
                turns = (tiles - (3 if tiles % 2 else 2)) // 2 if ends else tiles // 2
                start = 0

                def pair(i, count=2):
                    for b in range(count):
                        n = 2 * i + (at + b)
                        step_of(n, b, i + at // 2, kind, i, not isinstance(i, int) or n + 2 < nt)

                if peel and at == 0:
                    pair(0)
                    start = 1
                if turns > start:
                    with engine.Fori(start, turns) as i:
                        pair(i)
                if ends:
                    for i in range(max(turns, start), (tiles + 1) // 2):
                        pair(i, min(2, tiles - 2 * i))
                at += tiles

        @block.sync
        def _(sp):
            for b in two:
                sp.sem_inc(stored[b], 16)

            def load(n, b):
                sp.dma_start(raw[:, b, :], w_dram[bass.ds(n * P, P), :]).then_inc(raw_in[b], 16)

            def load_sides(n, b, use):
                if extras:
                    sp.wait_ge(drained[b], use + 1)
                    sp.sem_inc(storing, 1)
                    for j, e in enumerate(extras):
                        sp.dma_start(side[j][:, b, :], e[bass.ds(n * P, P), :]).then_inc(side_in[b], 16)

            def store(n, b, use, kind, i):
                if kind == "conv":
                    sp.wait_ge(silued[b], i + 1)
                else:
                    sp.wait_ge(drained[b], use + 2)
                sp.sem_inc(storing, 1)
                sp.dma_start(out_dram[bass.ds(n * P, P), :], out[:, b, :]).then_inc(stored[b], 16)

            def tile(n, b, use, kind, i, ahead):
                if ahead:
                    sp.wait_ge(low[b], use + 1)
                    sp.sem_inc(storing, 1)
                    load(n + 2, b)
                if not isinstance(n, int) or n + 1 < nt:
                    load_sides(n + 1, 1 - b, use + b)
                store(n, b, use, kind, i)

            load(0, 0)
            if source is not None:
                if normed:
                    sp.dma_start(gain[:], a.gain).then_inc(gain_in, 16)
                for k in range(kt):
                    if k >= depth:
                        sp.wait_ge(a_low, k - depth + 1)
                        if normed:
                            sp.wait_ge(squared, k - depth + 1)
                    sp.dma_start(a_raw[:, k % depth, :], source[k * P:(k + 1) * P, :]).then_inc(a_in[k % depth], 16)
            if nt > 1:
                load(1, 1)
            if "conv" in kinds:
                sp.dma_start(taps[:], taps_dram).then_inc(taps_in, 16)
            load_sides(0, 0, 0)
            all_turns(sp, tile)
            for b in two:
                sp.wait_ge(stored[b], 16 * (uses[b] + 1))

        @block.scalar
        def _(act):
            def split(b, use):
                act.wait_ge(raw_in[b], use * 16 + 16)
                if not (isinstance(use, int) and use == 0):
                    act.wait_ge(product[b], use)
                act.activation(w_hi[:, b, :], raw[:, b, :], ACT.Copy).then_inc(high[b], 1)

            def gate(b, use, kind, i):
                o = out[:, b, :]
                if kind in ("gate", "gate_add"):
                    act.wait_ge(side_in[b], use * (16 * len(extras)) + 16 * len(extras))
                    act.activation(side[0][:, b, :], side[0][:, b, :], ACT.Sigmoid).then_inc(gated[b], 1)
                if kind == "final":
                    act.wait_ge(scaled[b], use + 1)
                    act.activation(o, o, ACT.Sigmoid).then_inc(gated[b], 1)
                if kind == "conv":
                    act.wait_ge(drained[b], use + 2)
                    act.activation(o, o, ACT.Silu).then_inc(silued[b], 1)

            def tile(n, b, use, kind, i, ahead):
                if ahead:
                    split(b, use + 1)
                gate(b, use, kind, i)

            split(0, 0)
            if source is not None:
                if normed:
                    act.wait_ge(gain_in, 16)
                for k in range(kt):
                    act.wait_ge(a_in[k % depth], 16 * (k // depth + 1))
                    part = a_raw[:, k % depth, :]
                    if normed:
                        act.activation(a.hi[:, k, :], part, ACT.Copy, scale=gain[:, k:k + 1]).then_inc(a_high, 1)
                        if k >= 2:
                            act.wait_ge(summed, k - 1)
                        act.activation(square[:, k % 2, :], part, ACT.Square).then_inc(squared, 1)
                    else:
                        act.activation(a.hi[:, k, :], part, ACT.Copy).then_inc(a_high, 1)
            if nt > 1:
                split(1, 0)
            if source is not None and normed:
                act.wait_ge(inverse, 2)
                act.activation(a.rstd[:], a.rstd[:], ACT.Sqrt).then_inc(root, 1)
            all_turns(act, tile)

        @block.vector
        def _(dve):
            for b in two:
                dve.sem_inc(drained[b], 1)

            def split(b, use):
                dve.wait_ge(high[b], use + 1)
                dve.tensor_tensor(w_lo[:, b, :], raw[:, b, :], w_hi[:, b, :].bitcast(F32),
                                  ALU.subtract).then_inc(low[b], 1)

            def split_activations():
                for k in range(kt):
                    dve.wait_ge(a_high, k + 1)
                    part, hi = a_raw[:, k % depth, :], a.hi[:, k, :].bitcast(F32)
                    if normed:
                        ins = dve.scalar_tensor_tensor(out=a.lo[:, k, :], in0=part, scalar=gain[:, k:k + 1], in1=hi,
                                                       op0=ALU.mult, op1=ALU.subtract)
                    else:
                        ins = dve.tensor_tensor(a.lo[:, k, :], part, hi, ALU.subtract)
                    ins.then_inc(a_low, 1)

            def norm():
                dve.wait_ge(summed, kt)
                mean, aux, rstd = square[:, 0, :], square[:, 1, :], a.rstd[:]
                dve.tensor_scalar(mean, total[:, :, :].rearrange("p a b -> p (a b)"), 1.0 / (kt * P), EPS,
                                  ALU.mult, ALU.add).then_inc(inverse, 1)
                dve.wait_ge(inverse, 1)
                dve.reciprocal(rstd, mean).then_inc(inverse, 1)
                dve.wait_ge(root, 1)
                dve.tensor_tensor(aux, rstd, rstd, ALU.mult).then_inc(inverse, 1)
                dve.wait_ge(inverse, 3)
                dve.tensor_tensor(aux, aux, mean, ALU.mult).then_inc(inverse, 1)
                dve.wait_ge(inverse, 4)
                dve.tensor_scalar(aux, aux, -0.5, 1.5, ALU.mult, ALU.add).then_inc(inverse, 1)
                dve.wait_ge(inverse, 5)
                dve.tensor_tensor(rstd, rstd, aux, ALU.mult).then_inc(inverse, 1)
                dve.wait_ge(inverse, 6)

            def link(instruction, count):
                instruction.then_inc(step, 1)
                dve.wait_ge(step, count)

            def epilogue(b, use, kind, i):
                dve.wait_ge(product[b], use + 1)
                o, s0 = out[:, b, :], (side[0][:, b, :] if extras else None)
                dve.wait_ge(stored[b], use * 16 + 16)
                if kind == "copy":
                    if normed:
                        dve.tensor_tensor(o, bank(b), a.rstd[:], ALU.mult).then_inc(drained[b], 1)
                    else:
                        dve.tensor_copy(o, bank(b)).then_inc(drained[b], 1)
                elif kind == "add":
                    dve.wait_ge(side_in[b], use * 16 + 16)
                    dve.tensor_tensor(o, bank(b), s0, ALU.add).then_inc(drained[b], 1)
                elif kind == "gate":
                    dve.wait_ge(gated[b], use + 1)
                    dve.tensor_tensor(o, bank(b), s0, ALU.mult).then_inc(drained[b], 1)
                elif kind == "gate_add":
                    dve.wait_ge(gated[b], use + 1)
                    link(dve.tensor_tensor(o, bank(b), s0, ALU.mult), use * 2 + (b + 1))
                    dve.tensor_tensor(o, o, side[1][:, b, :], ALU.add).then_inc(drained[b], 1)
                elif kind == "final":
                    dve.tensor_tensor(o, bank(b), a.rstd[:], ALU.mult).then_inc(scaled[b], 1)
                    dve.wait_ge(gated[b], use + 1)
                    dve.wait_ge(side_in[b], use * 32 + 32)
                    link(dve.tensor_tensor(o, o, s0, ALU.mult), use * 2 + (b + 1))
                    dve.tensor_tensor(o, o, side[1][:, b, :], ALU.add).then_inc(drained[b], 1)
                elif kind == "conv":
                    tap = taps[:, bass.ds(2 * i + b, 1), :].rearrange("p a k -> p (a k)")
                    links = i * 8 + 4 * b
                    u = padded[:, b, :]
                    link(dve.tensor_tensor(u[:, TAPS - 1:], bank(b), a.rstd[:], ALU.mult), links + 1)
                    link(dve.tensor_scalar(o, u[:, 3:3 + T], tap[:, 3:4], tap[:, 4:5], ALU.mult, ALU.add), links + 2)
                    for k in range(TAPS - 1):
                        ins = dve.scalar_tensor_tensor(out=o, in0=u[:, k:k + T], scalar=tap[:, k:k + 1], in1=o,
                                                       op0=ALU.mult, op1=ALU.add)
                        if k < TAPS - 2:
                            link(ins, links + 3 + k)
                    ins.then_inc(drained[b], 1)

            def tile(n, b, use, kind, i, ahead):
                epilogue(b, use, kind, i)
                if ahead:
                    split(b, use + 1)

            split(0, 0)
            if source is not None:
                split_activations()
            if nt > 1:
                split(1, 0)
            if source is not None and normed:
                norm()
            if "conv" in kinds:
                dve.memset(padded[:, :, 0:TAPS - 1], 0.0)
                dve.wait_ge(taps_in, 16)
            all_turns(dve, tile)

        @block.tensor
        def _(pe):
            def multiply(n, b, use, kind, i, ahead):
                first = source is not None and isinstance(n, int) and n == 0
                pe.wait_ge(low[b], use + 1)
                pe.wait_ge(drained[b], use + 1)
                for k in range(kt):
                    if first:
                        pe.wait_ge(a_low, k + 1)
                    for n_pass, (w, h) in enumerate(((w_hi, a.hi), (w_hi, a.lo), (w_lo, a.hi))):
                        for half in two:
                            mm = pe.matmul(acc[:, 2 * b + half, :], w[:, b, k * P:(k + 1) * P],
                                           h[:, k, half * HALF:(half + 1) * HALF],
                                           start=(k == 0 and n_pass == 0), stop=(k == kt - 1 and n_pass == 2))
                    if first and normed:
                        pe.wait_ge(squared, k + 1)
                        for half in two:
                            ins = pe.matmul(total[:, half, :], const.ones, square[:, k % 2, half * HALF:(half + 1) * HALF],
                                            start=(k == 0), stop=(k == kt - 1))
                        ins.then_inc(summed, 1)
                mm.then_inc(product[b], 1)

            all_turns(pe, multiply, peel=source is not None)


PEER_HEADS = 8
TOP = 16
KEYS = 128
SCORE_SETS = 2 * PEER_HEADS
LOWEST = -3e38
EXPERT_TILES = KEYS
TURN_TILES = 14
GATE_GROUP = 4
GATE_GROUPS = P // GATE_GROUP


def select_phase(nc, name, a, u_dram, hidden_dram, q_dram, keys_dram, count_dram, gates_dram, const):
    ctx = Phase(nc)
    with ctx:
        def sb(what, shape, dt=F32):
            return ctx.enter_context(nc.sbuf_tensor(f"{name}_{what}", shape, dt))

        def sem(what):
            return ctx.semaphore(f"{name}_{what}")

        two = range(2)
        u_raw, u_hi, u_lo = sb("u_raw", [P, 2, D]), sb("u_hi", [P, 2, D], F32R), sb("u_lo", [P, 2, D], F32R)
        hidden = sb("hidden", [P, 2, T])
        gates = sb("gates", [P, KEYS, P])
        first = sb("first", [P, 2, GATE_GROUP, KEYS])
        second = sb("second", [P, 2, GATE_GROUP, KEYS])
        q = sb("q", [P, SCORE_SETS, P])
        keys = sb("keys", [P, SCORE_SETS, KEYS])
        count = sb("count", [P, KEYS])
        work = sb("work", [P, SCORE_SETS * KEYS])
        best = sb("best", [P, SCORE_SETS, TOP])
        index = sb("index", [P, SCORE_SETS, TOP], U32)
        index_f = sb("index_f", [P, SCORE_SETS, TOP])
        total = sb("total", [P, PEER_HEADS, TOP])
        place = sb("place", [P, PEER_HEADS, TOP], U32)
        part = sb("part", [P, 2, PEER_HEADS * TOP], U32)
        part_f = sb("part_f", [P, 2, PEER_HEADS * TOP])
        found = sb("found", [P, 3, PEER_HEADS * TOP])
        chosen = sb("chosen", [P, 3, P])
        denom = sb("denom", [P, 2, PEER_HEADS])
        score = work[:].rearrange("p (s n) -> p s n", s=SCORE_SETS)
        pair = work[:].rearrange("p (h i j) -> p h i j", h=PEER_HEADS, i=TOP)
        u_acc = ctx.enter_context(nc.psum_tensor(name + "_u_acc", [P, 2, 2, HALF], F32))
        s_acc = ctx.enter_context(nc.psum_tensor(name + "_s_acc", [P, 2, HALF], F32))
        g_acc = ctx.enter_context(nc.psum_tensor(name + "_g_acc", [P, 2, GATE_GROUP, KEYS], F32))
        u_in, u_high, u_split, u_done, normed, gelued, kept_hidden = (
            [sem(f"{what}{e}") for e in two] for what in
            ("u_in", "u_high", "u_split", "u_done", "normed", "gelued", "kept_hidden"))
        (small_in, q_in, scored, copied, begun, chain, shifted, exped, routed, turned, chosen_ready, made, spread,
         drained, storing, storing_gates, stored) = (
            sem(s) for s in ("small_in", "q_in", "scored", "copied", "begun", "chain", "shifted", "exped", "routed",
                             "turned", "chosen_ready", "made", "spread", "drained", "storing", "storing_gates", "stored"))
        block = ctx.enter_context(nc.Block())
        TURNS = T // P
        LAST_TILES = EXPERT_TILES - TURNS * TURN_TILES
        SPREAD = [0, 0, 2] + [3] * 8 + [1, 2, 3]
        SPREAD_LAST = [0, 0] + [3] * 10 + [2, 0, 0, 0]
        SPREAD_AT = (2, 5, 7)
        assert len(SPREAD) == TURN_TILES and len(SPREAD_LAST) == LAST_TILES and sum(SPREAD) == sum(SPREAD_LAST) == GATE_GROUPS

        def groups_by_tile(m):
            counts = SPREAD_LAST if isinstance(m, int) and m == TURNS else SPREAD
            return [range(sum(counts[:k]), sum(counts[:k + 1])) for k in range(len(counts))]

        def turns(engine, turn):
            turn(0, True, False)
            with engine.Fori(1, TURNS - 1) as m:
                turn(m, True, True)
            turn(TURNS - 1, True, True)
            turn(TURNS, False, True)

        def is_first(m):
            return isinstance(m, int) and m == 0

        def has_ahead(m, k, ahead):
            return not isinstance(m, int) or m * TURN_TILES + k + ahead < EXPERT_TILES

        @block.sync
        def _(sp):
            q_view = q_dram.rearrange("(s p) t -> p s t", p=P)

            def load_u(tile, e):
                sp.dma_start(u_raw[:, e, :], u_dram[bass.ds(tile * P, P), :]).then_inc(u_in[e], 16)

            def load_q(m):
                sp.dma_start(q[:], q_view[:, :, bass.ds(m * P, P)]).then_inc(q_in, 16)

            for e in two:
                load_u(e, e)
            load_q(0)
            sp.dma_start(keys[:], keys_dram).then_inc(small_in, 16)
            sp.dma_start(count[:], count_dram).then_inc(small_in, 16)

            def turn(m, route, spreads):
                for k in range(TURN_TILES if route else LAST_TILES):
                    if k == 4 and (not isinstance(m, int) or m < TURNS - 1):
                        sp.wait_ge(scored, m * 2 + 2)
                        sp.sem_inc(storing, 1)
                        load_q(m + 1)
                    e, use = k % 2, m * (TURN_TILES // 2) + k // 2
                    if has_ahead(m, k, 2):
                        sp.wait_ge(u_split[e], use + 1)
                        load_u(m * TURN_TILES + (k + 2), e)
                    sp.wait_ge(gelued[e], use + 1)
                    sp.sem_inc(storing, 1)
                    sp.dma_start(hidden_dram[bass.ds((m * TURN_TILES + k) * P, P), :],
                                 hidden[:, e, :]).then_inc(kept_hidden[e], 16)

            turns(sp, turn)
            sp.wait_ge(stored, 16 * (TURNS + 1))
            for e in two:
                sp.wait_ge(kept_hidden[e], 16 * (EXPERT_TILES // 2 + 1))

        @block.tensor
        def _(pe):
            def scores(m, half):
                if half == 0:
                    pe.wait_ge(q_in, m * 16 + 16)
                if half == 1 or not is_first(m):
                    pe.wait_ge(copied, m * 2 + half)
                    if half == 0:
                        pe.wait_ge(chosen_ready, m)
                for s in range(8):
                    mm = pe.matmul(s_acc[:, s // 4, s % 4 * KEYS:(s % 4 + 1) * KEYS], q[:, half * 8 + s, :],
                                   keys[:, half * 8 + s, :], start=True, stop=True)
                mm.then_inc(scored, 1)

            def turn_results(m):
                pe.wait_ge(routed, m + 1)
                for j in range(3):
                    mm = pe.transpose(s_acc[:, 0, j * P:(j + 1) * P], found[:, j, :], const.identity)
                mm.then_inc(turned, 1)

            def hidden_tile(m, k, groups):
                e, use = k % 2, m * (TURN_TILES // 2) + k // 2
                pe.wait_ge(u_split[e], use + 1)
                pe.wait_ge(normed[e], use + 1)
                for kd in range(KD):
                    for n_pass, (w, h) in enumerate(((u_hi, a.hi), (u_hi, a.lo), (u_lo, a.hi))):
                        for half in two:
                            mm = pe.matmul(u_acc[:, e, half, :], w[:, e, kd * P:(kd + 1) * P],
                                           h[:, kd, half * HALF:(half + 1) * HALF],
                                           start=(kd == 0 and n_pass == 0), stop=(kd == KD - 1 and n_pass == 2))
                    if kd == KD - 1:
                        mm.then_inc(u_done[e], 1)
                    for n, r in enumerate(groups):
                        if kd == SPREAD_AT[n]:
                            spread_group(m, r)

            def spread_group(m, r):
                b = r % 2
                pe.wait_ge(made, (m - 1) * GATE_GROUPS + (r + 1))
                pe.wait_ge(drained, (m - 1) * GATE_GROUPS + (r + 1))
                for n in range(GATE_GROUP):
                    mm = pe.matmul(g_acc[:, b, n, :], second[:, b, n, :], first[:, b, n, :], start=True, stop=True)
                mm.then_inc(spread, 1)

            def turn(m, route, spreads):
                groups = groups_by_tile(m)
                for k in range(len(groups)):
                    if k < 2 and route:
                        scores(m, k)
                    hidden_tile(m, k, groups[k - 1] if spreads and k >= 1 else ())
                if spreads:
                    for r in groups[-1]:
                        spread_group(m, r)
                if route:
                    turn_results(m)

            pe.sem_inc(spread, 2)
            pe.wait_ge(small_in, 32)
            turns(pe, turn)

        @block.scalar
        def _(act):
            def split_u(use, e):
                act.wait_ge(u_in[e], use * 16 + 16)
                if not (isinstance(use, int) and use == 0):
                    act.wait_ge(u_done[e], use)
                act.activation(u_hi[:, e, :], u_raw[:, e, :], ACT.Copy).then_inc(u_high[e], 1)

            def store_gates(m):
                act.wait_ge(drained, m * GATE_GROUPS + 2)
                act.sem_inc(storing_gates, 1)
                act.dma_start(gates_dram[:, :, bass.ds((m - 1) * P, P)], gates[:]).then_inc(stored, 16)

            def drain_group(m, r):
                act.wait_ge(spread, (m - 1) * GATE_GROUPS + (r + 3))
                if r == 0:
                    act.wait_ge(stored, m * 16)
                act.activation(gates[:, :, r * GATE_GROUP:(r + 1) * GATE_GROUP], g_acc[:, r % 2, :, :].rearrange("p n k -> p k n"),
                               ACT.Copy).then_inc(drained, 1)

            def copy_scores(m, half):
                act.wait_ge(scored, m * 2 + (half + 1))
                if half == 0 and not is_first(m):
                    act.wait_ge(routed, m)
                act.activation(work[:, half * T:(half + 1) * T], s_acc[:, :, :].rearrange("p a b -> p (a b)"),
                               ACT.Copy).then_inc(copied, 1)

            def turn(m, route, spreads):
                groups = groups_by_tile(m)
                for k in range(len(groups)):
                    e, use = k % 2, m * (TURN_TILES // 2) + k // 2
                    if k < 2 and route:
                        copy_scores(m, k)
                    if spreads and k >= 1:
                        for r in groups[k - 1]:
                            drain_group(m, r)
                        if not route and GATE_GROUPS - 1 in groups[k - 1]:
                            store_gates(m)
                    if has_ahead(m, k, 2):
                        split_u(use + 1, e)
                    act.wait_ge(normed[e], use + 2)
                    act.activation(hidden[:, e, :], hidden[:, e, :], ACT.Gelu_apprx_tanh).then_inc(gelued[e], 1)
                    if k == 11 and route:
                        act.wait_ge(shifted, m + 1)
                        act.activation(found[:, 2, :], found[:, 2, :], ACT.Exp).then_inc(exped, 1)
                if spreads and route:
                    for r in groups[-1]:
                        drain_group(m, r)
                    store_gates(m)
                if route:
                    act.wait_ge(turned, m + 1)
                    act.activation(chosen[:].rearrange("p a b -> p (a b)"), s_acc[:, 0, 0:3 * P],
                                   ACT.Copy).then_inc(chosen_ready, 1)

            act.sem_inc(drained, 2)
            for e in two:
                split_u(0, e)
            turns(act, turn)

        @block.gpsimd
        def _(pool):
            for e in two:
                pool.sem_inc(kept_hidden[e], 16)
            pool.sem_inc(stored, 16)

        @block.vector
        def _(dve):
            links = [0]

            def link(instruction):
                links[0] += 1
                instruction.then_inc(chain, 1)
                dve.wait_ge(chain, links[0])

            def search(values, best16, index16):
                link(dve.max(best16[:, 0:8], values))
                link(dve.max_index(index16[:, 0:8], best16[:, 0:8], values))
                link(dve.match_replace(values, best16[:, 0:8], values, LOWEST))
                link(dve.max(best16[:, 8:16], values))
                link(dve.max_index(index16[:, 8:16], best16[:, 8:16], values))

            shape = [P, PEER_HEADS, TOP, TOP]
            rows = [P, PEER_HEADS * TOP, TOP]

            def route_sets(lo, hi):
                for s in range(lo, hi):
                    search(score[:, s, :], best[:, s, :], index[:, s, :])

            def pair_sums():
                halves = best[:, :, :].rearrange("p (h two) k -> p h two k", two=2)
                link(dve.tensor_copy(index_f[:], index[:]))
                link(dve.tensor_tensor(pair, halves[:, :, 0, :].unsqueeze(3).to_broadcast(shape),
                                       halves[:, :, 1, :].unsqueeze(2).to_broadcast(shape), ALU.add))

            def route_head(h):
                search(pair[:, h, :, :].rearrange("p a b -> p (a b)"), total[:, h, :], place[:, h, :])

            def below_best(m):
                flat_place = place[:].rearrange("p h k -> p (h k)")
                link(dve.tensor_tensor(found[:, 2, :].rearrange("p (h k) -> p h k", k=TOP), total[:],
                                       total[:, :, 0:1].to_broadcast([P, PEER_HEADS, TOP]), ALU.subtract))
                dve.sem_inc(shifted, 1)
                link(dve.tensor_scalar(part[:, 0, :], flat_place, 4, None, ALU.logical_shift_right))
                link(dve.tensor_scalar(part[:, 1, :], flat_place, 15, None, ALU.bitwise_and))
                link(dve.tensor_copy(part_f[:], part[:]))

            def look_up(j):
                ids = index_f[:, :, :].rearrange("p (h two) k -> p h two k", two=2)
                hit_rows = work[:].rearrange("p (a j) -> p a j", j=TOP)
                link(dve.tensor_tensor(hit_rows, count[:, 0:TOP].unsqueeze(1).to_broadcast(rows),
                                       part_f[:, j, :].unsqueeze(2).to_broadcast(rows), ALU.is_equal))
                link(dve.tensor_tensor(pair, pair, ids[:, :, j, :].unsqueeze(2).to_broadcast(shape), ALU.mult))
                link(dve.tensor_reduce(found[:, j, :], hit_rows, AX.X, ALU.add))

            def weigh(m):
                dve.wait_ge(exped, m + 1)
                weights = found[:, 2, :].rearrange("p (h k) -> p h k", k=TOP)
                link(dve.tensor_reduce(denom[:, 0, :], weights, AX.X, ALU.add))
                link(dve.reciprocal(denom[:, 1, :], denom[:, 0, :]))
                link(dve.tensor_tensor(weights, weights,
                                       denom[:, 1, :].unsqueeze(2).to_broadcast([P, PEER_HEADS, TOP]), ALU.mult))
                dve.sem_inc(routed, 1)

            def one_hots(m, r):
                b = r % 2
                if r == 0:
                    dve.wait_ge(chosen_ready, m)
                dve.wait_ge(spread, (m - 1) * GATE_GROUPS + (r + 1))
                for n in range(GATE_GROUP):
                    t = r * GATE_GROUP + n
                    dve.tensor_scalar(second[:, b, n, :], count[:], chosen[:, 1, t:t + 1], None, ALU.is_equal)
                    ins = dve.tensor_scalar(first[:, b, n, :], count[:], chosen[:, 0, t:t + 1], chosen[:, 2, t:t + 1],
                                            ALU.is_equal, ALU.mult)
                ins.then_inc(made, 1)

            def split_u(use, e):
                dve.wait_ge(u_high[e], use + 1)
                dve.tensor_tensor(u_lo[:, e, :], u_raw[:, e, :], u_hi[:, e, :].bitcast(F32),
                                  ALU.subtract).then_inc(u_split[e], 1)

            def norm_hidden(use, e):
                dve.wait_ge(u_done[e], use + 1)
                dve.wait_ge(kept_hidden[e], use * 16 + 16)
                dve.tensor_tensor(hidden[:, e, :], u_acc[:, e, :, :].rearrange("p a b -> p (a b)"), a.rstd[:],
                                  ALU.mult).then_inc(normed[e], 1)

            def turn(m, route, spreads):
                links[0] = 0
                if not is_first(m) and route:
                    dve.sem_clear(chain)
                groups = groups_by_tile(m)
                for k in range(len(groups)):
                    n = k + 1
                    if k >= 1:
                        norm_hidden(m * (TURN_TILES // 2) + (k - 1) // 2, (k - 1) % 2)
                    if has_ahead(m, k, 1):
                        split_u(m * (TURN_TILES // 2) + n // 2, n % 2)
                    if route:
                        if k == 0 or k == 1:
                            dve.wait_ge(copied, m * 2 + (k + 1))
                            dve.sem_inc(begun, 1)
                        if k < 3:
                            route_sets(*((0, 5), (5, 10), (10, 15))[k])
                        elif k == 3:
                            route_sets(15, 16)
                            pair_sums()
                        elif k == 4:
                            route_head(0)
                            route_head(1)
                        elif k < 11:
                            route_head(k - 3)
                        elif k == 11:
                            below_best(m)
                            look_up(0)
                        elif k == 12:
                            look_up(1)
                        else:
                            weigh(m)
                    if spreads:
                        for r in groups[k]:
                            one_hots(m, r)
                norm_hidden(m * (TURN_TILES // 2) + len(groups) // 2 - 1, 1)

            dve.wait_ge(small_in, 32)
            for e in two:
                dve.sem_inc(normed[e], 1)
            split_u(0, 0)
            turns(dve, turn)


def combine_phase(nc, name, hidden_dram, gates_dram, v_dram, x_dram, out_dram):
    QUAD = 4
    STEPS = EXPERT_TILES // QUAD
    BANKS = 8
    OUTS = 2 * KD
    ctx = Phase(nc)
    with ctx:
        def sb(what, shape, dt=F32):
            return ctx.enter_context(nc.sbuf_tensor(f"{name}_{what}", shape, dt))

        def sem(what):
            return ctx.semaphore(f"{name}_{what}")

        two = range(2)
        v_raw, hidden, gate = sb("v_raw", [P, 2, D]), sb("hidden", [P, 2, T]), sb("gate", [P, 2, T])
        v_hi, v_lo = sb("v_hi", [P, 2, QUAD, D], F32R), sb("v_lo", [P, 2, QUAD, D], F32R)
        a_hi, a_lo = sb("a_hi", [P, 2, QUAD, T], F32R), sb("a_lo", [P, 2, QUAD, T], F32R)
        total = sb("total", [P, KD, T])
        acc = ctx.enter_context(nc.psum_tensor(name + "_acc", [P, BANKS, HALF], F32))
        v_in, a_in = ([sem(f"{what}{b}") for b in two] for what in ("v_in", "a_in"))
        x_in, v_high, v_split, gated, a_high, a_split, multiplied, added, stored = (
            sem(s) for s in ("x_in", "v_high", "v_split", "gated", "a_high", "a_split", "multiplied", "added", "stored"))
        block = ctx.enter_context(nc.Block())

        @block.sync
        def _(sp):
            def load(tile, b):
                sp.dma_start(v_raw[:, b, :], v_dram[bass.ds(tile * P, P), :]).then_inc(v_in[b], 16)
                sp.dma_start(hidden[:, b, :], hidden_dram[bass.ds(tile * P, P), :]).then_inc(a_in[b], 16)
                sp.dma_start(gate[:, b, :], gates_dram[:, bass.ds(tile, 1), :].rearrange("p a t -> p (a t)")
                             ).then_inc(a_in[b], 16)

            def load_pair(i):
                for b in two:
                    sp.wait_ge(v_split, i * 2 + (b + 1))
                    sp.wait_ge(a_split, i * 2 + (b + 1))
                    load(i * 2 + (b + 2), b)

            load(0, 0)
            load(1, 1)
            load_pair(0)
            for k in range(KD):
                sp.dma_start(total[:, k, :], x_dram[k * P:(k + 1) * P, :]).then_inc(x_in, 16)
            with sp.Fori(1, EXPERT_TILES // 2 - 1) as i:
                load_pair(i)
            sp.wait_ge(added, STEPS * OUTS + BANKS)
            for k in range(KD):
                sp.dma_start(out_dram[k * P:(k + 1) * P, :], total[:, k, :]).then_inc(stored, 16)
            sp.wait_ge(stored, 16 * KD)

        @block.tensor
        def _(pe):
            def step(s, slot):
                pe.wait_ge(v_split, s * QUAD + QUAD)
                pe.wait_ge(a_split, s * QUAD + QUAD)
                for n in range(OUTS):
                    d, half = divmod(n, 2)
                    pe.wait_ge(added, s * OUTS + (n + 1))
                    for e in range(QUAD):
                        for n_pass, (w, a) in enumerate(((v_hi, a_hi), (v_hi, a_lo), (v_lo, a_hi))):
                            mm = pe.matmul(acc[:, n % BANKS, :], w[:, slot, e, d * P:(d + 1) * P],
                                           a[:, slot, e, half * HALF:(half + 1) * HALF],
                                           start=(e == 0 and n_pass == 0), stop=(e == QUAD - 1 and n_pass == 2))
                    mm.then_inc(multiplied, 1)

            def first_step():
                for n0 in range(0, OUTS, BANKS):
                    for e in range(QUAD):
                        pe.wait_ge(v_split, e + 1)
                        pe.wait_ge(a_split, e + 1)
                        for n in range(n0, n0 + BANKS):
                            d, half = divmod(n, 2)
                            if e == 0:
                                pe.wait_ge(added, n + 1)
                            for n_pass, (w, a) in enumerate(((v_hi, a_hi), (v_hi, a_lo), (v_lo, a_hi))):
                                mm = pe.matmul(acc[:, n % BANKS, :], w[:, 0, e, d * P:(d + 1) * P],
                                               a[:, 0, e, half * HALF:(half + 1) * HALF],
                                               start=(e == 0 and n_pass == 0), stop=(e == QUAD - 1 and n_pass == 2))
                            if e == QUAD - 1:
                                mm.then_inc(multiplied, 1)

            pe.sem_inc(added, BANKS)
            first_step()
            step(1, 1)
            with pe.Fori(1, STEPS // 2) as i:
                step(i * 2, 0)
                step(i * 2 + 1, 1)

        def steps(engine, prepare, add):
            for e in range(QUAD):
                prepare(0, 0, e)
            engine.wait_ge(x_in, 16 * KD)
            with engine.Fori(0, STEPS // 2 - 1) as i:
                for half in two:
                    for e in range(QUAD):
                        prepare(i * 2 + (half + 1), 1 - half, e)
                        add(i * 2 + half, e)
            for e in range(QUAD):
                prepare(STEPS - 1, 1, e)
                add(STEPS - 2, e)
            for e in range(QUAD):
                add(STEPS - 1, e)

        @block.scalar
        def _(act):
            def prepare(s, slot, e):
                b, use = e % 2, s * 2 + e // 2
                act.wait_ge(v_in[b], use * 16 + 16)
                if not isinstance(s, int) or s >= 2:
                    act.wait_ge(multiplied, s * OUTS - OUTS)
                act.activation(v_hi[:, slot, e, :], v_raw[:, b, :], ACT.Copy).then_inc(v_high, 1)
                act.wait_ge(gated, s * QUAD + (e + 1))
                act.activation(a_hi[:, slot, e, :], hidden[:, b, :], ACT.Copy).then_inc(a_high, 1)

            for e in range(QUAD):
                prepare(0, 0, e)
            for e in range(QUAD):
                prepare(1, 1, e)
            with act.Fori(1, STEPS // 2) as i:
                for half in two:
                    for e in range(QUAD):
                        prepare(i * 2 + half, half, e)

        @block.vector
        def _(dve):
            def prepare(s, slot, e):
                b, use = e % 2, s * 2 + e // 2
                dve.wait_ge(a_in[b], use * 32 + 32)
                dve.tensor_tensor(hidden[:, b, :], hidden[:, b, :], gate[:, b, :], ALU.mult).then_inc(gated, 1)
                dve.wait_ge(v_high, s * QUAD + (e + 1))
                dve.tensor_tensor(v_lo[:, slot, e, :], v_raw[:, b, :], v_hi[:, slot, e, :].bitcast(F32),
                                  ALU.subtract).then_inc(v_split, 1)
                dve.wait_ge(a_high, s * QUAD + (e + 1))
                dve.tensor_tensor(a_lo[:, slot, e, :], hidden[:, b, :], a_hi[:, slot, e, :].bitcast(F32),
                                  ALU.subtract).then_inc(a_split, 1)

            def add(s, quarter):
                for n in range(4 * quarter, 4 * quarter + 4):
                    d, half = divmod(n, 2)
                    at = slice(half * HALF, (half + 1) * HALF)
                    dve.wait_ge(multiplied, s * OUTS + (n + 1))
                    dve.tensor_tensor(total[:, d, at], total[:, d, at], acc[:, n % BANKS, :], ALU.add).then_inc(added, 1)

            steps(dve, prepare, add)


def shape_constants():
    c = {}
    c["identity"] = np.eye(P, dtype=np.float32)
    c["flip"] = np.ascontiguousarray(c["identity"][::-1])
    p = np.arange(P)
    pick = (np.arange(32)[None, None, :] == 2 * np.arange(16)[None, :, None] + (p // 64)[:, None, None])
    c["head_pick"] = pick.astype(np.float32).reshape(P, 16 * 32)
    c["head_spread"] = np.ascontiguousarray(pick.transpose(2, 1, 0)).astype(np.float32).reshape(32, 16 * P)
    rel = np.arange(REL_COUNT) - (REL_COUNT - P)
    near = np.abs(rel)
    far = 8 + sum((rel * rel >= 64 * 2 ** q).astype(np.int64) for q in range(1, 8))
    bucket = np.where(rel > 0, 16, 0) + np.where(near < 8, near, far)
    c["bucket_onehot"] = (np.arange(32)[:, None] == bucket[None, :]).astype(np.float32)
    age = np.arange(BLOCK_KEYS)[None, :] // 64 - (p // 64)[:, None]
    c["band_mask"] = np.where((age == 0) | (age == 1), 0.0, NEGATIVE).astype(np.float32)
    c["causal_mask"] = np.where(p[:, None] <= p[None, :], 0.0, NEGATIVE).astype(np.float32)
    c["count"] = np.broadcast_to(np.arange(P, dtype=np.float32), (P, P)).copy()
    return c


NEGATIVE = -1e30


class Constants:

    def __init__(self, nc, ctx, arrays):
        def sb(what, shape, dt=F32):
            return ctx.enter_context(nc.sbuf_tensor("const_" + what, shape, dt))

        identity, ones = sb("identity", [P, P]), sb("ones", [P, P])
        loaded = ctx.enter_context(nc.semaphore("const_loaded"))
        with nc.Block() as block:
            @block.sync
            def _(sp):
                sp.dma_start(identity[:], arrays["identity"]).then_inc(loaded, 16)
                sp.wait_ge(loaded, 16)

            @block.vector
            def _(dve):
                dve.memset(ones[:], 1.0)
        self.identity, self.ones = identity[:], ones[:]

    def load_heads(self, nc, ctx, arrays):
        pick = ctx.enter_context(nc.sbuf_tensor("const_head_pick", [P, 16, 32], F32))
        spread = ctx.enter_context(nc.sbuf_tensor("const_head_spread", [32, 16, P], F32))
        loaded = ctx.semaphore("const_heads_loaded")
        with nc.Block() as block:
            @block.sync
            def _(sp):
                sp.dma_start(pick[:], arrays["head_pick"]).then_inc(loaded, 16)
                sp.dma_start(spread[:], arrays["head_spread"]).then_inc(loaded, 16)
                sp.wait_ge(loaded, 32)
        self.head_pick, self.head_spread = pick[:], spread[:]


IN_SEGMENTS = [(CONV_TILES, "conv"), (45, "copy")]
GATE_ATT_ROWS, GATE_SSM_ROWS = 6656, 7680


def build_layer(nc, a, out):
    def scratch(what, rows, cols=T):
        return nc.dram_tensor("scratch_" + what, (rows, cols), F32, kind="Internal").ap()

    proj = scratch("proj", (CONV_TILES + 45) * P)
    rel_row = scratch("rel_row", Q_HEADS, REL_COUNT)
    att, ssm = scratch("att", 1024), scratch("ssm", 2048)
    mixed_ssm, mixed = scratch("mixed_ssm", D), scratch("mixed", D)
    x1, x2, query, ple = scratch("x1", D), scratch("x2", D), scratch("query", 2048), scratch("ple", D)
    hidden = scratch("hidden", EXPERT_TILES * P)
    gates = nc.dram_tensor("scratch_gates", (KEYS, KEYS, T), F32, kind="Internal").ap()
    ctx = ExitStack()
    with ctx:
        const = Constants(nc, ctx, a)

        with ExitStack() as scope:
            h = Activations(nc, scope, "h_mix", KD, a["x"], a["norm_mix_g"])
            linear_phase(nc, "in_proj", h, a["w_in"], IN_SEGMENTS, proj, const=const, taps_dram=a["conv"])
        with Phase(nc) as scope:
            const.load_heads(nc, scope, a)
            attention_phase(nc, "attention", proj, a["qk_norm_g"], a["attn_sinks"], a["rel_bias"], a["bucket_onehot"],
                            a["band_mask"], a["flip"], rel_row, att, const)
        ssm_phase(nc, "ssm", proj, a["head_par"], a["tile_par"], a["causal_mask"], a["head_spread"], ssm, const)
        with ExitStack() as scope:
            y = Activations(nc, scope, "y_ssm", SSM_TILES, ssm)
            linear_phase(nc, "o_ssm", y, a["w_o_ssm"], [(KD, "gate")], mixed_ssm, proj[GATE_SSM_ROWS:GATE_SSM_ROWS + D, :])
        with ExitStack() as scope:
            o = Activations(nc, scope, "o_att", KD, att)
            linear_phase(nc, "o_att", o, a["w_o_attn"], [(KD, "gate_add")], mixed,
                         proj[GATE_ATT_ROWS:GATE_ATT_ROWS + D, :], mixed_ssm)
        with ExitStack() as scope:
            m = Activations(nc, scope, "mixed", KD, mixed)
            linear_phase(nc, "out_proj", m, a["w_out"], [(KD, "add")], x1, a["x"])
        with ExitStack() as scope:
            h = Activations(nc, scope, "h_ffn", KD, x1, a["norm_ffn_g"])
            linear_phase(nc, "query", h, a["w_peer_q"], [(SCORE_SETS, "copy")], query, const=const)
            select_phase(nc, "select", h, a["peer_u"], hidden, query, a["peer_keys"], a["count"], gates, const)
        combine_phase(nc, "combine", hidden, gates, a["peer_v"], x1, x2)
        with ExitStack() as scope:
            e = Activations(nc, scope, "embedding", 2, a["p"])
            linear_phase(nc, "ple", e, a["w_ple"], [(KD, "copy")], ple)
        with ExitStack() as scope:
            h = Activations(nc, scope, "h_ple", KD, x2, a["norm_ple_g"])
            linear_phase(nc, "ple_gate", h, a["w_ple_gate"], [(KD, "final")], out, ple, x2, const)


def weight_tiles(w):
    k, n = w.shape[0] // P, w.shape[1] // P
    return w.reshape(k, P, n, P).transpose(2, 1, 0, 3).reshape(n * P, k * P)


def per_partition(*rows):
    stacked = np.stack([r.reshape(-1, P).T for r in rows], axis=-1)
    return stacked[:, :, 0] if len(rows) == 1 else stacked


def kernel(**inputs):
    import concourse.bacc as bacc
    from concourse.bass_utils import run_bass_kernel_spmd

    i = {k: np.asarray(v) for k, v in inputs.items()}
    one = {k: v[0] for k, v in i.items()}
    w_in = one["w_in"]
    xbc_at = 1024 + 256 + 256 + 2048
    dt_at = xbc_at + 3072
    order = np.arange(Q_HEADS).reshape(KV_HEADS, 4)[:, list(HEAD_ORDER)].reshape(-1)
    w_dt = np.zeros((D, P), w_in.dtype)
    w_dt[:, :SSM_HEADS] = w_in[:, dt_at:dt_at + SSM_HEADS]
    arrays = {
        "x": one["x"].T,
        "p": one["p"][0].T,
        "norm_mix_g": per_partition(one["norm_mix_g"]),
        "norm_ffn_g": per_partition(one["norm_ffn_g"]),
        "norm_ple_g": per_partition(one["norm_ple_g"]),
        "w_in": weight_tiles(np.concatenate([w_in[:, xbc_at:dt_at], w_in[:, :xbc_at], w_in[:, dt_at + SSM_HEADS:], w_dt],
                                            axis=1)),
        "qk_norm_g": np.stack([np.tile(one["q_norm_g"], 2), np.tile(one["k_norm_g"], 2)], axis=1),
        "attn_sinks": one["attn_sinks"][order],
        "rel_bias": i["rel_bias"][:, order],
        "conv": per_partition(*one["conv_w"], one["conv_b"]),
        "head_par": np.stack([one["dt_bias"], one["a_log"]], axis=1),
        "tile_par": per_partition(np.repeat(one["d_skip"], 64), one["ssm_norm_g"]),
        "w_o_attn": weight_tiles(one["w_o_attn"]),
        "w_o_ssm": weight_tiles(one["w_o_ssm"]),
        "w_out": weight_tiles(one["w_out"]),
        "w_peer_q": weight_tiles(one["w_peer_q"]),
        "peer_keys": one["peer_sub_keys"].reshape(SCORE_SETS, KEYS, P).transpose(2, 0, 1),
        "peer_u": weight_tiles(one["peer_u"].T),
        "peer_v": one["peer_v"],
        "w_ple_gate": weight_tiles(one["w_ple_gate"]),
        "w_ple": weight_tiles(one["w_ple"]),
        **shape_constants(),
    }
    arrays = {k: np.ascontiguousarray(v) for k, v in arrays.items()}
    nc = bacc.Bacc("TRN2", target_bir_lowering=False, num_devices=1)
    aps = {k: nc.dram_tensor("in_" + k, v.shape, mybir.dt.from_np(v.dtype), kind="ExternalInput").ap()
           for k, v in arrays.items()}
    out = nc.dram_tensor("out", (D, T), F32, kind="ExternalOutput").ap()
    build_layer(nc, aps, out)
    r = run_bass_kernel_spmd(nc, [{"in_" + k: v for k, v in arrays.items()}], core_ids=[0])
    return np.ascontiguousarray(r.results[0]["out"].T)[None]
```

```python
import concourse.bass as bass
from concourse import mybir
from contextlib import ExitStack
import numpy as np

F32 = mybir.dt.float32
F32R = mybir.dt.float32r
BF16 = mybir.dt.bfloat16
U32 = mybir.dt.uint32
ACT = mybir.ActivationFunctionType
ALU = mybir.AluOpType
AX = mybir.AxisListType

P = 128
T = 1024
HALF = 512
D = 1024
KD = D // P
EPS = 1e-6


class Phase(ExitStack):

    def __init__(self, nc):
        super().__init__()
        self.nc, self.semaphores = nc, []

    def semaphore(self, name):
        self.semaphores.append(self.nc.alloc_semaphore(name))
        return self.semaphores[-1]

    def __exit__(self, *failure):
        super().__exit__(*failure)
        if failure[0] is None:
            self.nc.clear_and_free_semaphores(self.semaphores)
            self.nc.all_engine_barrier()




Q_HEADS, KV_HEADS, HEAD_DIM = 16, 4, 64
Q_ROWS, V_ROWS = 3072, 4352
HEAD_ORDER = (0, 2, 1, 3)
BLOCK_KEYS = 192
BAND = 256
REL_COUNT = BLOCK_KEYS + P - 1
NORMED = (Q_HEADS + KV_HEADS) // 2


def attention_phase(nc, name, proj, qk_gain_dram, sink_dram, rel_bias_dram, onehot_dram, band_mask_dram,
                    flip_dram, rel_row_dram, out, const):
    ctx = Phase(nc)
    with ctx:
        def sb(what, shape, dt=F32):
            return ctx.enter_context(nc.sbuf_tensor(f"{name}_{what}", shape, dt))

        def sem(what):
            return ctx.semaphore(f"{name}_{what}")

        qk = sb("qk", [P, NORMED, T])
        k_swap = sb("k_swap", [P, 2, T])
        v_t = sb("v_t", [P, 2, T])
        v = sb("v", [P, KD, KV_HEADS * HEAD_DIM])
        gain = sb("gain", [P, 2])
        square = sb("square", [P, 2, T])
        rstd = sb("rstd", [32, 3, T])
        bias = sb("bias", [P, Q_HEADS, BLOCK_KEYS])
        mask = sb("mask", [P, BLOCK_KEYS])
        onehot = sb("onehot", [32, REL_COUNT])
        rel_bias = sb("rel_bias", [32, Q_HEADS])
        rel_row = sb("rel_row", [Q_HEADS, REL_COUNT])
        sink = sb("sink", [P, Q_HEADS])
        score = sb("score", [P, 2, 4, BLOCK_KEYS])
        prob = sb("prob", [P, 2, 4, BAND])
        prob_t = sb("prob_t", [P, 2, 2, 4, P])
        top = sb("top", [P, 2, 4])
        neg_top = sb("neg_top", [P, 2, 4])
        sink_gap = sb("sink_gap", [P, 2, 4])
        sink_exp = sb("sink_exp", [P, 2, 4])
        denom = sb("denom", [P, 2, 4])
        inverse = sb("inverse", [P, 2, 4])

        qk_in = [sem(f"qk_in{k}") for k in range(NORMED)]
        v_in, small_in, swapped, rel_in = (sem(s) for s in ("v_in", "small_in", "swapped", "rel_in"))
        squared, summed, rooting, rooted, spread, normed = (
            sem(s) for s in ("squared", "summed", "rooting", "rooted", "spread", "normed"))
        v_turned, v_ready, row_made, row_ready, row_stored, flipped, bias_ready, zeroed = (
            sem(s) for s in ("v_turned", "v_ready", "row_made", "row_ready", "row_stored", "flipped", "bias_ready", "zeroed"))

        with ExitStack() as first:
            norm_acc = first.enter_context(nc.psum_tensor(name + "_norm_acc", [P, 2, 2, HALF], F32))
            turn_acc = first.enter_context(nc.psum_tensor(name + "_turn_acc", [P, 2, HALF], F32))
            bias_rev = first.enter_context(nc.sbuf_tensor(name + "_bias_rev", [P, Q_HEADS, BLOCK_KEYS], F32))
            flip = first.enter_context(nc.sbuf_tensor(name + "_flip", [P, P], F32))
            row_acc = first.enter_context(nc.psum_tensor(name + "_row_acc", [P, HALF], F32))
            block = first.enter_context(nc.Block())

            @block.sync
            def _(sp):
                for dst, src in ((gain[:], qk_gain_dram), (rel_bias[:], rel_bias_dram), (onehot[:], onehot_dram),
                                 (mask[:], band_mask_dram), (flip[:], flip_dram)):
                    sp.dma_start(dst, src).then_inc(small_in, 16)
                sp.dma_start(sink[:], sink_dram.partition_broadcast(P)).then_inc(small_in, 16)
                for k in range(2):
                    sp.dma_start(v_t[:, k, :], proj[V_ROWS + k * P:V_ROWS + (k + 1) * P, :]).then_inc(v_in, 16)
                for k in range(NORMED):
                    sp.dma_start(qk[:, k, :], proj[Q_ROWS + k * P:Q_ROWS + (k + 1) * P, :]).then_inc(qk_in[k], 16)
                sp.wait_ge(row_ready, 1)
                sp.dma_start(rel_row_dram, rel_row[:]).then_inc(row_stored, 16)
                sp.wait_ge(row_stored, 16)
                toeplitz = bass.AP(rel_row_dram.tensor, 0, [[1, P], [REL_COUNT, Q_HEADS], [1, BLOCK_KEYS]])
                sp.dma_start(bias_rev[:], toeplitz).then_inc(rel_in, 16)
                sp.wait_ge(normed, NORMED)
                for k in range(2):
                    for s in range(2):
                        sp.dma_start(k_swap[64 * s:64 * s + 64, k, :],
                                     qk[64 - 64 * s:128 - 64 * s, 8 + k, :]).then_inc(swapped, 16)
                sp.wait_ge(swapped, 64)

            @block.scalar
            def _(act):
                for k in range(NORMED):
                    act.wait_ge(qk_in[k], 16)
                    if k >= 2:
                        act.wait_ge(summed, k - 1)
                    act.activation(square[:, k % 2, :], qk[:, k, :], ACT.Square).then_inc(squared, 1)
                act.wait_ge(rooting, 2)
                act.activation(rstd[:, 0, :], rstd[:, 1, :], ACT.Sqrt).then_inc(rooted, 1)

            @block.tensor
            def _(pe):
                pe.wait_ge(small_in, 96)
                pe.matmul(row_acc[:Q_HEADS, :REL_COUNT], rel_bias[:], onehot[:], start=True, stop=True).then_inc(row_made, 1)
                pe.wait_ge(v_in, 32)
                for m in range(KD):
                    if m >= 2:
                        pe.wait_ge(v_ready, m - 1)
                    for k in range(2):
                        mm = pe.transpose(turn_acc[:, m % 2, k * P:(k + 1) * P], v_t[:, k, m * P:(m + 1) * P],
                                          const.identity)
                    mm.then_inc(v_turned, 1)
                for k in range(NORMED):
                    pe.wait_ge(squared, k + 1)
                    for half in range(2):
                        mm = pe.matmul(norm_acc[:32, 0, half, :], const.head_pick[:, k, :],
                                       square[:, k % 2, half * HALF:(half + 1) * HALF],
                                       start=(k == 0), stop=(k == NORMED - 1))
                    mm.then_inc(summed, 1)
                pe.wait_ge(rooting, 6)
                for k in range(NORMED):
                    if k >= 2:
                        pe.wait_ge(normed, k - 1)
                    for half in range(2):
                        mm = pe.matmul(norm_acc[:, k % 2, half, :], const.head_spread[:, k, :],
                                       rstd[:, 0, half * HALF:(half + 1) * HALF], start=True, stop=True)
                    mm.then_inc(spread, 1)
                pe.wait_ge(rel_in, 16)
                for n in range(Q_HEADS // 2):
                    pe.wait_ge(v_ready, KD)
                    if n >= 2:
                        pe.wait_ge(bias_ready, n - 1)
                    pe.matmul(turn_acc[:, n % 2, :2 * BLOCK_KEYS], flip[:],
                              bias_rev[:, 2 * n:2 * n + 2, :].rearrange("p a b -> p (a b)"),
                              start=True, stop=True).then_inc(flipped, 1)

            @block.vector
            def _(dve):
                dve.wait_ge(row_made, 1)
                dve.tensor_copy(rel_row[:], row_acc[:Q_HEADS, :REL_COUNT]).then_inc(row_ready, 1)
                for m in range(KD):
                    dve.wait_ge(v_turned, m + 1)
                    dve.tensor_copy(v[:, m, :], turn_acc[:, m % 2, :2 * P]).then_inc(v_ready, 1)
                dve.memset(prob[:, :, :, 0:64], 0.0).then_inc(zeroed, 1)
                dve.wait_ge(summed, NORMED)
                mean, root, aux = rstd[:, 2, :], rstd[:, 0, :], rstd[:, 1, :]
                dve.tensor_scalar(mean, norm_acc[:32, 0, :, :].rearrange("p a b -> p (a b)"), 1.0 / HEAD_DIM, EPS,
                                  ALU.mult, ALU.add).then_inc(rooting, 1)
                dve.wait_ge(rooting, 1)
                dve.reciprocal(aux, mean).then_inc(rooting, 1)
                dve.wait_ge(rooted, 1)
                dve.tensor_tensor(aux, root, root, ALU.mult).then_inc(rooting, 1)
                dve.wait_ge(rooting, 3)
                dve.tensor_tensor(aux, aux, mean, ALU.mult).then_inc(rooting, 1)
                dve.wait_ge(rooting, 4)
                dve.tensor_scalar(aux, aux, -0.5, 1.5, ALU.mult, ALU.add).then_inc(rooting, 1)
                dve.wait_ge(rooting, 5)
                dve.tensor_tensor(root, root, aux, ALU.mult).then_inc(rooting, 1)
                for k in range(NORMED):
                    dve.wait_ge(spread, k + 1)
                    g = gain[:, 0:1] if k < 8 else gain[:, 1:2]
                    dve.scalar_tensor_tensor(out=qk[:, k, :], in0=qk[:, k, :], scalar=g,
                                             in1=norm_acc[:, k % 2, :, :].rearrange("p a b -> p (a b)"),
                                             op0=ALU.mult, op1=ALU.mult).then_inc(normed, 1)
                dve.wait_ge(small_in, 96)
                for n in range(Q_HEADS // 2):
                    dve.wait_ge(flipped, n + 1)
                    dve.tensor_tensor(bias[:, 2 * n:2 * n + 2, :],
                                      turn_acc[:, n % 2, :2 * BLOCK_KEYS].rearrange("p (a b) -> p a b", a=2),
                                      mask[:].unsqueeze(1).to_broadcast([P, 2, BLOCK_KEYS]), ALU.add).then_inc(bias_ready, 1)

        scores_made, scaled, topped, exped, probs_ready, turned, probs_turned, summed_up, out_ready, chain = (
            sem(s) for s in ("scores_made", "scaled", "topped", "exped", "probs_ready", "turned", "probs_turned",
                             "summed_up", "out_ready", "chain"))
        STEPS = KD * KV_HEADS
        with ExitStack() as second:
            s_acc = second.enter_context(nc.psum_tensor(name + "_s_acc", [P, 2, 4, 256], F32))
            t_acc = second.enter_context(nc.psum_tensor(name + "_t_acc", [P, 2, 4, P], F32))
            o_acc = second.enter_context(nc.psum_tensor(name + "_o_acc", [P, 2, 4, P], F32))
            block = second.enter_context(nc.Block())

            def reach(m):
                return 64 if m == 0 else 0

            @block.tensor
            def _(pe):
                def scores(s):
                    m, kv = divmod(s, KV_HEADS)
                    first_key = m * P - 64 + reach(m)
                    if s >= 2:
                        pe.wait_ge(scaled, s - 1)
                    for h in range(4):
                        head = 4 * kv + HEAD_ORDER[h]
                        at = 64 * (head % 2)
                        keys = qk[:, 8 + kv // 2, :] if kv % 2 == head % 2 else k_swap[:, kv // 2, :]
                        mm = pe.matmul(s_acc[:, s % 2, h, reach(m):BLOCK_KEYS],
                                       qk[at:at + 64, head // 2, m * P:(m + 1) * P],
                                       keys[at:at + 64, first_key:(m + 1) * P], start=True, stop=True)
                    mm.then_inc(scores_made, 1)

                def halves(s):
                    return (1,) if s < KV_HEADS else (0, 1)

                def turn(s):
                    pe.wait_ge(probs_ready, s + 1)
                    if s >= 1:
                        pe.wait_ge(probs_turned, s)
                    for half in halves(s):
                        for h in range(4):
                            mm = pe.transpose(t_acc[:, half, h, :], prob[:, s % 2, h, half * P:(half + 1) * P],
                                              const.identity)
                    mm.then_inc(turned, 1)

                def sum_up(s):
                    m, kv = divmod(s, KV_HEADS)
                    pe.wait_ge(probs_turned, s + 1)
                    if s >= 2:
                        pe.wait_ge(out_ready, s - 1)
                    for parity in range(2):
                        for n, half in enumerate(halves(s)):
                            mm = pe.matmul(o_acc[64 * parity:64 * parity + 64, s % 2, 0:2, :],
                                           v[:, m - 1 + half, kv * HEAD_DIM:(kv + 1) * HEAD_DIM],
                                           prob_t[:, s % 2, half, 2 * parity:2 * parity + 2, :],
                                           start=(n == 0), stop=(n == len(halves(s)) - 1))
                    mm.then_inc(summed_up, 1)

                scores(0)
                scores(1)
                for s in range(STEPS):
                    turn(s)
                    if s + 2 < STEPS:
                        scores(s + 2)
                    if s >= 1:
                        sum_up(s - 1)
                sum_up(STEPS - 1)

            @block.scalar
            def _(act):
                def exps(s):
                    m, kv = divmod(s, KV_HEADS)
                    lo = reach(m)
                    act.wait_ge(topped, s + 1)
                    if s >= 2:
                        act.wait_ge(turned, s - 1)
                        act.wait_ge(probs_ready, s - 1)
                    for h in range(4):
                        act.activation(prob[:, s % 2, h, 64 + lo:BAND], score[:, s % 2, h, lo:], ACT.Exp,
                                       bias=neg_top[:, s % 2, h:h + 1], accum_out=denom[:, s % 2, h:h + 1])
                    act.activation(sink_exp[:, s % 2, :], sink_gap[:, s % 2, :], ACT.Exp).then_inc(exped, 1)

                exps(0)
                exps(1)
                for s in range(STEPS):
                    half = slice(1, 2) if s < KV_HEADS else slice(0, 2)
                    act.wait_ge(turned, s + 1)
                    if s >= 2:
                        act.wait_ge(summed_up, s - 1)
                    act.activation(prob_t[:, s % 2, half, :, :], t_acc[:, half, :, :], ACT.Copy).then_inc(probs_turned, 1)
                    if s + 2 < STEPS:
                        exps(s + 2)

            @block.vector
            def _(dve):
                links = [0]

                def link(instruction):
                    links[0] += 1
                    instruction.then_inc(chain, 1)
                    dve.wait_ge(chain, links[0])

                def tops(s):
                    m, kv = divmod(s, KV_HEADS)
                    b, lo, heads = s % 2, reach(m), slice(4 * kv, 4 * kv + 4)
                    dve.wait_ge(scores_made, s + 1)
                    if s >= 2:
                        dve.wait_ge(exped, s - 1)
                    ins = dve.scalar_tensor_tensor(out=score[:, b, :, lo:], in0=s_acc[:, b, :, lo:BLOCK_KEYS],
                                                   scalar=HEAD_DIM ** -0.5, in1=bias[:, heads, lo:],
                                                   op0=ALU.mult, op1=ALU.add)
                    ins.then_inc(scaled, 1)
                    dve.wait_ge(scaled, s + 1)
                    link(dve.tensor_reduce(top[:, b, :], score[:, b, :, lo:], AX.X, ALU.max))
                    link(dve.tensor_tensor(top[:, b, :], top[:, b, :], sink[:, heads], ALU.max))
                    dve.tensor_scalar(neg_top[:, b, :], top[:, b, :], -1.0, None, ALU.mult)
                    dve.tensor_tensor(sink_gap[:, b, :], sink[:, heads], top[:, b, :], ALU.subtract).then_inc(topped, 1)

                def normalise(s):
                    b = s % 2
                    dve.wait_ge(exped, s + 1)
                    link(dve.tensor_tensor(denom[:, b, :], denom[:, b, :], sink_exp[:, b, :], ALU.add))
                    link(dve.reciprocal(inverse[:, b, :], denom[:, b, :]))
                    lo = 64 + reach(s // KV_HEADS)
                    dve.tensor_tensor(prob[:, b, :, lo:], prob[:, b, :, lo:],
                                      inverse[:, b, :].unsqueeze(2).to_broadcast([P, 4, BAND - lo]),
                                      ALU.mult).then_inc(probs_ready, 1)

                def drain(s):
                    m, kv = divmod(s, KV_HEADS)
                    dve.wait_ge(summed_up, s + 1)
                    dve.tensor_copy(out[:, 2 * kv:2 * kv + 2, m * P:(m + 1) * P], o_acc[:, s % 2, 0:2, :]).then_inc(out_ready, 1)

                tops(0)
                tops(1)
                normalise(0)
                for s in range(STEPS):
                    if s + 1 < STEPS:
                        normalise(s + 1)
                    if s + 2 < STEPS:
                        tops(s + 2)
                    if s >= 2:
                        drain(s - 2)
                drain(STEPS - 2)
                drain(STEPS - 1)


SSM_TILES = 16
SSM_HEADS = 32
GROUPS = 4
CHUNKS = T // P
CONV_TILES = 24
TAPS = 4
XBC_ROWS, Z_ROWS, DT_ROWS = 0, 4608, 8704
XS_BUFFERS = 3


def ssm_phase(nc, name, proj, head_dram, tile_dram, causal_dram, spread_dram, out_dram, const):
    ctx = Phase(nc)
    with ctx:
        def sb(what, shape, dt=F32):
            return ctx.enter_context(nc.sbuf_tensor(f"{name}_{what}", shape, dt))

        def sem(what):
            return ctx.semaphore(f"{name}_{what}")

        b_c = sb("b_c", [P, 2 * GROUPS, T])
        a_hi, a_lo = sb("a_hi", [32, T], F32R), sb("a_lo", [32, T], F32R)
        spread = sb("spread", [32, SSM_TILES, P], F32R)
        neg_a = sb("neg_a", [P, CHUNKS, SSM_HEADS])
        dt = sb("dt", [P, CHUNKS, SSM_HEADS])
        dt_out = sb("dt_out", [P, CHUNKS, SSM_HEADS])
        decay = sb("decay", [P, CHUNKS, SSM_HEADS])
        tile_par = sb("tile_par", [P, SSM_TILES, 2])
        identity16 = sb("identity16", [P, P], BF16)
        causal16 = sb("causal16", [P, 4, P], BF16)
        b_nat = sb("b_nat", [P, CHUNKS, GROUPS, P])
        cb = sb("cb", [P, GROUPS, T])

        with ExitStack() as first:
            def fsb(what, shape, dt=F32):
                return first.enter_context(nc.sbuf_tensor(f"{name}_{what}", shape, dt))

            head = fsb("head", [32, 2])
            rate = fsb("rate", [32, 1])
            raw = fsb("dt_raw", [32, T])
            one = fsb("one", [32, P])
            a_t = fsb("a_t", [32, T])
            work = [fsb(f"work{k}", [32, T]) for k in range(6)]
            spread_decay = fsb("spread_decay", [32, CHUNKS, 32])
            causal = fsb("causal", [P, P])
            spread_in = fsb("spread_in", [32, SSM_TILES, P])
            turn = first.enter_context(nc.psum_tensor(name + "_b_acc", [P, 2, GROUPS, P], F32))
            dots = first.enter_context(nc.psum_tensor(name + "_cb_acc", [P, 2, HALF], F32))
            t_acc = first.enter_context(nc.psum_tensor(name + "_turn_acc", [P, 3, HALF], F32))
            d_acc = first.enter_context(nc.psum_tensor(name + "_decay_acc", [P, HALF], F32))
            small_in, pick_in, dt_in, b_in, c_in, chain, acted, turned, b_turned, b_read, dotted, dots_read, a_high = (
                sem(s) for s in ("small_in", "pick_in", "dt_in", "b_in", "c_in", "chain", "acted", "turned", "b_turned",
                                 "b_read", "dotted", "dots_read", "a_high"))
            block = first.enter_context(nc.Block())

            @block.sync
            def _(sp):
                sp.dma_start(raw[:], proj[DT_ROWS:DT_ROWS + 32, :]).then_inc(dt_in, 16)
                for dst, src in ((head[:], head_dram), (tile_par[:], tile_dram), (causal[:], causal_dram)):
                    sp.dma_start(dst, src).then_inc(small_in, 16)
                for g in range(2 * GROUPS):
                    at = XBC_ROWS + (SSM_TILES + g) * P
                    sp.dma_start(b_c[:, g, :], proj[at:at + P, :]).then_inc(b_in if g < GROUPS else c_in, 16)
                sp.dma_start(spread_in[:], spread_dram).then_inc(pick_in, 16)

            @block.scalar
            def _(act):
                act.wait_ge(chain, 2)
                act.activation(work[1][:], work[1][:], ACT.Exp, scale=-1.0).then_inc(acted, 1)
                act.wait_ge(small_in, 48)
                act.activation(rate[:], head[:, 1:2], ACT.Exp).then_inc(acted, 1)
                act.wait_ge(chain, 3)
                act.activation(work[3][:], work[2][:], ACT.Ln).then_inc(acted, 1)
                for c in range(CHUNKS):
                    act.wait_ge(b_turned, c + 1)
                    act.activation(b_nat[:, c, :, :], turn[:, c % 2, :, :], ACT.Copy).then_inc(b_read, 1)
                    act.wait_ge(dotted, c + 1)
                    act.activation(cb[:, :, c * P:(c + 1) * P], dots[:, c % 2, :].rearrange("p (g t) -> p g t", g=GROUPS),
                                   ACT.Copy).then_inc(dots_read, 1)
                act.wait_ge(chain, 13 + CHUNKS + 1)
                act.activation(work[0][:], work[0][:], ACT.Exp, scale=-1.0).then_inc(acted, 1)
                act.activation(work[2][:, 0:CHUNKS], a_t[:, P - 1::P], ACT.Exp).then_inc(acted, 1)
                act.activation(a_hi[:], a_t[:], ACT.Copy).then_inc(a_high, 1)
                act.wait_ge(pick_in, 16)
                act.activation(spread[:], spread_in[:], ACT.Copy)

            @block.tensor
            def _(pe):
                pe.wait_ge(b_in, 16 * GROUPS)
                for c in range(CHUNKS):
                    at = slice(c * P, (c + 1) * P)
                    if c >= 2:
                        pe.wait_ge(b_read, c - 1)
                        pe.wait_ge(dots_read, c - 1)
                    for g in range(GROUPS):
                        mm = pe.transpose(turn[:, c % 2, g, :], b_c[:, g, at], const.identity)
                    mm.then_inc(b_turned, 1)
                    if c == 0:
                        pe.wait_ge(c_in, 16 * GROUPS)
                    for g in range(GROUPS):
                        mm = pe.matmul(dots[:, c % 2, g * P:(g + 1) * P], b_c[:, g, at], b_c[:, GROUPS + g, at],
                                       start=True, stop=True)
                    mm.then_inc(dotted, 1)
                pe.wait_ge(chain, 13 + CHUNKS + 2)
                for j, src in enumerate((a_t, work[5], work[0])):
                    for c in range(CHUNKS):
                        mm = pe.transpose(t_acc[:, j, c * 32:(c + 1) * 32], src[:, c * P:(c + 1) * P],
                                          const.identity[0:32, 0:32])
                mm.then_inc(turned, 1)
                pe.wait_ge(chain, 13 + CHUNKS + 3)
                pe.matmul(d_acc[:, 0:256], const.ones[0:32, :], spread_decay[:, :, :].rearrange("p a b -> p (a b)"),
                          start=True, stop=True).then_inc(turned, 1)

            @block.vector
            def _(dve):
                links = [0]

                def link(instruction):
                    links[0] += 1
                    instruction.then_inc(chain, 1)
                    dve.wait_ge(chain, links[0])

                x, e, u, log, w4, dt_t = (w[:] for w in work)
                dve.memset(one[:], 1.0)
                dve.wait_ge(small_in, 48)
                dve.wait_ge(dt_in, 16)
                link(dve.tensor_scalar(x, raw[:], head[:, 0:1], None, ALU.add))
                link(dve.scalar_tensor_tensor(out=e, in0=x, scalar=-1.0, in1=x, op0=ALU.mult, op1=ALU.max))
                dve.wait_ge(acted, 1)
                link(dve.tensor_scalar(u, e, 1.0, None, ALU.add))
                link(dve.tensor_scalar(w4, u, -1.0, None, ALU.add))
                link(dve.tensor_scalar(dt_t, w4, 0.0, None, ALU.is_equal))
                link(dve.tensor_tensor(w4, w4, dt_t, ALU.add))
                link(dve.tensor_tensor(dt_t, dt_t, e, ALU.mult))
                dve.wait_ge(acted, 3)
                link(dve.tensor_tensor(e, log, e, ALU.mult))
                link(dve.reciprocal(log, w4))
                link(dve.tensor_tensor(e, e, log, ALU.mult))
                link(dve.tensor_tensor(dt_t, dt_t, e, ALU.add))
                link(dve.scalar_tensor_tensor(out=dt_t, in0=x, scalar=0.0, in1=dt_t, op0=ALU.max, op1=ALU.add))
                link(dve.tensor_scalar(x, dt_t, rate[:, 0:1], -1.0, ALU.mult, ALU.mult))
                for c in range(CHUNKS):
                    at = slice(c * P, (c + 1) * P)
                    link(dve.tensor_tensor_scan(out=a_t[:, at], data0=one[:], data1=x[:, at], initial=0.0,
                                                op0=ALU.mult, op1=ALU.add))
                a3 = a_t[:].rearrange("p (c t) -> p c t", c=CHUNKS)
                link(dve.tensor_tensor(x.rearrange("p (c t) -> p c t", c=CHUNKS), a3,
                                       a3[:, :, P - 1:P].to_broadcast([32, CHUNKS, P]), ALU.subtract))
                dve.wait_ge(acted, 5)
                link(dve.tensor_tensor(x, x, dt_t, ALU.mult))
                link(dve.tensor_tensor(spread_decay[:], work[2][:, 0:CHUNKS].unsqueeze(2).to_broadcast([32, CHUNKS, 32]),
                                       const.identity[0:32, 0:32].unsqueeze(1).to_broadcast([32, CHUNKS, 32]), ALU.mult))
                dve.tensor_copy(identity16[:], const.identity)
                dve.tensor_copy(causal16[:], causal[:].unsqueeze(1).to_broadcast([P, 4, P]))
                dve.wait_ge(a_high, 1)
                dve.tensor_tensor(a_lo[:], a_t[:], a_hi[:].bitcast(F32), ALU.subtract)
                dve.wait_ge(turned, 2)
                dve.tensor_scalar(neg_a[:].rearrange("p a b -> p (a b)"), t_acc[:, 0, 0:256], -1.0, None, ALU.mult)
                for j, dst in ((1, dt), (2, dt_out)):
                    dve.tensor_copy(dst[:].rearrange("p a b -> p (a b)"), t_acc[:, j, 0:256])
                dve.tensor_copy(decay[:].rearrange("p a b -> p (a b)"), d_acc[:, 0:256])

        xs = sb("xs", [P, XS_BUFFERS, T])
        scaled_x = sb("scaled_x", [P, CHUNKS, 2, 64])
        out_x = sb("out_x", [P, CHUNKS, 2, 64])
        weight = sb("weight", [P, 2, T])
        state = sb("state", [P, CHUNKS, 2, 64])
        grown = sb("grown", [P, T])
        z = sb("z", [P, 4, T])
        y = sb("y", [P, 4, T])
        square = sb("square", [P, 4, T])
        rstd = sb("rstd", [P, T])
        mean, root, aux = (sb(what, [P, CHUNKS]) for what in ("mean", "root", "aux"))
        diagonal = sb("diagonal", [P, CHUNKS, P])
        pair_a = ctx.enter_context(nc.psum_tensor(name + "_pair_a", [P, 2, HALF], F32))
        pair_b = ctx.enter_context(nc.psum_tensor(name + "_pair_b", [P, 2, HALF], F32))
        pair_c = ctx.enter_context(nc.psum_tensor(name + "_pair_c", [P, 2, HALF], F32))
        pair_d = ctx.enter_context(nc.psum_tensor(name + "_pair_d", [P, 2, HALF], F32))
        xs_in = [sem(f"xs_in{b}") for b in range(XS_BUFFERS)]
        z_in = [sem(f"z_in{g}") for g in range(GROUPS)]
        (x_turned, x_scaled, b_made, decayed, grown_up, states_made, state_ready, weighted, from_state, off_done, within,
         y_read, y_done, squared, summed, rooting, rooted, diagonal_made, root_spread, normed, gated, chain2) = (
            sem(s) for s in ("x_turned", "x_scaled", "b_made", "decayed", "grown_up", "states_made", "state_ready",
                             "weighted", "from_state", "off_done", "within", "y_read", "y_done", "squared", "summed",
                             "rooting", "rooted", "diagonal_made", "root_spread", "normed", "gated",
                             "chain2"))
        stored = [sem(f"stored{k}") for k in range(4)]
        block = ctx.enter_context(nc.Block())

        @block.sync
        def _(sp):
            def load_xs(j):
                sp.dma_start(xs[:, j % XS_BUFFERS, :],
                             proj[XBC_ROWS + j * P:XBC_ROWS + (j + 1) * P, :]).then_inc(xs_in[j % XS_BUFFERS], 16)

            def load_z(g):
                for k in range(4):
                    at = Z_ROWS + (4 * g + k) * P
                    sp.dma_start(z[:, k, :], proj[at:at + P, :]).then_inc(z_in[g], 16)

            load_xs(0)
            load_z(0)
            for j in range(1, XS_BUFFERS):
                load_xs(j)
            for j in range(SSM_TILES):
                if j >= 4:
                    sp.wait_ge(normed, j - 3)
                    sp.dma_start(out_dram[(j - 4) * P:(j - 3) * P, :], y[:, j % 4, :]).then_inc(stored[j % 4], 16)
                if j % 4 == 3 and j + 1 < SSM_TILES:
                    sp.wait_ge(y_done, j + 1)
                    load_z(j // 4 + 1)
                if j + XS_BUFFERS < SSM_TILES:
                    sp.wait_ge(y_done, j + 1)
                    load_xs(j + XS_BUFFERS)
            for k in range(4):
                sp.wait_ge(normed, 13 + k)
                sp.dma_start(out_dram[(12 + k) * P:(13 + k) * P, :], y[:, k, :]).then_inc(stored[k], 16)
            for k in range(4):
                sp.wait_ge(stored[k], 16 * GROUPS)

        @block.tensor
        def _(pe):
            def turn_xs(j):
                pe.wait_ge(xs_in[j % XS_BUFFERS], 16 * (j // XS_BUFFERS + 1))
                if j >= 1:
                    pe.wait_ge(x_scaled, j)
                for c in range(CHUNKS):
                    mm = pe.transpose(pair_a[:, c // 4, c % 4 * P:(c % 4 + 1) * P],
                                      xs[:, j % XS_BUFFERS, c * P:(c + 1) * P], const.identity)
                mm.then_inc(x_turned, 1)

            def spread_a(j, h):
                if h < 2:
                    if h == 0 and j >= 1:
                        pe.wait_ge(grown_up, j)
                    if h == 1:
                        pe.wait_ge(decayed, 2 * j + 1)
                else:
                    pe.wait_ge(decayed, 2 * j + 2)
                for half in range(2):
                    lhs = (spread[:, j, 64 * h:64 * h + 1].to_broadcast([32, P]) if h < 2 else spread[:, j, :])
                    pe.matmul(pair_b[:, half, :], lhs, a_hi[:, half * HALF:(half + 1) * HALF], start=True, stop=False)
                    mm = pe.matmul(pair_b[:, half, :], lhs, a_lo[:, half * HALF:(half + 1) * HALF],
                                   start=False, stop=(h == 2))
                    if h < 2:
                        mm = pe.matmul(pair_b[:, half, :], identity16[:], causal16[:, :, :].rearrange("p a b -> p (a b)"),
                                       start=False, stop=True)
                mm.then_inc(b_made, 1)

            def sum_group(g):
                pe.wait_ge(off_done, 4 * g + 4)
                pe.wait_ge(squared, 4 * g + 4)
                for c in range(CHUNKS):
                    for k in range(4):
                        mm = pe.matmul(pair_c[:, 0, c:c + 1], square[:, k, c * P:(c + 1) * P], const.ones[:, 0:1],
                                       start=(k == 0), stop=(k == 3))
                mm.then_inc(summed, 1)

            def spread_root(g):
                pe.wait_ge(diagonal_made, g + 1)
                for half in range(2):
                    mm = pe.matmul(pair_c[:, half, :], const.ones,
                                   diagonal[:, 4 * half:4 * half + 4, :].rearrange("p a b -> p (a b)"), start=True, stop=True)
                mm.then_inc(root_spread, 1)

            turn_xs(0)
            spread_a(0, 0)
            spread_a(0, 1)
            for j in range(SSM_TILES):
                g = j // 4
                pe.wait_ge(x_scaled, j + 1)
                if j >= 1:
                    pe.wait_ge(off_done, j)
                for c in range(CHUNKS - 1):
                    mm = pe.matmul(pair_c[:, c // 4, c % 4 * P:(c % 4 + 1) * P], b_nat[:, c, g, :],
                                   out_x[:, c, :, :].rearrange("p a b -> p (a b)"), start=True, stop=True)
                mm.then_inc(states_made, 1)
                if j + 1 < SSM_TILES:
                    turn_xs(j + 1)
                spread_a(j, 2)
                if j >= 1:
                    pe.wait_ge(y_read, j)
                for h in range(2):
                    pe.wait_ge(weighted, 2 * j + h + 1)
                    for c in range(CHUNKS):
                        mm = pe.matmul(pair_d[64 * h:64 * h + 64, c // 4, c % 4 * P:(c % 4 + 1) * P],
                                       scaled_x[:, c, h, :], weight[:, h, c * P:(c + 1) * P], start=True, stop=True)
                mm.then_inc(within, 1)
                if j + 1 < SSM_TILES:
                    spread_a(j + 1, 0)
                pe.wait_ge(state_ready, j + 1)
                if j % 4 == 0 and j >= 4:
                    sum_group(g - 1)
                    spread_root(g - 1)
                    pe.wait_ge(rooted, 2 * g)
                for c in range(1, CHUNKS):
                    mm = pe.matmul(pair_c[:, c // 4, c % 4 * P:(c % 4 + 1) * P],
                                   state[:, c, :, :].rearrange("p a b -> p (a b)"), b_c[:, GROUPS + g, c * P:(c + 1) * P],
                                   start=True, stop=True)
                mm.then_inc(from_state, 1)
                if j + 1 < SSM_TILES:
                    spread_a(j + 1, 1)
            sum_group(GROUPS - 1)
            spread_root(GROUPS - 1)

        @block.scalar
        def _(act):
            def decays(j, h):
                act.wait_ge(b_made, 3 * j + h + 1)
                if j >= 1:
                    act.wait_ge(within, j)
                for c in range(CHUNKS):
                    ins = act.activation(weight[:, h, c * P:(c + 1) * P], pair_b[:, c // 4, c % 4 * P:(c % 4 + 1) * P],
                                         ACT.Exp, bias=neg_a[:, c, 2 * j + h:2 * j + h + 1])
                ins.then_inc(decayed, 1)

            def silu_gates(g):
                act.wait_ge(z_in[g], 64)
                for k in range(4):
                    act.activation(z[:, k, :], z[:, k, :], ACT.Silu).then_inc(gated, 1)

            def table_root(g):
                act.wait_ge(rooting, 6 * g + 2)
                act.activation(root[:], aux[:], ACT.Sqrt).then_inc(rooted, 1)
                act.wait_ge(root_spread, g + 1)
                if g >= 1:
                    act.wait_ge(normed, 4 * g)
                act.activation(rstd[:], pair_c[:, :, :].rearrange("p a b -> p (a b)"), ACT.Copy).then_inc(rooted, 1)

            silu_gates(0)
            decays(0, 0)
            decays(0, 1)
            for j in range(SSM_TILES):
                g = j // 4
                act.wait_ge(b_made, 3 * j + 3)
                if j >= 1:
                    act.wait_ge(off_done, j)
                act.activation(grown[:], pair_b[:, :, :].rearrange("p a b -> p (a b)"), ACT.Exp).then_inc(grown_up, 1)
                if j % 4 == 0 and j >= 4:
                    silu_gates(g)
                if j + 1 < SSM_TILES:
                    decays(j + 1, 0)
                if j % 4 == 0 and j >= 4:
                    table_root(g - 1)
                if j + 1 < SSM_TILES:
                    decays(j + 1, 1)
                act.wait_ge(y_done, j + 1)
                act.activation(square[:, j % 4, :], y[:, j % 4, :], ACT.Square).then_inc(squared, 1)
            table_root(GROUPS - 1)

        @block.vector
        def _(dve):
            links = [0]

            def link(instruction):
                links[0] += 1
                instruction.then_inc(chain2, 1)
                dve.wait_ge(chain2, links[0])

            def flat(ap):
                return ap.rearrange("p a b -> p (a b)")

            def scale_xs(j):
                dve.wait_ge(x_turned, j + 1)
                if j >= 1:
                    dve.wait_ge(within, j)
                turned = pair_a[:, :, :].rearrange("p a (c h d) -> p (a c) h d", c=4, h=2)
                for dst, scale in ((out_x, dt_out), (scaled_x, dt)):
                    ins = dve.tensor_tensor(dst[:, :, :, :], turned,
                                            scale[:, :, 2 * j:2 * j + 2].unsqueeze(3).to_broadcast([P, CHUNKS, 2, 64]),
                                            ALU.mult)
                ins.then_inc(x_scaled, 1)

            def weigh(j, h):
                dve.wait_ge(decayed, 2 * j + h + 1)
                dve.tensor_tensor(weight[:, h, :], weight[:, h, :], cb[:, j // 4, :], ALU.mult).then_inc(weighted, 1)

            def scan(j):
                dve.wait_ge(states_made, j + 1)
                if j >= 1:
                    dve.wait_ge(from_state, j)
                for c in range(CHUNKS - 1):
                    made = pair_c[:, c // 4, c % 4 * P:(c % 4 + 1) * P].rearrange("p (h d) -> p h d", h=2)
                    if c == 0:
                        link(dve.tensor_copy(state[:, 1, :, :], made))
                        continue
                    for h in range(2):
                        ins = dve.scalar_tensor_tensor(out=state[:, c + 1, h, :], in0=state[:, c, h, :],
                                                       scalar=decay[:, c, 2 * j + h:2 * j + h + 1], in1=made[:, h, :],
                                                       op0=ALU.mult, op1=ALU.add)
                        if h == 1 and c < CHUNKS - 2:
                            link(ins)
                ins.then_inc(state_ready, 1)

            def outputs(j):
                dve.wait_ge(from_state, j + 1)
                dve.wait_ge(grown_up, j + 1)
                out, g = y[:, j % 4, :], j // 4
                if j >= 4:
                    dve.wait_ge(stored[j % 4], 16 * g)
                dve.tensor_tensor(out[:, P:], flat(pair_c[:, :, :])[:, P:], grown[:, P:], ALU.mult).then_inc(off_done, 1)
                dve.wait_ge(within, j + 1)
                dve.tensor_copy(out[:, :P], pair_d[:, 0, :P])
                dve.wait_ge(off_done, j + 1)
                dve.tensor_tensor(out[:, P:], out[:, P:], flat(pair_d[:, :, :])[:, P:], ALU.add).then_inc(y_read, 1)
                dve.wait_ge(y_read, j + 1)
                link(dve.scalar_tensor_tensor(out=out, in0=xs[:, j % XS_BUFFERS, :], scalar=tile_par[:, j, 0:1], in1=out,
                                              op0=ALU.mult, op1=ALU.add))
                dve.wait_ge(gated, j + 1)
                dve.tensor_tensor(out, out, z[:, j % 4, :], ALU.mult).then_inc(y_done, 1)

            def norm_root(g):
                base = 6 * g
                dve.wait_ge(summed, g + 1)
                dve.tensor_scalar(mean[:], pair_c[:, 0, 0:CHUNKS], 1.0 / 512, EPS, ALU.mult, ALU.add).then_inc(rooting, 1)
                dve.wait_ge(rooting, base + 1)
                dve.reciprocal(aux[:], mean[:]).then_inc(rooting, 1)
                dve.wait_ge(rooted, 2 * g + 1)
                dve.tensor_tensor(aux[:], root[:], root[:], ALU.mult).then_inc(rooting, 1)
                dve.wait_ge(rooting, base + 3)
                dve.tensor_tensor(aux[:], aux[:], mean[:], ALU.mult).then_inc(rooting, 1)
                dve.wait_ge(rooting, base + 4)
                dve.tensor_scalar(aux[:], aux[:], -0.5, 1.5, ALU.mult, ALU.add).then_inc(rooting, 1)
                dve.wait_ge(rooting, base + 5)
                dve.tensor_tensor(root[:], root[:], aux[:], ALU.mult).then_inc(rooting, 1)
                dve.wait_ge(rooting, base + 6)
                shape = [P, CHUNKS, P]
                dve.tensor_tensor(diagonal[:], const.identity.unsqueeze(1).to_broadcast(shape),
                                  root[:].unsqueeze(2).to_broadcast(shape), ALU.mult).then_inc(diagonal_made, 1)

            def norm_group(g):
                dve.wait_ge(rooted, 2 * g + 2)
                for k in range(4):
                    dve.scalar_tensor_tensor(out=y[:, k, :], in0=y[:, k, :], scalar=tile_par[:, 4 * g + k, 1:2],
                                             in1=rstd[:], op0=ALU.mult, op1=ALU.mult).then_inc(normed, 1)

            scale_xs(0)
            weigh(0, 0)
            weigh(0, 1)
            for j in range(SSM_TILES):
                scan(j)
                if j + 1 < SSM_TILES:
                    scale_xs(j + 1)
                    weigh(j + 1, 0)
                if j % 4 == 0 and j >= 4:
                    norm_root(j // 4 - 1)
                    norm_group(j // 4 - 1)
                outputs(j)
                if j + 1 < SSM_TILES:
                    weigh(j + 1, 1)
            norm_root(GROUPS - 1)
            norm_group(GROUPS - 1)
class Activations:

    def __init__(self, nc, scope, what, kt, source, gain=None, resident=False):
        self.kt, self.source, self.gain, self.resident = kt, source, gain, resident
        self.hi, self.lo = (scope.enter_context(nc.sbuf_tensor(f"{what}_{part}", [P, kt, T], F32R)) for part in ("hi", "lo"))
        self.rstd = scope.enter_context(nc.sbuf_tensor(what + "_rstd", [P, T], F32)) if gain is not None else None


def linear_phase(nc, name, a, w_dram, segments, out_dram, extra1=None, extra2=None, const=None, taps_dram=None,
                 keep=None, resident_extra2=None):
    kt, source, normed = a.kt, a.source, a.gain is not None
    extras = [e for e in (extra1, extra2) if e is not None]
    nt = sum(tiles for tiles, _ in segments)
    kinds = [kind for _, kind in segments]
    uses = [(nt + 1) // 2, nt // 2]
    depth = 4 if kt <= 8 and keep is None else 2
    depth = min(depth, kt)
    ctx = Phase(nc)
    with ctx:
        def sb(what, shape, dt=F32):
            return ctx.enter_context(nc.sbuf_tensor(f"{name}_{what}", shape, dt))

        def sem(what):
            return ctx.semaphore(f"{name}_{what}")

        two = range(2)
        raw, w_hi, w_lo = sb("raw", [P, 2, kt * P]), sb("w_hi", [P, 2, kt * P], F32R), sb("w_lo", [P, 2, kt * P], F32R)
        out = sb("out", [P, 2, T]) if keep is None else keep
        side = [sb(f"side{j}", [P, 2, T]) for j in range(len(extras))]
        acc = ctx.enter_context(nc.psum_tensor(name + "_acc", [P, 4, HALF], F32))
        raw_in, high, low, product, drained, side_in, gated, stored, silued, scaled = (
            [sem(f"{what}{b}") for b in two] for what in
            ("raw_in", "high", "low", "product", "drained", "side_in", "gated", "stored", "silued", "scaled"))
        step, storing = sem("step"), sem("storing")
        if source is not None:
            if not a.resident:
                a_raw = out if depth == 2 and keep is None else sb("a_raw", [P, depth, T])
            a_in = [sem(f"a_in{b}") for b in range(depth)]
            a_high, a_low, squared, added, summed, inverse, root, root_made, root_spread, rstd_ready, gain_in = (
                sem(s) for s in ("a_high", "a_low", "squared", "added", "summed", "inverse", "root", "root_made", "root_spread",
                                 "rstd_ready", "gain_in"))
        if source is not None and normed:
            gain, square, square_sum = sb("gain", [P, kt]), sb("square", [P, 2, T]), sb("square_sum", [P, T])
            mean, root_col, aux = (sb(what, [P, T // P]) for what in ("mean", "root_col", "aux"))
            diagonal = square[:, 0, :].rearrange("p (c t) -> p c t", t=P)
            total = ctx.enter_context(nc.psum_tensor(name + "_total", [P, 2, HALF], F32))
        if "conv" in kinds:
            conv_tiles = dict((kind, tiles) for tiles, kind in segments)["conv"]
            taps, padded = sb("taps", [P, conv_tiles, TAPS + 1]), sb("padded", [P, 2, T + TAPS - 1])
            taps_in = sem("taps_in")
        block = ctx.enter_context(nc.Block())

        def bank(b):
            return acc[:, 2 * b:2 * b + 2, :].rearrange("p a b -> p (a b)")

        def out_at(n, b):
            return out[:, b, :] if keep is None else keep[:, bass.ds(n, 1), :].rearrange("p a t -> p (a t)")

        def input_tile(k):
            return a.source[:, k, :] if a.resident else a_raw[:, k % depth, :]

        def all_turns(engine, step_of, peel=False):
            at = 0
            for tiles, kind in segments:
                ends = at + tiles == nt
                turns = (tiles - (3 if tiles % 2 else 2)) // 2 if ends else tiles // 2
                start = 0

                def pair(i, count=2):
                    for b in range(count):
                        n = 2 * i + (at + b)
                        step_of(n, b, i + at // 2, kind, i, not isinstance(i, int) or n + 2 < nt)

                if peel and at == 0:
                    pair(0)
                    start = 1
                if turns > start:
                    with engine.Fori(start, turns) as i:
                        pair(i)
                if ends:
                    for i in range(max(turns, start), (tiles + 1) // 2):
                        pair(i, min(2, tiles - 2 * i))
                at += tiles

        @block.sync
        def _(sp):
            for b in two:
                sp.sem_inc(stored[b], 16)

            def load(n, b):
                sp.dma_start(raw[:, b, :], w_dram[bass.ds(n * P, P), :]).then_inc(raw_in[b], 16)

            def load_sides(n, b, use):
                if extras:
                    sp.wait_ge(drained[b], use + 1)
                    sp.sem_inc(storing, 1)
                    for j, e in enumerate(extras):
                        sp.dma_start(side[j][:, b, :], e[bass.ds(n * P, P), :]).then_inc(side_in[b], 16)

            def store(n, b, use, kind, i):
                if kind == "conv":
                    sp.wait_ge(silued[b], i + 1)
                else:
                    sp.wait_ge(drained[b], use + 2)
                sp.sem_inc(storing, 1)
                sp.dma_start(out_dram[bass.ds(n * P, P), :], out_at(n, b)).then_inc(stored[b], 16)

            def tile(n, b, use, kind, i, ahead):
                if ahead:
                    sp.wait_ge(low[b], use + 1)
                    sp.sem_inc(storing, 1)
                    load(n + 2, b)
                if not isinstance(n, int) or n + 1 < nt:
                    load_sides(n + 1, 1 - b, use + b)
                store(n, b, use, kind, i)

            load(0, 0)
            if source is not None:
                if normed:
                    sp.dma_start(gain[:], a.gain).then_inc(gain_in, 16)
                for k in range(0 if a.resident else kt):
                    if k >= depth:
                        sp.wait_ge(a_low, k - depth + 1)
                        if normed:
                            sp.wait_ge(squared, k - depth + 1)
                    sp.dma_start(a_raw[:, k % depth, :], source[k * P:(k + 1) * P, :]).then_inc(a_in[k % depth], 16)
                    if k == 1:
                        load(1, 1)
            if source is None or a.resident:
                load(1, 1)
            if "conv" in kinds:
                sp.dma_start(taps[:], taps_dram).then_inc(taps_in, 16)
            load_sides(0, 0, 0)
            all_turns(sp, tile)
            for b in two:
                sp.wait_ge(stored[b], 16 * (uses[b] + 1))

        @block.scalar
        def _(act):
            def split(b, use):
                act.wait_ge(raw_in[b], use * 16 + 16)
                if not (isinstance(use, int) and use == 0):
                    act.wait_ge(product[b], use)
                act.activation(w_hi[:, b, :], raw[:, b, :], ACT.Copy).then_inc(high[b], 1)

            def gate(n, b, use, kind, i):
                o = out_at(n, b)
                if kind in ("gate", "gate_add"):
                    act.wait_ge(side_in[b], use * (16 * len(extras)) + 16 * len(extras))
                    act.activation(side[0][:, b, :], side[0][:, b, :], ACT.Sigmoid).then_inc(gated[b], 1)
                if kind == "final":
                    act.wait_ge(scaled[b], use + 1)
                    act.activation(o, o, ACT.Sigmoid).then_inc(gated[b], 1)
                if kind == "conv":
                    act.wait_ge(drained[b], use + 2)
                    act.activation(o, o, ACT.Silu).then_inc(silued[b], 1)

            def tile(n, b, use, kind, i, ahead):
                if ahead:
                    split(b, use + 1)
                gate(n, b, use, kind, i)

            split(0, 0)
            if source is not None:
                if normed:
                    act.wait_ge(gain_in, 16)
                for k in range(kt):
                    if not a.resident:
                        act.wait_ge(a_in[k % depth], 16 * (k // depth + 1))
                    part = input_tile(k)
                    if normed:
                        act.activation(a.hi[:, k, :], part, ACT.Copy, scale=gain[:, k:k + 1]).then_inc(a_high, 1)
                        if k >= 3:
                            act.wait_ge(added, k - 2)
                        act.activation(square_sum[:] if k == 0 else square[:, k % 2, :], part,
                                       ACT.Square).then_inc(squared, 1)
                    else:
                        act.activation(a.hi[:, k, :], part, ACT.Copy).then_inc(a_high, 1)
                    if k == 1:
                        split(1, 0)
            else:
                split(1, 0)
            if source is not None and normed:
                act.wait_ge(inverse, 2)
                act.activation(root_col[:], aux[:], ACT.Sqrt).then_inc(root, 1)
                act.wait_ge(root_spread, 1)
                act.activation(a.rstd[:], total[:, :, :].rearrange("p a b -> p (a b)"), ACT.Copy).then_inc(rstd_ready, 1)
            all_turns(act, tile)

        @block.vector
        def _(dve):
            for b in two:
                dve.sem_inc(drained[b], 1)

            def split(b, use):
                dve.wait_ge(high[b], use + 1)
                dve.tensor_tensor(w_lo[:, b, :], raw[:, b, :], w_hi[:, b, :].bitcast(F32),
                                  ALU.subtract).then_inc(low[b], 1)

            def split_activations():
                for k in range(kt):
                    dve.wait_ge(a_high, k + 1)
                    part, hi = input_tile(k), a.hi[:, k, :].bitcast(F32)
                    if normed:
                        ins = dve.scalar_tensor_tensor(out=a.lo[:, k, :], in0=part, scalar=gain[:, k:k + 1], in1=hi,
                                                       op0=ALU.mult, op1=ALU.subtract)
                    else:
                        ins = dve.tensor_tensor(a.lo[:, k, :], part, hi, ALU.subtract)
                    ins.then_inc(a_low, 1)
                    if normed and k >= 1:
                        dve.wait_ge(squared, k + 1)
                        if k >= 2:
                            dve.wait_ge(added, k - 1)
                        dve.tensor_tensor(square_sum[:], square_sum[:], square[:, k % 2, :], ALU.add).then_inc(added, 1)
                    if k == 1:
                        split(1, 0)

            def norm():
                dve.wait_ge(summed, 1)
                dve.tensor_scalar(mean[:], total[:, 0, 0:T // P], 1.0 / (kt * P), EPS, ALU.mult, ALU.add).then_inc(inverse, 1)
                dve.wait_ge(inverse, 1)
                dve.reciprocal(aux[:], mean[:]).then_inc(inverse, 1)
                dve.wait_ge(root, 1)
                dve.tensor_tensor(aux[:], root_col[:], root_col[:], ALU.mult).then_inc(inverse, 1)
                dve.wait_ge(inverse, 3)
                dve.tensor_tensor(aux[:], aux[:], mean[:], ALU.mult).then_inc(inverse, 1)
                dve.wait_ge(inverse, 4)
                dve.tensor_scalar(aux[:], aux[:], -0.5, 1.5, ALU.mult, ALU.add).then_inc(inverse, 1)
                dve.wait_ge(inverse, 5)
                dve.tensor_tensor(root_col[:], root_col[:], aux[:], ALU.mult).then_inc(inverse, 1)
                dve.wait_ge(inverse, 6)
                shape = [P, T // P, P]
                dve.tensor_tensor(diagonal, const.identity.unsqueeze(1).to_broadcast(shape),
                                  root_col[:].unsqueeze(2).to_broadcast(shape), ALU.mult).then_inc(root_made, 1)

            def link(instruction, count):
                instruction.then_inc(step, 1)
                dve.wait_ge(step, count)

            def epilogue(n, b, use, kind, i):
                dve.wait_ge(product[b], use + 1)
                o, s0 = out_at(n, b), (side[0][:, b, :] if extras else None)
                dve.wait_ge(stored[b], use * 16 + 16)
                if kind == "copy":
                    if normed:
                        dve.tensor_tensor(o, bank(b), a.rstd[:], ALU.mult).then_inc(drained[b], 1)
                    else:
                        dve.tensor_copy(o, bank(b)).then_inc(drained[b], 1)
                elif kind == "add":
                    dve.wait_ge(side_in[b], use * 16 + 16)
                    dve.tensor_tensor(o, bank(b), s0, ALU.add).then_inc(drained[b], 1)
                elif kind == "gate":
                    dve.wait_ge(gated[b], use + 1)
                    dve.tensor_tensor(o, bank(b), s0, ALU.mult).then_inc(drained[b], 1)
                elif kind == "gate_add":
                    dve.wait_ge(gated[b], use + 1)
                    link(dve.tensor_tensor(o, bank(b), s0, ALU.mult), use * 2 + (b + 1))
                    dve.tensor_tensor(o, o, side[1][:, b, :], ALU.add).then_inc(drained[b], 1)
                elif kind == "final":
                    dve.tensor_tensor(o, bank(b), a.rstd[:], ALU.mult).then_inc(scaled[b], 1)
                    dve.wait_ge(gated[b], use + 1)
                    dve.wait_ge(side_in[b], use * 16 + 16)
                    link(dve.tensor_tensor(o, o, s0, ALU.mult), use * 2 + (b + 1))
                    s1 = resident_extra2[:, bass.ds(n, 1), :].rearrange("p a t -> p (a t)")
                    dve.tensor_tensor(o, o, s1, ALU.add).then_inc(drained[b], 1)
                elif kind == "conv":
                    tap = taps[:, bass.ds(2 * i + b, 1), :].rearrange("p a k -> p (a k)")
                    links = i * 8 + 4 * b
                    u = padded[:, b, :]
                    link(dve.tensor_tensor(u[:, TAPS - 1:], bank(b), a.rstd[:], ALU.mult), links + 1)
                    link(dve.tensor_scalar(o, u[:, 3:3 + T], tap[:, 3:4], tap[:, 4:5], ALU.mult, ALU.add), links + 2)
                    for k in range(TAPS - 1):
                        ins = dve.scalar_tensor_tensor(out=o, in0=u[:, k:k + T], scalar=tap[:, k:k + 1], in1=o,
                                                       op0=ALU.mult, op1=ALU.add)
                        if k < TAPS - 2:
                            link(ins, links + 3 + k)
                    ins.then_inc(drained[b], 1)

            def tile(n, b, use, kind, i, ahead):
                epilogue(n, b, use, kind, i)
                if ahead:
                    split(b, use + 1)

            split(0, 0)
            if source is not None:
                split_activations()
            else:
                split(1, 0)
            if source is not None and normed:
                norm()
            if "conv" in kinds:
                dve.memset(padded[:, :, 0:TAPS - 1], 0.0)
                dve.wait_ge(taps_in, 16)
            if source is not None and normed:
                dve.wait_ge(rstd_ready, 1)
            all_turns(dve, tile)

        @block.tensor
        def _(pe):
            def multiply_input(b, k):
                for n_pass, (w, h) in enumerate(((w_hi, a.hi), (w_hi, a.lo), (w_lo, a.hi))):
                    for half in two:
                        mm = pe.matmul(acc[:, 2 * b + half, :], w[:, b, k * P:(k + 1) * P],
                                       h[:, k, half * HALF:(half + 1) * HALF],
                                       start=(k == 0 and n_pass == 0), stop=(k == kt - 1 and n_pass == 2))
                if k == kt - 1:
                    mm.then_inc(product[b], 1)

            def sum_squares():
                pe.wait_ge(added, kt - 1)
                for c in range(T // P):
                    mm = pe.matmul(total[:, 0, c:c + 1], square_sum[:, c * P:(c + 1) * P], const.ones[:, 0:1],
                                   start=True, stop=True)
                mm.then_inc(summed, 1)

            def spread_root():
                pe.wait_ge(root_made, 1)
                for half in two:
                    mm = pe.matmul(total[:, half, :], const.ones, square[:, 0, half * HALF:(half + 1) * HALF],
                                   start=True, stop=True)
                mm.then_inc(root_spread, 1)

            def multiply_as_it_comes():
                lag = kt // 2
                for b in two:
                    pe.wait_ge(drained[b], 1)
                pe.wait_ge(low[0], 1)
                for k in range(kt + lag):
                    if k < kt:
                        pe.wait_ge(a_low, k + 1)
                        multiply_input(0, k)
                    if normed and k == kt:
                        sum_squares()
                    if k == lag:
                        pe.wait_ge(low[1], 1)
                    if k >= lag:
                        multiply_input(1, k - lag)
                    if normed and k == kt + lag - 2:
                        spread_root()

            def multiply(n, b, use, kind, i, ahead):
                if isinstance(n, int) and n < 2 and source is not None:
                    return
                pe.wait_ge(low[b], use + 1)
                pe.wait_ge(drained[b], use + 1)
                for k in range(kt):
                    multiply_input(b, k)

            if source is not None:
                multiply_as_it_comes()
            all_turns(pe, multiply, peel=source is not None)


PEER_HEADS = 8
TOP = 16
KEYS = 128
SCORE_SETS = 2 * PEER_HEADS
LOWEST = -3e38
EXPERT_TILES = KEYS
TURN_TILES = 14
GATE_GROUP = 4
GATE_GROUPS = P // GATE_GROUP
PIECES = 4


def select_phase(nc, name, a, u_dram, hidden_dram, q_dram, keys_dram, count_dram, gates_dram, const):
    ctx = Phase(nc)
    with ctx:
        def sb(what, shape, dt=F32):
            return ctx.enter_context(nc.sbuf_tensor(f"{name}_{what}", shape, dt))

        def sem(what):
            return ctx.semaphore(f"{name}_{what}")

        two = range(2)
        u_raw, u_hi, u_lo = sb("u_raw", [P, 2, D]), sb("u_hi", [P, 2, D], F32R), sb("u_lo", [P, 2, D], F32R)
        hidden = sb("hidden", [P, 2, T])
        gates = sb("gates", [P, KEYS, P])
        first = sb("first", [P, 2, GATE_GROUP, KEYS])
        second = sb("second", [P, 2, GATE_GROUP, KEYS])
        q = sb("q", [P, SCORE_SETS, P])
        keys = sb("keys", [P, SCORE_SETS, KEYS])
        count = sb("count", [P, KEYS])
        work = sb("work", [P, SCORE_SETS * KEYS])
        best = sb("best", [P, SCORE_SETS, TOP])
        index = sb("index", [P, SCORE_SETS, TOP], U32)
        index_f = sb("index_f", [P, SCORE_SETS, TOP])
        total = sb("total", [P, PEER_HEADS, TOP])
        place = sb("place", [P, PEER_HEADS, TOP], U32)
        part = sb("part", [P, 2, PEER_HEADS * TOP], U32)
        part_f = sb("part_f", [P, 2, PEER_HEADS * TOP])
        found = sb("found", [P, 3, PEER_HEADS * TOP])
        chosen = sb("chosen", [P, 3, P])
        denom = sb("denom", [P, 2, PEER_HEADS])
        score = work[:].rearrange("p (s n) -> p s n", s=SCORE_SETS)
        pair = work[:].rearrange("p (h i j) -> p h i j", h=PEER_HEADS, i=TOP)
        u_acc = ctx.enter_context(nc.psum_tensor(name + "_u_acc", [P, 2, 2, HALF], F32))
        s_acc = ctx.enter_context(nc.psum_tensor(name + "_s_acc", [P, 2, HALF], F32))
        g_acc = ctx.enter_context(nc.psum_tensor(name + "_g_acc", [P, 2, GATE_GROUP, KEYS], F32))
        u_in, u_high, u_split, u_done, normed, gelued, kept_hidden = (
            [sem(f"{what}{e}") for e in two] for what in
            ("u_in", "u_high", "u_split", "u_done", "normed", "gelued", "kept_hidden"))
        (small_in, q_in, scored, copied, begun, chain, shifted, exped, routed, turned, chosen_ready, made, spread,
         drained, storing, storing_gates, stored) = (
            sem(s) for s in ("small_in", "q_in", "scored", "copied", "begun", "chain", "shifted", "exped", "routed",
                             "turned", "chosen_ready", "made", "spread", "drained", "storing", "storing_gates", "stored"))
        block = ctx.enter_context(nc.Block())
        TURNS = T // P
        LAST_TILES = EXPERT_TILES - TURNS * TURN_TILES
        SPREAD = [0, 0, 2, 3, 3, 4, 3, 3, 4, 4, 3, 1, 2, 0]
        SETS = [range(0, 5), range(5, 10), range(10, 14), range(14, 16)]
        HEADS = {4: (0,), 5: (1,), 6: (2,), 7: (3, 4), 8: (5,), 9: (6,), 10: (7,)}
        SPREAD_LAST = [0, 0] + [3] * 10 + [2, 0, 0, 0]
        SPREAD_AT = (1, 3, 5, 7)
        assert len(SPREAD) == TURN_TILES and len(SPREAD_LAST) == LAST_TILES and sum(SPREAD) == sum(SPREAD_LAST) == GATE_GROUPS

        def groups_by_tile(m):
            counts = SPREAD_LAST if isinstance(m, int) and m == TURNS else SPREAD
            return [range(sum(counts[:k]), sum(counts[:k + 1])) for k in range(len(counts))]

        def turns(engine, turn):
            turn(0, True, False)
            turn(1, True, True)
            with engine.Fori(2, TURNS - 1) as m:
                turn(m, True, True)
            turn(TURNS - 1, True, True)
            turn(TURNS, False, True)

        def is_first(m):
            return isinstance(m, int) and m == 0

        def has_ahead(m, k, ahead):
            return not isinstance(m, int) or m * TURN_TILES + k + ahead < EXPERT_TILES

        @block.sync
        def _(sp):
            q_view = q_dram.rearrange("(s p) t -> p s t", p=P)

            def load_u(tile, e):
                sp.dma_start(u_raw[:, e, :], u_dram[bass.ds(tile * P, P), :]).then_inc(u_in[e], 16)

            def load_q(m):
                sp.dma_start(q[:], q_view[:, :, bass.ds(m * P, P)]).then_inc(q_in, 16)

            for e in two:
                load_u(e, e)
            load_q(0)
            sp.dma_start(keys[:], keys_dram).then_inc(small_in, 16)
            sp.dma_start(count[:], count_dram).then_inc(small_in, 16)

            def turn(m, route, spreads):
                for k in range(TURN_TILES if route else LAST_TILES):
                    if k == 4 and (not isinstance(m, int) or m < TURNS - 1):
                        sp.wait_ge(scored, m * 2 + 2)
                        sp.sem_inc(storing, 1)
                        load_q(m + 1)
                    e, use = k % 2, m * (TURN_TILES // 2) + k // 2
                    if has_ahead(m, k, 2):
                        sp.wait_ge(u_split[e], use + 1)
                        load_u(m * TURN_TILES + (k + 2), e)
                    sp.wait_ge(gelued[e], use + 1)
                    sp.sem_inc(storing, 1)
                    sp.dma_start(hidden_dram[bass.ds((m * TURN_TILES + k) * P, P), :],
                                 hidden[:, e, :]).then_inc(kept_hidden[e], 16)

            turns(sp, turn)
            sp.wait_ge(stored, 16 * PIECES * (TURNS + 1))
            for e in two:
                sp.wait_ge(kept_hidden[e], 16 * (EXPERT_TILES // 2 + 1))

        @block.tensor
        def _(pe):
            def scores(m, half):
                if half == 0:
                    pe.wait_ge(q_in, m * 16 + 16)
                if half == 1 or not is_first(m):
                    pe.wait_ge(copied, m * 2 + half)
                    if half == 0:
                        pe.wait_ge(chosen_ready, m)
                for s in range(8):
                    mm = pe.matmul(s_acc[:, s // 4, s % 4 * KEYS:(s % 4 + 1) * KEYS], q[:, half * 8 + s, :],
                                   keys[:, half * 8 + s, :], start=True, stop=True)
                mm.then_inc(scored, 1)

            def turn_results(m):
                pe.wait_ge(routed, m + 1)
                for j in range(3):
                    mm = pe.transpose(s_acc[:, 0, j * P:(j + 1) * P], found[:, j, :], const.identity)
                mm.then_inc(turned, 1)

            def hidden_tile(m, k, groups, results):
                e, use = k % 2, m * (TURN_TILES // 2) + k // 2
                pe.wait_ge(u_split[e], use + 1)
                pe.wait_ge(normed[e], use + 1)
                for kd in range(KD):
                    for n_pass, (w, h) in enumerate(((u_hi, a.hi), (u_hi, a.lo), (u_lo, a.hi))):
                        for half in two:
                            mm = pe.matmul(u_acc[:, e, half, :], w[:, e, kd * P:(kd + 1) * P],
                                           h[:, kd, half * HALF:(half + 1) * HALF],
                                           start=(kd == 0 and n_pass == 0), stop=(kd == KD - 1 and n_pass == 2))
                    if kd == KD - 1:
                        mm.then_inc(u_done[e], 1)
                    for n, r in enumerate(groups):
                        if kd == SPREAD_AT[n]:
                            spread_group(m, r)
                    if kd == KD - 2 and results:
                        turn_results(m)

            def spread_group(m, r):
                b = r % 2
                pe.wait_ge(made, (m - 1) * GATE_GROUPS + (r + 1))
                pe.wait_ge(drained, (m - 1) * GATE_GROUPS + (r + 1))
                for n in range(GATE_GROUP):
                    mm = pe.matmul(g_acc[:, b, n, :], second[:, b, n, :], first[:, b, n, :], start=True, stop=True)
                mm.then_inc(spread, 1)

            def turn(m, route, spreads):
                groups = groups_by_tile(m)
                for k in range(len(groups)):
                    if k < 2 and route:
                        scores(m, k)
                    hidden_tile(m, k, groups[k - 1] if spreads and k >= 1 else (), route and k == TURN_TILES - 1)

            pe.sem_inc(spread, 2)
            pe.wait_ge(small_in, 32)
            turns(pe, turn)

        @block.scalar
        def _(act):
            def split_u(use, e):
                act.wait_ge(u_in[e], use * 16 + 16)
                if not (isinstance(use, int) and use == 0):
                    act.wait_ge(u_done[e], use)
                act.activation(u_hi[:, e, :], u_raw[:, e, :], ACT.Copy).then_inc(u_high[e], 1)

            def store_gates(m, piece):
                if piece == 0:
                    act.wait_ge(drained, m * GATE_GROUPS + 2)
                act.sem_inc(storing_gates, 1)
                keys1 = slice(piece * KEYS // PIECES, (piece + 1) * KEYS // PIECES)
                act.dma_start(gates_dram[:, keys1, bass.ds((m - 1) * P, P)], gates[:, keys1, :]).then_inc(stored, 16)

            def drain_group(m, r):
                act.wait_ge(spread, (m - 1) * GATE_GROUPS + (r + 3))
                if r == 0:
                    act.wait_ge(stored, m * (16 * PIECES))
                act.activation(gates[:, :, r * GATE_GROUP:(r + 1) * GATE_GROUP], g_acc[:, r % 2, :, :].rearrange("p n k -> p k n"),
                               ACT.Copy).then_inc(drained, 1)

            def copy_scores(m, half):
                act.wait_ge(scored, m * 2 + (half + 1))
                if half == 0 and not is_first(m):
                    act.wait_ge(routed, m)
                act.activation(work[:, half * T:(half + 1) * T], s_acc[:, :, :].rearrange("p a b -> p (a b)"),
                               ACT.Copy).then_inc(copied, 1)

            def turn(m, route, spreads):
                groups = groups_by_tile(m)
                for k in range(len(groups)):
                    e, use = k % 2, m * (TURN_TILES // 2) + k // 2
                    if k < 2 and route:
                        copy_scores(m, k)
                    if spreads and k >= 1:
                        for r in groups[k - 1]:
                            drain_group(m, r)
                        if GATE_GROUPS - 1 in groups[k - 1]:
                            store_gates(m, 0)
                            if not route:
                                for piece in range(1, PIECES):
                                    store_gates(m, piece)
                    if not (isinstance(m, int) and m < 2) and k < PIECES - 1:
                        store_gates(m - 1, k + 1)
                    if route and k == TURN_TILES - 1:
                        act.wait_ge(turned, m + 1)
                        act.activation(chosen[:].rearrange("p a b -> p (a b)"), s_acc[:, 0, 0:3 * P],
                                       ACT.Copy).then_inc(chosen_ready, 1)
                    if has_ahead(m, k, 2):
                        split_u(use + 1, e)
                    act.wait_ge(normed[e], use + 2)
                    act.activation(hidden[:, e, :], hidden[:, e, :], ACT.Gelu_apprx_tanh).then_inc(gelued[e], 1)
                    if k == 11 and route:
                        act.wait_ge(shifted, m + 1)
                        act.activation(found[:, 2, :], found[:, 2, :], ACT.Exp).then_inc(exped, 1)

            act.sem_inc(drained, 2)
            for e in two:
                split_u(0, e)
            turns(act, turn)

        @block.gpsimd
        def _(pool):
            for e in two:
                pool.sem_inc(kept_hidden[e], 16)
            pool.sem_inc(stored, 16 * PIECES)

        @block.vector
        def _(dve):
            links = [0]

            def link(instruction):
                links[0] += 1
                instruction.then_inc(chain, 1)
                dve.wait_ge(chain, links[0])

            def search(values, best16, index16):
                link(dve.max(best16[:, 0:8], values))
                link(dve.max_index(index16[:, 0:8], best16[:, 0:8], values))
                link(dve.match_replace(values, best16[:, 0:8], values, LOWEST))
                link(dve.max(best16[:, 8:16], values))
                link(dve.max_index(index16[:, 8:16], best16[:, 8:16], values))

            shape = [P, PEER_HEADS, TOP, TOP]
            rows = [P, PEER_HEADS * TOP, TOP]

            def route_sets(lo, hi):
                for s in range(lo, hi):
                    search(score[:, s, :], best[:, s, :], index[:, s, :])

            def pair_sums():
                halves = best[:, :, :].rearrange("p (h two) k -> p h two k", two=2)
                link(dve.tensor_copy(index_f[:], index[:]))
                link(dve.tensor_tensor(pair, halves[:, :, 0, :].unsqueeze(3).to_broadcast(shape),
                                       halves[:, :, 1, :].unsqueeze(2).to_broadcast(shape), ALU.add))

            def route_head(h):
                search(pair[:, h, :, :].rearrange("p a b -> p (a b)"), total[:, h, :], place[:, h, :])

            def below_best(m):
                flat_place = place[:].rearrange("p h k -> p (h k)")
                link(dve.tensor_tensor(found[:, 2, :].rearrange("p (h k) -> p h k", k=TOP), total[:],
                                       total[:, :, 0:1].to_broadcast([P, PEER_HEADS, TOP]), ALU.subtract))
                dve.sem_inc(shifted, 1)
                link(dve.tensor_scalar(part[:, 0, :], flat_place, 4, None, ALU.logical_shift_right))
                link(dve.tensor_scalar(part[:, 1, :], flat_place, 15, None, ALU.bitwise_and))
                link(dve.tensor_copy(part_f[:], part[:]))

            def look_up(j):
                ids = index_f[:, :, :].rearrange("p (h two) k -> p h two k", two=2)
                hit_rows = work[:].rearrange("p (a j) -> p a j", j=TOP)
                link(dve.tensor_tensor(hit_rows, count[:, 0:TOP].unsqueeze(1).to_broadcast(rows),
                                       part_f[:, j, :].unsqueeze(2).to_broadcast(rows), ALU.is_equal))
                link(dve.tensor_tensor(pair, pair, ids[:, :, j, :].unsqueeze(2).to_broadcast(shape), ALU.mult))
                link(dve.tensor_reduce(found[:, j, :], hit_rows, AX.X, ALU.add))

            def weigh(m):
                dve.wait_ge(exped, m + 1)
                weights = found[:, 2, :].rearrange("p (h k) -> p h k", k=TOP)
                link(dve.tensor_reduce(denom[:, 0, :], weights, AX.X, ALU.add))
                link(dve.reciprocal(denom[:, 1, :], denom[:, 0, :]))
                link(dve.tensor_tensor(weights, weights,
                                       denom[:, 1, :].unsqueeze(2).to_broadcast([P, PEER_HEADS, TOP]), ALU.mult))
                dve.sem_inc(routed, 1)

            def one_hots(m, r):
                b = r % 2
                if r == 0:
                    dve.wait_ge(chosen_ready, m)
                dve.wait_ge(spread, (m - 1) * GATE_GROUPS + (r + 1))
                for n in range(GATE_GROUP):
                    t = r * GATE_GROUP + n
                    dve.tensor_scalar(second[:, b, n, :], count[:], chosen[:, 1, t:t + 1], None, ALU.is_equal)
                    ins = dve.tensor_scalar(first[:, b, n, :], count[:], chosen[:, 0, t:t + 1], chosen[:, 2, t:t + 1],
                                            ALU.is_equal, ALU.mult)
                ins.then_inc(made, 1)

            def split_u(use, e):
                dve.wait_ge(u_high[e], use + 1)
                dve.tensor_tensor(u_lo[:, e, :], u_raw[:, e, :], u_hi[:, e, :].bitcast(F32),
                                  ALU.subtract).then_inc(u_split[e], 1)

            def norm_hidden(use, e):
                dve.wait_ge(u_done[e], use + 1)
                dve.wait_ge(kept_hidden[e], use * 16 + 16)
                dve.tensor_tensor(hidden[:, e, :], u_acc[:, e, :, :].rearrange("p a b -> p (a b)"), a.rstd[:],
                                  ALU.mult).then_inc(normed[e], 1)

            def turn(m, route, spreads):
                links[0] = 0
                if not is_first(m) and route:
                    dve.sem_clear(chain)
                groups = groups_by_tile(m)
                for k in range(len(groups)):
                    n = k + 1
                    if k >= 1:
                        norm_hidden(m * (TURN_TILES // 2) + (k - 1) // 2, (k - 1) % 2)
                    if has_ahead(m, k, 1):
                        split_u(m * (TURN_TILES // 2) + n // 2, n % 2)
                    if route:
                        if k == 0 or k == 1:
                            dve.wait_ge(copied, m * 2 + (k + 1))
                            dve.sem_inc(begun, 1)
                        if k < 4:
                            route_sets(SETS[k][0], SETS[k][-1] + 1)
                            if k == 3:
                                pair_sums()
                        elif k in HEADS:
                            for head in HEADS[k]:
                                route_head(head)
                        elif k == 11:
                            below_best(m)
                            look_up(0)
                        elif k == 12:
                            look_up(1)
                        else:
                            weigh(m)
                    if spreads:
                        for r in groups[k]:
                            one_hots(m, r)
                norm_hidden(m * (TURN_TILES // 2) + len(groups) // 2 - 1, 1)

            dve.wait_ge(small_in, 32)
            for e in two:
                dve.sem_inc(normed[e], 1)
            split_u(0, 0)
            turns(dve, turn)


def combine_phase(nc, name, hidden_dram, gates_dram, v_dram, x_dram, total):
    QUAD = 4
    STEPS = EXPERT_TILES // QUAD
    BANKS = 8
    OUTS = 2 * KD
    ctx = Phase(nc)
    with ctx:
        def sb(what, shape, dt=F32):
            return ctx.enter_context(nc.sbuf_tensor(f"{name}_{what}", shape, dt))

        def sem(what):
            return ctx.semaphore(f"{name}_{what}")

        two = range(2)
        v_raw, hidden, gate = sb("v_raw", [P, 2, D]), sb("hidden", [P, 2, T]), sb("gate", [P, 2, T])
        v_hi, v_lo = sb("v_hi", [P, 2, QUAD, D], F32R), sb("v_lo", [P, 2, QUAD, D], F32R)
        a_hi, a_lo = sb("a_hi", [P, 2, QUAD, T], F32R), sb("a_lo", [P, 2, QUAD, T], F32R)
        acc = ctx.enter_context(nc.psum_tensor(name + "_acc", [P, BANKS, HALF], F32))
        v_in, a_in = ([sem(f"{what}{b}") for b in two] for what in ("v_in", "a_in"))
        x_in, v_high, v_split, gated, a_high, a_split, multiplied, added = (
            sem(s) for s in ("x_in", "v_high", "v_split", "gated", "a_high", "a_split", "multiplied", "added"))
        block = ctx.enter_context(nc.Block())

        @block.sync
        def _(sp):
            def load(tile, b):
                sp.dma_start(v_raw[:, b, :], v_dram[bass.ds(tile * P, P), :]).then_inc(v_in[b], 16)
                sp.dma_start(hidden[:, b, :], hidden_dram[bass.ds(tile * P, P), :]).then_inc(a_in[b], 16)
                sp.dma_start(gate[:, b, :], gates_dram[:, bass.ds(tile, 1), :].rearrange("p a t -> p (a t)")
                             ).then_inc(a_in[b], 16)

            def load_pair(i):
                for b in two:
                    sp.wait_ge(v_split, i * 2 + (b + 1))
                    sp.wait_ge(a_split, i * 2 + (b + 1))
                    load(i * 2 + (b + 2), b)

            load(0, 0)
            load(1, 1)
            load_pair(0)
            for k in range(KD):
                sp.dma_start(total[:, k, :], x_dram[k * P:(k + 1) * P, :]).then_inc(x_in, 16)
            with sp.Fori(1, EXPERT_TILES // 2 - 1) as i:
                load_pair(i)

        @block.tensor
        def _(pe):
            def step(s, slot):
                pe.wait_ge(v_split, s * QUAD + QUAD)
                pe.wait_ge(a_split, s * QUAD + QUAD)
                for n in range(OUTS):
                    d, half = divmod(n, 2)
                    pe.wait_ge(added, s * OUTS + (n + 1))
                    for e in range(QUAD):
                        for n_pass, (w, a) in enumerate(((v_hi, a_hi), (v_hi, a_lo), (v_lo, a_hi))):
                            mm = pe.matmul(acc[:, n % BANKS, :], w[:, slot, e, d * P:(d + 1) * P],
                                           a[:, slot, e, half * HALF:(half + 1) * HALF],
                                           start=(e == 0 and n_pass == 0), stop=(e == QUAD - 1 and n_pass == 2))
                    mm.then_inc(multiplied, 1)

            def first_step():
                for n0 in range(0, OUTS, BANKS):
                    for e in range(QUAD):
                        pe.wait_ge(v_split, e + 1)
                        pe.wait_ge(a_split, e + 1)
                        for n in range(n0, n0 + BANKS):
                            d, half = divmod(n, 2)
                            if e == 0:
                                pe.wait_ge(added, n + 1)
                            for n_pass, (w, a) in enumerate(((v_hi, a_hi), (v_hi, a_lo), (v_lo, a_hi))):
                                mm = pe.matmul(acc[:, n % BANKS, :], w[:, 0, e, d * P:(d + 1) * P],
                                               a[:, 0, e, half * HALF:(half + 1) * HALF],
                                               start=(e == 0 and n_pass == 0), stop=(e == QUAD - 1 and n_pass == 2))
                            if e == QUAD - 1:
                                mm.then_inc(multiplied, 1)

            pe.sem_inc(added, BANKS)
            first_step()
            step(1, 1)
            with pe.Fori(1, STEPS // 2) as i:
                step(i * 2, 0)
                step(i * 2 + 1, 1)

        def steps(engine, prepare, add):
            for e in range(QUAD):
                prepare(0, 0, e)
            engine.wait_ge(x_in, 16 * KD)
            with engine.Fori(0, STEPS // 2 - 1) as i:
                for half in two:
                    for e in range(QUAD):
                        prepare(i * 2 + (half + 1), 1 - half, e)
                        add(i * 2 + half, e)
            for e in range(QUAD):
                prepare(STEPS - 1, 1, e)
                add(STEPS - 2, e)
            for e in range(QUAD):
                add(STEPS - 1, e)

        @block.scalar
        def _(act):
            def prepare(s, slot, e):
                b, use = e % 2, s * 2 + e // 2
                act.wait_ge(v_in[b], use * 16 + 16)
                if not isinstance(s, int) or s >= 2:
                    act.wait_ge(multiplied, s * OUTS - OUTS)
                act.activation(v_hi[:, slot, e, :], v_raw[:, b, :], ACT.Copy).then_inc(v_high, 1)
                act.wait_ge(gated, s * QUAD + (e + 1))
                act.activation(a_hi[:, slot, e, :], hidden[:, b, :], ACT.Copy).then_inc(a_high, 1)

            for e in range(QUAD):
                prepare(0, 0, e)
            for e in range(QUAD):
                prepare(1, 1, e)
            with act.Fori(1, STEPS // 2) as i:
                for half in two:
                    for e in range(QUAD):
                        prepare(i * 2 + half, half, e)

        @block.vector
        def _(dve):
            def prepare(s, slot, e):
                b, use = e % 2, s * 2 + e // 2
                dve.wait_ge(a_in[b], use * 32 + 32)
                dve.tensor_tensor(hidden[:, b, :], hidden[:, b, :], gate[:, b, :], ALU.mult).then_inc(gated, 1)
                dve.wait_ge(v_high, s * QUAD + (e + 1))
                dve.tensor_tensor(v_lo[:, slot, e, :], v_raw[:, b, :], v_hi[:, slot, e, :].bitcast(F32),
                                  ALU.subtract).then_inc(v_split, 1)
                dve.wait_ge(a_high, s * QUAD + (e + 1))
                dve.tensor_tensor(a_lo[:, slot, e, :], hidden[:, b, :], a_hi[:, slot, e, :].bitcast(F32),
                                  ALU.subtract).then_inc(a_split, 1)

            def add(s, quarter):
                for n in range(4 * quarter, 4 * quarter + 4):
                    d, half = divmod(n, 2)
                    at = slice(half * HALF, (half + 1) * HALF)
                    dve.wait_ge(multiplied, s * OUTS + (n + 1))
                    dve.tensor_tensor(total[:, d, at], total[:, d, at], acc[:, n % BANKS, :], ALU.add).then_inc(added, 1)

            steps(dve, prepare, add)


def shape_constants():
    c = {}
    c["identity"] = np.eye(P, dtype=np.float32)
    c["flip"] = np.ascontiguousarray(c["identity"][::-1])
    p = np.arange(P)
    pick = (np.arange(32)[None, None, :] == 2 * np.arange(16)[None, :, None] + (p // 64)[:, None, None])
    c["head_pick"] = pick.astype(np.float32).reshape(P, 16 * 32)
    c["head_spread"] = np.ascontiguousarray(pick.transpose(2, 1, 0)).astype(np.float32).reshape(32, 16 * P)
    rel = np.arange(REL_COUNT) - (REL_COUNT - P)
    near = np.abs(rel)
    far = 8 + sum((rel * rel >= 64 * 2 ** q).astype(np.int64) for q in range(1, 8))
    bucket = np.where(rel > 0, 16, 0) + np.where(near < 8, near, far)
    c["bucket_onehot"] = (np.arange(32)[:, None] == bucket[None, :]).astype(np.float32)
    age = np.arange(BLOCK_KEYS)[None, :] // 64 - (p // 64)[:, None]
    c["band_mask"] = np.where((age == 0) | (age == 1), 0.0, NEGATIVE).astype(np.float32)
    c["causal_mask"] = np.where(p[:, None] <= p[None, :], 0.0, NEGATIVE).astype(np.float32)
    c["count"] = np.broadcast_to(np.arange(P, dtype=np.float32), (P, P)).copy()
    return c


NEGATIVE = -1e30


class Constants:

    def __init__(self, nc, ctx, arrays):
        def sb(what, shape, dt=F32):
            return ctx.enter_context(nc.sbuf_tensor("const_" + what, shape, dt))

        identity, ones = sb("identity", [P, P]), sb("ones", [P, P])
        loaded = ctx.enter_context(nc.semaphore("const_loaded"))
        with nc.Block() as block:
            @block.sync
            def _(sp):
                sp.dma_start(identity[:], arrays["identity"]).then_inc(loaded, 16)
                sp.wait_ge(loaded, 16)

            @block.vector
            def _(dve):
                dve.memset(ones[:], 1.0)
        self.identity, self.ones = identity[:], ones[:]

    def load_heads(self, nc, ctx, arrays):
        pick = ctx.enter_context(nc.sbuf_tensor("const_head_pick", [P, 16, 32], F32))
        spread = ctx.enter_context(nc.sbuf_tensor("const_head_spread", [32, 16, P], F32))
        loaded = ctx.semaphore("const_heads_loaded")
        with nc.Block() as block:
            @block.sync
            def _(sp):
                sp.dma_start(pick[:], arrays["head_pick"]).then_inc(loaded, 16)
                sp.dma_start(spread[:], arrays["head_spread"]).then_inc(loaded, 16)
                sp.wait_ge(loaded, 32)
        self.head_pick, self.head_spread = pick[:], spread[:]


IN_SEGMENTS = [(CONV_TILES, "conv"), (45, "copy")]
GATE_ATT_ROWS, GATE_SSM_ROWS = 6656, 7680


def build_layer(nc, a, out):
    def scratch(what, rows, cols=T):
        return nc.dram_tensor("scratch_" + what, (rows, cols), F32, kind="Internal").ap()

    proj = scratch("proj", (CONV_TILES + 45) * P)
    rel_row = scratch("rel_row", Q_HEADS, REL_COUNT)
    ssm, mixed_att, mixed = scratch("ssm", 2048), scratch("mixed_att", D), scratch("mixed", D)
    x1, query, ple = scratch("x1", D), scratch("query", 2048), scratch("ple", D)
    hidden = scratch("hidden", EXPERT_TILES * P)
    gates = nc.dram_tensor("scratch_gates", (KEYS, KEYS, T), F32, kind="Internal").ap()
    ctx = ExitStack()
    with ctx:
        const = Constants(nc, ctx, a)

        with ExitStack() as scope:
            h = Activations(nc, scope, "h_mix", KD, a["x"], a["norm_mix_g"])
            linear_phase(nc, "in_proj", h, a["w_in"], IN_SEGMENTS, proj, const=const, taps_dram=a["conv"])
        with ExitStack() as scope:
            att = scope.enter_context(nc.sbuf_tensor("att", [P, KD, T], F32))
            with Phase(nc) as heads:
                const.load_heads(nc, heads, a)
                attention_phase(nc, "attention", proj, a["qk_norm_g"], a["attn_sinks"], a["rel_bias"], a["bucket_onehot"],
                                a["band_mask"], a["flip"], rel_row, att, const)
            o = Activations(nc, scope, "o_att", KD, att, resident=True)
            linear_phase(nc, "o_att", o, a["w_o_attn"], [(KD, "gate")], mixed_att, proj[GATE_ATT_ROWS:GATE_ATT_ROWS + D, :])
        ssm_phase(nc, "ssm", proj, a["head_par"], a["tile_par"], a["causal_mask"], a["head_spread"], ssm, const)
        with ExitStack() as scope:
            y = Activations(nc, scope, "y_ssm", SSM_TILES, ssm)
            linear_phase(nc, "o_ssm", y, a["w_o_ssm"], [(KD, "gate_add")], mixed,
                         proj[GATE_SSM_ROWS:GATE_SSM_ROWS + D, :], mixed_att)
        with ExitStack() as scope:
            with ExitStack() as residual:
                h = Activations(nc, scope, "h_ffn", KD, None, a["norm_ffn_g"], resident=True)
                h.source = residual.enter_context(nc.sbuf_tensor("x1_tiles", [P, KD, T], F32))
                with ExitStack() as mixing:
                    m = Activations(nc, mixing, "mixed", KD, mixed)
                    linear_phase(nc, "out_proj", m, a["w_out"], [(KD, "add")], x1, a["x"], keep=h.source)
                linear_phase(nc, "query", h, a["w_peer_q"], [(SCORE_SETS, "copy")], query, const=const)
            select_phase(nc, "select", h, a["peer_u"], hidden, query, a["peer_keys"], a["count"], gates, const)
        x2 = ctx.enter_context(nc.sbuf_tensor("x2", [P, KD, T], F32))
        combine_phase(nc, "combine", hidden, gates, a["peer_v"], x1, x2)
        with ExitStack() as scope:
            e = Activations(nc, scope, "embedding", 2, a["p"])
            linear_phase(nc, "ple", e, a["w_ple"], [(KD, "copy")], ple)
        with ExitStack() as scope:
            h = Activations(nc, scope, "h_ple", KD, x2, a["norm_ple_g"], resident=True)
            linear_phase(nc, "ple_gate", h, a["w_ple_gate"], [(KD, "final")], out, ple, const=const, resident_extra2=x2)


def weight_tiles(w):
    k, n = w.shape[0] // P, w.shape[1] // P
    return w.reshape(k, P, n, P).transpose(2, 1, 0, 3).reshape(n * P, k * P)


def per_partition(*rows):
    stacked = np.stack([r.reshape(-1, P).T for r in rows], axis=-1)
    return stacked[:, :, 0] if len(rows) == 1 else stacked


def kernel(**inputs):
    import concourse.bacc as bacc
    from concourse.bass_utils import run_bass_kernel_spmd

    i = {k: np.asarray(v) for k, v in inputs.items()}
    one = {k: v[0] for k, v in i.items()}
    w_in = one["w_in"]
    xbc_at = 1024 + 256 + 256 + 2048
    dt_at = xbc_at + 3072
    order = np.arange(Q_HEADS).reshape(KV_HEADS, 4)[:, list(HEAD_ORDER)].reshape(-1)
    w_dt = np.zeros((D, P), w_in.dtype)
    w_dt[:, :SSM_HEADS] = w_in[:, dt_at:dt_at + SSM_HEADS]
    arrays = {
        "x": one["x"].T,
        "p": one["p"][0].T,
        "norm_mix_g": per_partition(one["norm_mix_g"]),
        "norm_ffn_g": per_partition(one["norm_ffn_g"]),
        "norm_ple_g": per_partition(one["norm_ple_g"]),
        "w_in": weight_tiles(np.concatenate([w_in[:, xbc_at:dt_at], w_in[:, :xbc_at], w_in[:, dt_at + SSM_HEADS:], w_dt],
                                            axis=1)),
        "qk_norm_g": np.stack([np.tile(one["q_norm_g"], 2), np.tile(one["k_norm_g"], 2)], axis=1),
        "attn_sinks": one["attn_sinks"][order],
        "rel_bias": i["rel_bias"][:, order],
        "conv": per_partition(*one["conv_w"], one["conv_b"]),
        "head_par": np.stack([one["dt_bias"], one["a_log"]], axis=1),
        "tile_par": per_partition(np.repeat(one["d_skip"], 64), one["ssm_norm_g"]),
        "w_o_attn": weight_tiles(one["w_o_attn"]),
        "w_o_ssm": weight_tiles(one["w_o_ssm"]),
        "w_out": weight_tiles(one["w_out"]),
        "w_peer_q": weight_tiles(one["w_peer_q"]),
        "peer_keys": one["peer_sub_keys"].reshape(SCORE_SETS, KEYS, P).transpose(2, 0, 1),
        "peer_u": weight_tiles(one["peer_u"].T),
        "peer_v": one["peer_v"],
        "w_ple_gate": weight_tiles(one["w_ple_gate"]),
        "w_ple": weight_tiles(one["w_ple"]),
        **shape_constants(),
    }
    arrays = {k: np.ascontiguousarray(v) for k, v in arrays.items()}
    nc = bacc.Bacc("TRN2", target_bir_lowering=False, num_devices=1)
    aps = {k: nc.dram_tensor("in_" + k, v.shape, mybir.dt.from_np(v.dtype), kind="ExternalInput").ap()
           for k, v in arrays.items()}
    out = nc.dram_tensor("out", (D, T), F32, kind="ExternalOutput").ap()
    build_layer(nc, aps, out)
    r = run_bass_kernel_spmd(nc, [{"in_" + k: v for k, v in arrays.items()}], core_ids=[0])
    return np.ascontiguousarray(r.results[0]["out"].T)[None]
```
